# Optimizing a Trainium2 kernel written in Bass

```python
import math, functools
import jax, jax.numpy as jnp
from jax import lax
import numpy as np

D_MODEL = 2048
BATCH = 1
SEQ = 512
DEPTH = 1

GRID_W = 64
CTX_LEN = 256
GROUP_W = D_MODEL // 4
MIX_W = 4 * GROUP_W
CHUNK = 64
SHORT_CONV = 5
FFN_CONV = 3
D_FF = ((8 * D_MODEL // 3 + 255) // 256) * 256
N_MOD = 6
EPS = 1e-6

DN_HEADS = 4
DN_DK = GROUP_W // DN_HEADS
DN_DV = GROUP_W // DN_HEADS
DN_QKV = 2 * DN_HEADS * DN_DK + DN_HEADS * DN_DV

SSD_HEAD_DIM = 64
SSD_HEADS = GROUP_W // SSD_HEAD_DIM
SSD_GROUPS = 2
SSD_STATE = 128
SSD_XBC = SSD_HEADS * SSD_HEAD_DIM + 2 * SSD_GROUPS * SSD_STATE

LRU_W = GROUP_W
LRU_BLOCKS = 8
LRU_BW = LRU_W // LRU_BLOCKS
LRU_C = 8.0

ML_HEADS = 4
ML_DV = GROUP_W // ML_HEADS
ML_DK = ML_DV // 2

IN_SPLITS = (
    ("dn_q", DN_HEADS * DN_DK), ("dn_k", DN_HEADS * DN_DK), ("dn_v", DN_HEADS * DN_DV),
    ("dn_z", DN_HEADS * DN_DV), ("dn_a", 2 * DN_HEADS), ("dn_b", 2 * DN_HEADS),
    ("ssd_x", SSD_HEADS * SSD_HEAD_DIM), ("ssd_z", SSD_HEADS * SSD_HEAD_DIM),
    ("ssd_B", SSD_GROUPS * SSD_STATE), ("ssd_C", SSD_GROUPS * SSD_STATE), ("ssd_dt", 2 * SSD_HEADS),
    ("lru_x", LRU_W), ("lru_g", LRU_W),
    ("ml_q", ML_HEADS * ML_DK), ("ml_k", ML_HEADS * ML_DK), ("ml_v", ML_HEADS * ML_DV),
    ("ml_o", ML_HEADS * ML_DV), ("ml_i", 2 * ML_HEADS), ("ml_f", 2 * ML_HEADS),
)
D_IN = sum(w for _, w in IN_SPLITS)

kernel_name = "hybrid_parallel_groups_prefix_ctx"

F32 = jnp.float32

def _rmsnorm(x, g):
    xf = x.astype(F32)
    y = xf * lax.rsqrt(jnp.mean(xf * xf, axis=-1, keepdims=True) + EPS)
    return (y * g.astype(F32)).astype(x.dtype)

def _l2norm(x):
    return x * lax.rsqrt(jnp.sum(x * x, axis=-1, keepdims=True) + EPS)

def _dwconv(x, w, b=None):
    k = w.shape[0]
    y = lax.conv_general_dilated(x, w[:, None, :].astype(x.dtype), window_strides=(1,),
                                 padding=((k // 2, k // 2),),
                                 dimension_numbers=("NWC", "WIO", "NWC"),
                                 feature_group_count=w.shape[1])
    return y if b is None else y + b.astype(x.dtype)

def _split_proj(p):
    out, off = {}, 0
    for name, width in IN_SPLITS:
        out[name] = p[..., off:off + width]
        off += width
    return out

def _to_col_major(t):
    b_, n, ch = t.shape
    rows = n // GRID_W
    return t.reshape(b_, rows, GRID_W, ch).transpose(0, 2, 1, 3).reshape(b_, n, ch)

def _from_col_major(t):
    b_, n, ch = t.shape
    rows = n // GRID_W
    return t.reshape(b_, GRID_W, rows, ch).transpose(0, 2, 1, 3).reshape(b_, n, ch)

def _to_chunks(t):
    b_, n, h = t.shape[:3]
    t = t.reshape(b_, n // CHUNK, CHUNK, h, *t.shape[3:])
    return jnp.moveaxis(t, (1, 3), (0, 2))

def _from_chunks(t):
    t = jnp.moveaxis(t, (0, 2), (1, 3))
    return t.reshape(t.shape[0], -1, *t.shape[3:])

def _seg_decay(cs):
    n = cs.shape[-1]
    tri = jnp.tril(jnp.ones((n, n), bool))
    diff = cs[..., :, None] - cs[..., None, :]
    return jnp.where(tri, jnp.exp(jnp.where(tri, diff, 0.0)), 0.0)

def _bidir(core, ctx_args, lat_args):
    flip = functools.partial(jnp.flip, axis=1)
    yc_f, s_f = core(ctx_args[0], None)
    yl_f, _ = core(lat_args[0], s_f)
    yc_b, s_b = core(tuple(map(flip, ctx_args[1])), None)
    yl_b, _ = core(tuple(map(flip, lat_args[1])), s_b)
    return yc_f + flip(yc_b), yl_f + flip(yl_b)

def _gated_delta_chunked(args, s0):
    q, k, v, g, beta = args
    b_, _, h, dk = q.shape
    dv = v.shape[-1]
    q, k, v, g, beta = map(_to_chunks, (q, k, v, g, beta))
    gc = jnp.cumsum(g, axis=-1)
    decay = _seg_decay(gc)
    strict = jnp.tril(jnp.ones((CHUNK, CHUNK), bool), -1)
    kb = k * beta[..., None]
    amat = jnp.eye(CHUNK, dtype=F32) + jnp.where(
        strict, jnp.einsum("nbhcd,nbhsd->nbhcs", kb, k) * decay, 0.0)
    rhs = jnp.concatenate([v * beta[..., None], kb * jnp.exp(gc)[..., None]], axis=-1)
    sol = lax.linalg.triangular_solve(amat, rhs, left_side=True, lower=True, unit_diagonal=True)
    u, w = sol[..., :dv], sol[..., dv:]
    attn = jnp.einsum("nbhcd,nbhsd->nbhcs", q, k) * decay
    if s0 is None:
        s0 = jnp.zeros((b_, h, dk, dv), F32)

    def step(s, xs):
        q_i, k_i, u_i, w_i, a_i, gc_i = xs
        v_new = u_i - w_i @ s
        o = (q_i * jnp.exp(gc_i)[..., None]) @ s + a_i @ v_new
        g_last = gc_i[..., -1:]
        s = s * jnp.exp(g_last)[..., None] + jnp.einsum(
            "bhcd,bhce->bhde", k_i * jnp.exp(g_last - gc_i)[..., None], v_new)
        return s, o

    s_fin, o = lax.scan(step, s0, (q, k, u, w, attn, gc))
    return _from_chunks(o), s_fin

def _gated_deltanet(pc, pl, conv_w, a_log, dt_bias, norm_g):
    hk = DN_HEADS * DN_DK

    def prep(p):
        qkv = jnp.concatenate([p["dn_q"], p["dn_k"], p["dn_v"]], axis=-1)
        qkv = jax.nn.silu(_dwconv(qkv, conv_w)).astype(F32)
        b_, t = qkv.shape[:2]
        q, k, v = jnp.split(qkv, [hk, 2 * hk], axis=-1)
        q = _l2norm(q.reshape(b_, t, DN_HEADS, DN_DK)) * DN_DK ** -0.5
        k = _l2norm(k.reshape(b_, t, DN_HEADS, DN_DK))
        v = v.reshape(b_, t, DN_HEADS, DN_DV)
        a = p["dn_a"].astype(F32).reshape(b_, t, 2, DN_HEADS)
        g = -jnp.exp(a_log.astype(F32)) * jax.nn.softplus(a + dt_bias.astype(F32))
        beta = jax.nn.sigmoid(p["dn_b"].astype(F32).reshape(b_, t, 2, DN_HEADS))
        return tuple((q, k, v, g[:, :, d], beta[:, :, d]) for d in range(2))

    def finish(o, p):
        b_, t = o.shape[:2]
        z = p["dn_z"].astype(F32).reshape(b_, t, DN_HEADS, DN_DV)
        return (_rmsnorm(o, norm_g) * jax.nn.silu(z)).reshape(b_, t, DN_HEADS * DN_DV)

    oc, ol = _bidir(_gated_delta_chunked, prep(pc), prep(pl))
    return finish(oc, pc), finish(ol, pl)

def _ssd_chunked(args, s0):
    xd, a, bm, cm = args
    b_, t, h, p = xd.shape
    n, nc = bm.shape[-1], t // CHUNK
    xd = xd.reshape(b_, nc, CHUNK, h, p)
    bm = bm.reshape(b_, nc, CHUNK, h, n)
    cm = cm.reshape(b_, nc, CHUNK, h, n)
    acs = jnp.cumsum(a.reshape(b_, nc, CHUNK, h), axis=2)
    lmat = _seg_decay(jnp.moveaxis(acs, 3, 2))
    scores = jnp.einsum("bclhn,bcshn->bchls", cm, bm) * lmat
    y_diag = jnp.einsum("bchls,bcshp->bclhp", scores, xd)
    w_state = jnp.exp(acs[:, :, -1:, :] - acs)
    local = jnp.einsum("bclhn,bclhp->bchpn", bm, xd * w_state[..., None])
    chunk_dec = jnp.exp(acs[:, :, -1, :])
    if s0 is None:
        s0 = jnp.zeros((b_, h, p, n), F32)

    def step(s, inp):
        dec, loc = inp
        return s * dec[..., None, None] + loc, s

    s_fin, s_in = lax.scan(step, s0, (jnp.moveaxis(chunk_dec, 1, 0), jnp.moveaxis(local, 1, 0)))
    s_in = jnp.moveaxis(s_in, 0, 1)
    y_off = jnp.einsum("bclhn,bchpn->bclhp", cm, s_in) * jnp.exp(acs)[..., None]
    return (y_diag + y_off).reshape(b_, t, h, p), s_fin

def _mamba2_ssd(pc, pl, conv_w, conv_b, a_log, dt_bias, d_skip, norm_g):
    hp, gn = SSD_HEADS * SSD_HEAD_DIM, SSD_GROUPS * SSD_STATE
    rep = SSD_HEADS // SSD_GROUPS

    def prep(p):
        xbc = jnp.concatenate([p["ssd_x"], p["ssd_B"], p["ssd_C"]], axis=-1)
        xbc = jax.nn.silu(_dwconv(xbc, conv_w, conv_b)).astype(F32)
        b_, t = xbc.shape[:2]
        xs, bm, cm = jnp.split(xbc, [hp, hp + gn], axis=-1)
        xs = xs.reshape(b_, t, SSD_HEADS, SSD_HEAD_DIM)
        bm = jnp.repeat(bm.reshape(b_, t, SSD_GROUPS, SSD_STATE), rep, axis=2)
        cm = jnp.repeat(cm.reshape(b_, t, SSD_GROUPS, SSD_STATE), rep, axis=2)
        dt = jax.nn.softplus(p["ssd_dt"].astype(F32).reshape(b_, t, 2, SSD_HEADS) + dt_bias.astype(F32))
        a = -jnp.exp(a_log.astype(F32)) * dt
        xd = xs[:, :, None] * dt[..., None]
        return tuple((xd[:, :, d], a[:, :, d], bm, cm) for d in range(2)), xs

    def finish(y, xs, p):
        b_, t = y.shape[:2]
        y = (y + d_skip.astype(F32)[:, None] * xs).reshape(b_, t, hp)
        y = y * jax.nn.silu(p["ssd_z"].astype(F32))
        y = _rmsnorm(y.reshape(b_, t, SSD_GROUPS, hp // SSD_GROUPS), norm_g.reshape(SSD_GROUPS, -1))
        return y.reshape(b_, t, hp)

    (args_c, xs_c), (args_l, xs_l) = prep(pc), prep(pl)
    yc, yl = _bidir(_ssd_chunked, args_c, args_l)
    return finish(yc, xs_c, pc), finish(yl, xs_l, pl)

def _linear_scan(args, h0):
    a, b = args
    if h0 is not None:
        b = b.at[:, 0].add(a[:, 0] * h0)

    def comb(l, r):
        return l[0] * r[0], r[0] * l[1] + r[1]

    _, h = lax.associative_scan(comb, (a, b), axis=1)
    return h, h[:, -1]

def _rglru(pc, pl, conv_w, conv_b, w_a, b_a, w_i, b_i, lam):
    def prep(p, col_major):
        xr = _to_col_major(p["lru_x"]) if col_major else p["lru_x"]
        xr = _dwconv(xr, conv_w, conv_b).astype(F32)
        b_, t = xr.shape[:2]
        xb = xr.reshape(b_, t, LRU_BLOCKS, LRU_BW)
        r = jax.nn.sigmoid(jnp.einsum("btnj,dnjk->btdnk", xb, w_a.astype(F32)).reshape(b_, t, 2, LRU_W)
                           + b_a.astype(F32))
        i = jax.nn.sigmoid(jnp.einsum("btnj,dnjk->btdnk", xb, w_i.astype(F32)).reshape(b_, t, 2, LRU_W)
                           + b_i.astype(F32))
        log_a = -LRU_C * r * jax.nn.softplus(-lam.astype(F32))
        b = jnp.sqrt(-jnp.expm1(2.0 * log_a)) * i * xr[:, :, None]
        a = jnp.exp(log_a)
        return tuple((a[:, :, d], b[:, :, d]) for d in range(2))

    hc, hl = _bidir(_linear_scan, prep(pc, False), prep(pl, True))
    hl = _from_col_major(hl)
    return (hc * jax.nn.gelu(pc["lru_g"].astype(F32)),
            hl * jax.nn.gelu(pl["lru_g"].astype(F32)))

def _mlstm_chunked(args, state):
    q, k, v, ig, lf = map(_to_chunks, args)
    nb, hh, dk, dv = q.shape[1], q.shape[2], q.shape[-1], v.shape[-1]
    if state is None:
        state = (jnp.zeros((nb, hh, dk, dv), F32), jnp.zeros((nb, hh, dk), F32),
                 jnp.zeros((nb, hh), F32))
    tri = jnp.tril(jnp.ones((CHUNK, CHUNK), bool))

    def step(carry, xs):
        c_s, n_s, m_s = carry
        qc, kc, vc, ic, fc = xs
        b = jnp.cumsum(fc, axis=-1)
        log_d = jnp.where(tri, b[..., :, None] - b[..., None, :] + ic[..., None, :], -jnp.inf)
        inter = b + m_s[..., None]
        m = jnp.maximum(inter, jnp.max(log_d, axis=-1))
        s = jnp.einsum("bhcd,bhsd->bhcs", qc, kc) * jnp.exp(log_d - m[..., None])
        w_inter = jnp.exp(inter - m)
        num = w_inter[..., None] * (qc @ c_s) + s @ vc
        den = w_inter * jnp.einsum("bhcd,bhd->bhc", qc, n_s) + jnp.sum(s, axis=-1)
        h = num / jnp.maximum(jnp.abs(den), jnp.exp(-m))[..., None]
        b_last = b[..., -1]
        log_g = b_last[..., None] - b + ic
        m_new = jnp.maximum(b_last + m_s, jnp.max(log_g, axis=-1))
        dec = jnp.exp(b_last + m_s - m_new)
        wk = jnp.exp(log_g - m_new[..., None])[..., None] * kc
        c_s = dec[..., None, None] * c_s + jnp.einsum("bhcd,bhce->bhde", wk, vc)
        n_s = dec[..., None] * n_s + jnp.sum(wk, axis=-2)
        return (c_s, n_s, m_new), h

    state, h = lax.scan(step, state, (q, k, v, ig, lf))
    return _from_chunks(h), state

def _mlstm(pc, pl, ig_b, fg_b, norm_g):
    def prep(p):
        b_, t = p["ml_q"].shape[:2]
        q = p["ml_q"].astype(F32).reshape(b_, t, ML_HEADS, ML_DK) * ML_DK ** -0.5
        k = p["ml_k"].astype(F32).reshape(b_, t, ML_HEADS, ML_DK)
        v = p["ml_v"].astype(F32).reshape(b_, t, ML_HEADS, ML_DV)
        ig = p["ml_i"].astype(F32).reshape(b_, t, 2, ML_HEADS) + ig_b.astype(F32)
        lf = jax.nn.log_sigmoid(p["ml_f"].astype(F32).reshape(b_, t, 2, ML_HEADS) + fg_b.astype(F32))
        return tuple((q, k, v, ig[:, :, d], lf[:, :, d]) for d in range(2))

    def finish(h, p):
        b_, t = h.shape[:2]
        h = _rmsnorm(h, norm_g.reshape(ML_HEADS, ML_DV)).reshape(b_, t, ML_HEADS * ML_DV)
        return h * jax.nn.sigmoid(p["ml_o"].astype(F32))

    hc, hl = _bidir(_mlstm_chunked, prep(pc), prep(pl))
    return finish(hc, pc), finish(hl, pl)

def _conv_ffn(h, w_up, conv_w, w_down):
    u, g = jnp.split(h @ w_up, 2, axis=-1)
    return (jax.nn.silu(_dwconv(g, conv_w)) * u) @ w_down

def setup_inputs(seed: int = 0) -> dict:
    key = jax.random.key(seed)
    ks = iter(jax.random.split(key, 40))
    L, D = DEPTH, D_MODEL

    def nrm(shape, scale=1.0):
        return jax.random.normal(next(ks), shape, F32) * scale

    def unif(shape, lo, hi):
        return jax.random.uniform(next(ks), shape, F32, lo, hi)

    def gain(shape):
        return 1.0 + nrm(shape, 0.05)

    def dt_bias(shape):
        dt = jnp.exp(unif(shape, math.log(1e-3), math.log(1e-1)))
        return dt + jnp.log(-jnp.expm1(-dt))

    def lru_lambda(shape):
        s = unif(shape, 0.9, 0.999) ** (1.0 / LRU_C)
        return jnp.log(s) - jnp.log1p(-s)

    return {
        "x": nrm((BATCH, SEQ, D)),
        "c": nrm((BATCH, D)),
        "ctx": nrm((BATCH, CTX_LEN, D)),
        "c_ctx": nrm((D,)),
        "ada_w": nrm((L, D, N_MOD * D), D ** -0.5),
        "ada_b": nrm((L, N_MOD * D), 0.01),
        "norm1_g": gain((L, D)),
        "norm2_g": gain((L, D)),
        "w_in": nrm((L, D, D_IN), D ** -0.5),
        "dn_conv_w": nrm((L, SHORT_CONV, DN_QKV), SHORT_CONV ** -0.5),
        "dn_a_log": jnp.log(unif((L, 2, DN_HEADS), 1.0, 16.0)),
        "dn_dt_bias": dt_bias((L, 2, DN_HEADS)),
        "dn_norm_g": gain((L, DN_DV)),
        "ssd_conv_w": nrm((L, SHORT_CONV, SSD_XBC), SHORT_CONV ** -0.5),
        "ssd_conv_b": nrm((L, SSD_XBC), 0.01),
        "ssd_a_log": jnp.log(unif((L, 2, SSD_HEADS), 1.0, 16.0)),
        "ssd_dt_bias": dt_bias((L, 2, SSD_HEADS)),
        "ssd_d": 1.0 + nrm((L, SSD_HEADS), 0.1),
        "ssd_norm_g": gain((L, SSD_HEADS * SSD_HEAD_DIM)),
        "lru_conv_w": nrm((L, SHORT_CONV, LRU_W), SHORT_CONV ** -0.5),
        "lru_conv_b": nrm((L, LRU_W), 0.01),
        "lru_w_a": nrm((L, 2, LRU_BLOCKS, LRU_BW, LRU_BW), LRU_BW ** -0.5),
        "lru_b_a": nrm((L, 2, LRU_W), 0.01),
        "lru_w_i": nrm((L, 2, LRU_BLOCKS, LRU_BW, LRU_BW), LRU_BW ** -0.5),
        "lru_b_i": nrm((L, 2, LRU_W), 0.01),
        "lru_lambda": lru_lambda((L, 2, LRU_W)),
        "ml_ig_b": nrm((L, 2, ML_HEADS), 0.1),
        "ml_fg_b": unif((L, 2, ML_HEADS), 3.0, 6.0),
        "ml_norm_g": gain((L, ML_HEADS * ML_DV)),
        "w_out": nrm((L, MIX_W, D), MIX_W ** -0.5),
        "ffn_w_up": nrm((L, D, 2 * D_FF), D ** -0.5),
        "ffn_conv_w": nrm((L, FFN_CONV, D_FF), FFN_CONV ** -0.5),
        "ffn_w_down": nrm((L, D_FF, D), D_FF ** -0.5),
        "final_norm_g": gain((D,)),
    }

def reference(x, c, ctx, c_ctx, ada_w, ada_b, norm1_g, norm2_g, w_in,
              dn_conv_w, dn_a_log, dn_dt_bias, dn_norm_g,
              ssd_conv_w, ssd_conv_b, ssd_a_log, ssd_dt_bias, ssd_d, ssd_norm_g,
              lru_conv_w, lru_conv_b, lru_w_a, lru_b_a, lru_w_i, lru_b_i, lru_lambda,
              ml_ig_b, ml_fg_b, ml_norm_g, w_out, ffn_w_up, ffn_conv_w, ffn_w_down,
              final_norm_g):
    lat, hctx = x, ctx
    nb = c.shape[0]
    for l in range(DEPTH):
        mod_l = (jax.nn.silu(c) @ ada_w[l] + ada_b[l]).reshape(nb, N_MOD, 1, D_MODEL)
        mod_c = (jax.nn.silu(c_ctx) @ ada_w[l] + ada_b[l]).reshape(N_MOD, D_MODEL)
        sh1_l, sc1_l, g1_l, sh2_l, sc2_l, g2_l = (mod_l[:, j] for j in range(N_MOD))
        sh1_c, sc1_c, g1_c, sh2_c, sc2_c, g2_c = (mod_c[j] for j in range(N_MOD))

        hl = _rmsnorm(lat, norm1_g[l]) * (1.0 + sc1_l) + sh1_l
        hc = _rmsnorm(hctx, norm1_g[l]) * (1.0 + sc1_c) + sh1_c
        pl = _split_proj(hl @ w_in[l])
        pc = _split_proj(hc @ w_in[l])
        a_c, a_l = _gated_deltanet(pc, pl, dn_conv_w[l], dn_a_log[l], dn_dt_bias[l], dn_norm_g[l])
        b_c, b_l = _mamba2_ssd(pc, pl, ssd_conv_w[l], ssd_conv_b[l], ssd_a_log[l], ssd_dt_bias[l],
                               ssd_d[l], ssd_norm_g[l])
        r_c, r_l = _rglru(pc, pl, lru_conv_w[l], lru_conv_b[l], lru_w_a[l], lru_b_a[l],
                          lru_w_i[l], lru_b_i[l], lru_lambda[l])
        m_c, m_l = _mlstm(pc, pl, ml_ig_b[l], ml_fg_b[l], ml_norm_g[l])
        mix_l = jnp.concatenate([a_l, b_l, r_l, m_l], axis=-1).astype(lat.dtype)
        lat = lat + g1_l * (mix_l @ w_out[l])

        hl = _rmsnorm(lat, norm2_g[l]) * (1.0 + sc2_l) + sh2_l
        lat = lat + g2_l * _conv_ffn(hl, ffn_w_up[l], ffn_conv_w[l], ffn_w_down[l])

        if l < DEPTH - 1:
            mix_c = jnp.concatenate([a_c, b_c, r_c, m_c], axis=-1).astype(hctx.dtype)
            hctx = hctx + g1_c * (mix_c @ w_out[l])
            hc = _rmsnorm(hctx, norm2_g[l]) * (1.0 + sc2_c) + sh2_c
            hctx = hctx + g2_c * _conv_ffn(hc, ffn_w_up[l], ffn_conv_w[l], ffn_w_down[l])

    return _rmsnorm(lat, final_norm_g)


_drawn_inputs = setup_inputs


def setup_inputs(seed=0):
    import zlib

    import numpy as np

    out = dict(_drawn_inputs(seed))
    spreads = {}
    factors = {'dn_a_log': 4.384,
     'dn_norm_g': 8.0,
     'ssd_conv_b': 8.0,
     'ssd_d': 25.845,
     'ssd_norm_g': 7.889,
     'lru_conv_b': 3.629,
     'lru_b_a': 64.0,
     'lru_b_i': 56.225,
     'ml_ig_b': 64.0,
     'ml_norm_g': 25.143,
     'norm2_g': 4.524}
    for name, (base, spread) in spreads.items():
        noise = np.random.default_rng([zlib.crc32(name.encode()), seed]).standard_normal(out[name].shape)
        drawn = base * np.exp(spread * noise) if base else spread * noise
        out[name] = __import__('jax').numpy.asarray(drawn.astype(out[name].dtype))
    for name, factor in factors.items():
        out[name] = (out[name] * factor).astype(out[name].dtype)
    return out
```

```python
import numpy as np

import concourse.bass as bass
from concourse import mybir

F32 = mybir.dt.float32
F32R = mybir.dt.float32r
ALU = mybir.AluOpType
ACT = mybir.ActivationFunctionType

P = 128
D_MODEL = 2048
SEQ = 512
CTX = 256
TOK = CTX + SEQ
GRID_W = 64
GRID_ROWS = SEQ // GRID_W
GROUP_W = D_MODEL // 4
D_FF = 5632
EPS = 1e-6
KT = D_MODEL // P
FT = D_FF // P
N_MOD = 6
SH1, SC1, G1, SH2, SC2, G2 = range(N_MOD)
CHUNKS = TOK // P
CTX_CHUNKS = CTX // P
NEG = -1e30

DN_HEADS, SSD_HEADS, SSD_P, ML_HEADS, ML_DK = 4, 8, 64, 4, 64
SHORT = 5
DN_A, DN_B = 2048, 2056
SSD_DT, ML_I, ML_F = 3600, 6176, 6184

REGIONS = [
    (0, 4, False, "conv"),
    (4, 8, True, "conv"),
    (12, 4, False, "silu"),
    (16, 4, True, "conv"),
    (20, 4, False, "silu"),
    (24, 2, True, "conv"),
    (26, 2, False, "conv"),
    (28, 4, True, "lru"),
    (32, 4, False, "gelu"),
    (36, 2, False, "copy"),
    (38, 6, True, "copy"),
    (44, 4, False, "sigmoid"),
]
T_Q, T_K, T_V, T_Z, T_SX, T_SZ, T_SB, T_SC = 0, 4, 8, 12, 16, 20, 24, 26
T_LX, T_LG, T_MQ, T_MK, T_MV, T_MO, TILES = 28, 32, 36, 38, 40, 44, 48
COLUMN_RUNS = [(0, 2, 0), (2, 14, 2 * P), (16, 12, 2064), (28, 6, 3616), (34, 14, 3616 + 6 * P)]

PAR = {}
_at = 0
for _name, _n in (("norm1", KT), ("norm2", KT), ("final", KT), ("dn_norm", 1), ("ssd_norm", 4),
                  ("ml_norm", 4), ("ssd_cb", 8), ("lru_cb", 4), ("lru_ba", 8), ("lru_bi", 8),
                  ("lru_lam", 8), ("ssd_d", 4)):
    PAR[_name] = _at
    _at += _n
N_VEC = _at
PAR["dn_cw"], PAR["ssd_cw"], PAR["lru_cw"] = N_VEC, N_VEC + 60, N_VEC + 100
N_CW = 120
PAR["ffn_cw"] = N_VEC + N_CW
PAR["ada_b"] = N_VEC + N_CW + 3 * FT
N_LATE = (N_MOD - G1) * KT
N_PAR = PAR["ada_b"] + N_LATE

R_DN, R_SSD, R_ML, GROWS = 0, 4, 12, 16

KB = 1024
AT_LOW = 8 * KB
AT_LAT = 72 * KB
AT_RING = 104 * KB
AT_HIGH = 152 * KB


def chunk_of(d, n):
    if d == 0:
        return n
    return CTX_CHUNKS - 1 - n if n < CTX_CHUNKS else CHUNKS - 1 - (n - CTX_CHUNKS)


class Kit:

    def __init__(self, nc, io, out):
        self.nc, self.io, self.out = nc, io, out
        self.base = (nc.sbuf_base + 63) // 64 * 64
        self.sems = {}
        self.psum = [nc.alloc_psum_tensor(f"bank{b}", [P, 512], F32) for b in range(8)]
        self.at = self.base
        self.n = 0

    def sem(self, name):
        if name not in self.sems:
            self.sems[name] = self.nc.alloc_semaphore(name)
        return self.sems[name]

    def end_block(self):
        self.nc.clear_and_free_semaphores(list(self.sems.values()))
        self.nc.all_engine_barrier()
        self.sems = {}

    def go(self, offset):
        self.at = self.base + offset

    def sb(self, name, shape, dtype=F32):
        size = 4
        for s in shape[1:]:
            size *= s
        t = self.nc.alloc_sbuf_tensor_at(name, shape, dtype, offset=self.at)
        self.at += (size + 63) // 64 * 64
        return t

    def dram(self, name, shape):
        return self.nc.dram_tensor(name, shape, F32, kind="Internal").ap()




def constants_and_state(k):
    k.go(0)
    k.ident = k.sb("ident", [P, P])
    k.ones = k.sb("ones", [P, P])
    k.par = k.sb("par", [P, N_PAR])
    k.mod = k.sb("mod", [P, N_MOD * KT, 2])
    k.csil = k.sb("csil", [P, KT, 2])
    k.gain1 = k.sb("gain1", [P, 2, KT])
    k.gain2 = k.sb("gain2", [P, KT])
    k.eps = k.sb("eps", [P, 1])
    k.gpar = k.sb("gpar", [P, 8])
    assert k.at - k.base <= AT_LOW, k.at - k.base
    k.xT_dram = k.dram("xT_dram", [P, KT, SEQ])
    k.proj = k.dram("proj", [TILES, P, TOK])
    k.rows_dram = k.dram("rows_dram", [2, 64, TOK])
    k.mix = k.dram("mix", [KT, P, SEQ])


GP_ALOG, GP_BIAS, GP_IGB, GP_SIGN, GP_COEF, GP_ML = range(6)


def modulation_and_norm1(k):
    nc, io = k.nc, k.io
    k.go(AT_LOW)
    adaw = [k.sb(f"adaw{s}", [P, KT, 512]) for s in range(2)]
    sheet = k.sb("sheet", [P, 5, P])
    dval = k.sb("dval", [1, SSD_HEADS])
    dwide = k.sb("dwide", [1, SSD_HEADS * SSD_P])
    cvec = k.sb("cvec", [P, 2, KT])
    modrow = [k.sb(f"modrow{s}", [2, 512]) for s in range(2)]
    biasrow = [k.sb(f"biasrow{s}", [2, 512]) for s in range(2)]
    assert k.at - k.base <= AT_RING
    k.go(AT_LOW)
    k.hh = k.sb("hh", [P, KT, TOK], F32R)
    k.hl = k.sb("hl", [P, KT, TOK], F32R)
    assert k.at - k.base <= AT_RING
    k.go(AT_RING)
    xT = k.sb("xT", [P, KT, TOK])
    k.go(AT_HIGH)
    xin = k.sb("xin", [P, TOK // P, D_MODEL])
    sq = [k.sb(f"sq{s}", [P, TOK]) for s in range(2)]
    k.go(AT_HIGH)
    norm = k.sb("norm", [P, 2, TOK])
    rstd = k.sb("rstd1", [P, TOK])

    x_loaded = [k.sem(f"x_loaded{t}") for t in range(2)]
    const_ready, zero_ready = k.sem("const_ready"), k.sem("zero_ready")
    d_loaded, d_ready = k.sem("d_loaded"), k.sem("d_ready")
    par_loaded, c_loaded, c_ready = k.sem("par_loaded"), k.sem("c_loaded"), k.sem("c_ready")
    gp_loaded = k.sem("gp_loaded")
    xt_done, xt_kept, sq_done, ss_done = (k.sem(n) for n in ("xt_done", "xt_kept", "sq_done", "ss_done"))
    ada_loaded = [k.sem(f"ada_loaded{s}") for s in range(2)]
    ada_done, row_kept, turn_done, mod_kept = (k.sem(n) for n in ("ada_done", "row_kept", "turn_done", "mod_kept"))
    par_done, par_kept = k.sem("par_done"), k.sem("par_kept")
    std_ready, rstd_ready, gain_ready = k.sem("std_ready"), k.sem("rstd_ready"), k.sem("gain_ready")
    n_scaled, n_mod, hi_done, lo_done = (k.sem(n) for n in ("n_scaled", "n_mod", "h_hi_done", "h_lo_done"))
    xt_stored = k.sem("xt_stored")
    g_ready = k.sem("g_ready")
    NADA = G1 * D_MODEL // 512

    x2 = io["x"].rearrange("b (t p) d -> p (b t) d", p=P)
    c2 = io["ctx"].rearrange("b (t p) d -> p (b t) d", p=P)
    adaw_d = io["ada_w"].rearrange("l (p k) n -> p (l k) n", p=P)
    adab_d = io["ada_b"]

    def rows(name, per):
        return io[name].rearrange(per, p=P)

    vec_rows = [("norm1", rows("norm1_g", "l (j p) -> (l j) p")), ("norm2", rows("norm2_g", "l (j p) -> (l j) p")),
                ("final", rows("final_norm_g", "(j p) -> j p")), ("dn_norm", io["dn_norm_g"]),
                ("ssd_norm", rows("ssd_norm_g", "l (j p) -> (l j) p")), ("ml_norm", rows("ml_norm_g", "l (j p) -> (l j) p")),
                ("ssd_cb", rows("ssd_conv_b", "l (j p) -> (l j) p")), ("lru_cb", rows("lru_conv_b", "l (j p) -> (l j) p")),
                ("lru_ba", rows("lru_b_a", "l d (j p) -> (l d j) p")), ("lru_bi", rows("lru_b_i", "l d (j p) -> (l d j) p")),
                ("lru_lam", rows("lru_lambda", "l d (j p) -> (l d j) p"))]

    with nc.Block() as block:
        @block.sync
        def _(sp):
            sp.dma_start(xin[:, 0:CTX // P, :], c2).then_inc(x_loaded[0], 16)
            sp.dma_start(xin[:, CTX // P:, :], x2).then_inc(x_loaded[1], 16)
            for t in range(NADA):
                s = t % 2
                if t >= 2:
                    sp.wait_ge(ada_done, t - 1)
                    sp.wait_ge(row_kept, t - 1)
                sp.dma_start(adaw[s][:], adaw_d[:, :, t * 512:(t + 1) * 512]).then_inc(ada_loaded[s], 16)
                sp.dma_start(biasrow[s][:], adab_d[:, t * 512:(t + 1) * 512].to_broadcast([2, 512])).then_inc(ada_loaded[s], 16)
            sp.wait_ge(xt_kept, 2 * KT)
            sp.dma_start(k.xT_dram, xT[:, :, CTX:]).then_inc(xt_stored, 16)
            sp.wait_ge(xt_stored, 16)

        @block.gpsimd
        def _(pool):
            pool.memset(k.ident[:], 0.0).then_inc(zero_ready, 1)
            pool.memset(k.ones[:], 1.0).then_inc(const_ready, 1)
            pool.memset(k.eps[:], EPS).then_inc(const_ready, 1)
            pool.memset(sheet[:], 0.0).then_inc(zero_ready, 1)
            pool.memset(k.gpar[:], 0.0).then_inc(zero_ready, 1)
            pool.wait_ge(zero_ready, 1)
            pool.affine_select(out=k.ident[:], in_=k.ident[:], compare_op=ALU.not_equal, fill=1.0, base=0,
                               pattern=[[-1, P]], channel_multiplier=1).then_inc(const_ready, 1)

        @block.scalar
        def _(act):
            act.wait_ge(zero_ready, 3)
            act.dma_start(dval[:], io["ssd_d"]).then_inc(d_loaded, 16)
            act.dma_start(cvec[:, 0, :], io["c"].rearrange("b (p k) -> p (b k)", p=P)).then_inc(c_loaded, 16)
            act.dma_start(cvec[:, 1, :], io["c_ctx"].rearrange("(p k) -> p k", p=P)).then_inc(c_loaded, 16)
            for name, src in vec_rows:
                at = PAR[name]
                act.dma_start(sheet[at:at + src.shape[0], 0, :], src).then_inc(par_loaded, 16)
            act.dma_start(sheet[0:60, 1, :], rows("dn_conv_w", "l t (j p) -> (l t j) p")).then_inc(par_loaded, 16)
            act.dma_start(sheet[60:100, 1, :], rows("ssd_conv_w", "l t (j p) -> (l t j) p")).then_inc(par_loaded, 16)
            act.dma_start(sheet[100:120, 1, :], rows("lru_conv_w", "l t (j p) -> (l t j) p")).then_inc(par_loaded, 16)
            ffn_rows = rows("ffn_conv_w", "l t (j p) -> (l t j) p")
            act.dma_start(sheet[0:88, 2, :], ffn_rows[0:88]).then_inc(par_loaded, 16)
            act.dma_start(sheet[0:44, 3, :], ffn_rows[88:132]).then_inc(par_loaded, 16)
            act.dma_start(sheet[0:N_LATE, 4, :], rows("ada_b", "l (j p) -> (l j) p")[G1 * KT:]).then_inc(par_loaded, 16)
            for d in range(2):
                for at, n, col, name in ((R_DN, 4, GP_ALOG, "dn_a_log"), (R_DN, 4, GP_BIAS, "dn_dt_bias"),
                                         (R_SSD, 8, GP_ALOG, "ssd_a_log"), (R_SSD, 8, GP_BIAS, "ssd_dt_bias"),
                                         (R_ML, 4, GP_BIAS, "ml_fg_b"), (R_ML, 4, GP_IGB, "ml_ig_b")):
                    act.dma_start(k.gpar[32 * d + at:32 * d + at + n, col:col + 1],
                                  io[name][0:1, d, :].rearrange("l h -> h l")).then_inc(gp_loaded, 16)
            act.wait_ge(d_loaded, 16)
            act.activation(dwide[:].rearrange("a (h p) -> a h p", p=SSD_P),
                           dval[:].unsqueeze(2).to_broadcast([1, SSD_HEADS, SSD_P]), ACT.Copy).then_inc(d_ready, 1)
            act.wait_ge(d_ready, 1)
            act.dma_start(sheet[PAR["ssd_d"]:PAR["ssd_d"] + 4, 0, :],
                          dwide[:].rearrange("a (j p) -> a j p", p=P)).then_inc(par_loaded, 16)
            act.wait_ge(c_loaded, 32)
            act.activation(k.csil[:].rearrange("p k b -> p b k"), cvec[:], ACT.Silu).then_inc(c_ready, 1)
            for i in range(KT):
                act.wait_ge(xt_kept, 2 * (i + 1))
                if i >= 2:
                    act.wait_ge(ss_done, i - 1)
                act.activation(sq[i % 2][:], xT[:, i, :], ACT.Square).then_inc(sq_done, 1)
            act.wait_ge(ss_done, KT)
            act.wait_ge(const_ready, 3)
            act.activation(rstd[:, CTX:], k.psum[4][:], ACT.Ln, scale=1.0 / D_MODEL, bias=k.eps[:]).then_inc(std_ready, 1)
            act.activation(rstd[:, 0:CTX], k.psum[5][:, 0:CTX], ACT.Ln, scale=1.0 / D_MODEL, bias=k.eps[:]).then_inc(std_ready, 1)
            act.wait_ge(std_ready, 2)
            act.activation(rstd[:], rstd[:], ACT.Exp, scale=-0.5).then_inc(rstd_ready, 1)
            act.wait_ge(gp_loaded, 16 * 12)
            act.activation(k.gpar[0:64, GP_COEF:GP_COEF + 1], k.gpar[0:64, GP_ALOG:GP_ALOG + 1], ACT.Exp).then_inc(g_ready, 1)
            for i in range(KT):
                act.wait_ge(n_scaled, i + 1)
                if i == 0:
                    act.wait_ge(gain_ready, 2)
                for part, cols in ((0, slice(CTX, TOK)), (1, slice(0, CTX))):
                    act.activation(norm[:, i % 2, cols], norm[:, i % 2, cols], ACT.Identity,
                                   bias=k.mod[:, SH1 * KT + i, part:part + 1],
                                   scale=k.gain1[:, part, i:i + 1]).then_inc(n_mod, 1)
                act.wait_ge(n_mod, 2 * (i + 1))
                act.activation(k.hh[:, i, :], norm[:, i % 2, :], ACT.Copy).then_inc(hi_done, 1)

        @block.tensor
        def _(pe):
            pe.wait_ge(const_ready, 3)
            pe.wait_ge(x_loaded[0], 16)
            pe.wait_ge(x_loaded[1], 16)
            for i in range(KT):
                if i >= 2:
                    pe.wait_ge(xt_kept, 2 * (i - 1))
                for t in range(CTX // P):
                    pe.transpose(k.psum[2 + i % 2][:, t * P:(t + 1) * P], xin[:, t, i * P:(i + 1) * P], k.ident[:])
                for t in range(SEQ // P):
                    mm = pe.transpose(k.psum[i % 2][:, t * P:(t + 1) * P], xin[:, CTX // P + t, i * P:(i + 1) * P], k.ident[:])
                mm.then_inc(xt_done, 1)
            pe.wait_ge(par_loaded, 16 * (len(vec_rows) + 7))
            pe.wait_ge(xt_kept, 2 * KT)
            for n, (r, at) in enumerate(((N_VEC, 0), (N_CW, N_VEC), (88, N_VEC + N_CW), (44, N_VEC + N_CW + 88), (N_LATE, PAR["ada_b"]))):
                mm = pe.transpose(k.psum[1][:, at:at + r], sheet[0:r, n, :], k.ident[0:r, 0:r])
            mm.then_inc(par_done, 1)
            for i in range(KT):
                pe.wait_ge(sq_done, i + 1)
                pe.matmul(k.psum[4][:], k.ones[:], sq[i % 2][:, CTX:], start=(i == 0), stop=(i == KT - 1))
                pe.matmul(k.psum[5][:, 0:CTX], k.ones[:], sq[i % 2][:, 0:CTX], start=(i == 0), stop=(i == KT - 1)).then_inc(ss_done, 1)
            pe.wait_ge(c_ready, 1)

            def turn(t):
                pe.wait_ge(row_kept, t + 1)
                for q in range(4):
                    j = 4 * t + q
                    mm = pe.transpose(k.psum[0][:, 2 * j:2 * j + 2], modrow[t % 2][:, q * P:(q + 1) * P], k.ident[0:2, 0:2])
                mm.then_inc(turn_done, 1)

            for t in range(NADA):
                s = t % 2
                pe.wait_ge(ada_loaded[s], 32 * (t // 2 + 1))
                if t >= 2:
                    pe.wait_ge(row_kept, t - 1)
                for i in range(KT):
                    mm = pe.matmul(k.psum[6 + s][0:2, :], k.csil[:, i, :], adaw[s][:, i, :], start=(i == 0), stop=(i == KT - 1))
                mm.then_inc(ada_done, 1)
                if t >= 1:
                    turn(t - 1)
            turn(NADA - 1)

        @block.vector
        def _(dve):
            for i in range(KT):
                dve.wait_ge(xt_done, i + 1)
                dve.tensor_copy(xT[:, i, CTX:], k.psum[i % 2][:]).then_inc(xt_kept, 1)
                dve.tensor_copy(xT[:, i, 0:CTX], k.psum[2 + i % 2][:, 0:CTX]).then_inc(xt_kept, 1)
            dve.wait_ge(par_done, 1)
            dve.tensor_copy(k.par[:], k.psum[1][:, 0:N_PAR]).then_inc(par_kept, 1)
            for t in range(NADA):
                dve.wait_ge(ada_done, t + 1)
                dve.wait_ge(ada_loaded[t % 2], 32 * (t // 2 + 1))
                if t >= 2:
                    dve.wait_ge(turn_done, t - 1)
                dve.tensor_tensor(modrow[t % 2][:], k.psum[6 + t % 2][0:2, :], biasrow[t % 2][:], ALU.add).then_inc(row_kept, 1)
            dve.wait_ge(turn_done, NADA)
            dve.tensor_copy(k.mod[:, 0:G1 * KT, :], k.psum[0][:, 0:2 * G1 * KT].rearrange("p (j b) -> p j b", b=2)).then_inc(mod_kept, 1)
            dve.wait_ge(mod_kept, 1)
            dve.wait_ge(par_kept, 1)
            for part in range(2):
                dve.scalar_tensor_tensor(out=k.gain1[:, part, :], in0=k.mod[:, SC1 * KT:(SC1 + 1) * KT, part], scalar=1.0,
                                         in1=k.par[:, PAR["norm1"]:PAR["norm1"] + KT], op0=ALU.add, op1=ALU.mult).then_inc(gain_ready, 1)
            dve.wait_ge(const_ready, 3)
            dve.wait_ge(gp_loaded, 16 * 12)
            dve.reduce_sum(k.gpar[0:64, GP_ML:GP_ML + 1], k.ident[0:64, R_ML:R_ML + 4], axis=mybir.AxisListType.X).then_inc(g_ready, 1)
            dve.reduce_sum(k.gpar[0:64, GP_SIGN:GP_SIGN + 1], k.ident[0:64, 32 + R_ML:32 + R_ML + 4], axis=mybir.AxisListType.X).then_inc(g_ready, 1)
            dve.wait_ge(g_ready, 3)
            dve.tensor_tensor(k.gpar[0:64, GP_ML:GP_ML + 1], k.gpar[0:64, GP_ML:GP_ML + 1], k.gpar[0:64, GP_SIGN:GP_SIGN + 1], ALU.add).then_inc(g_ready, 1)
            dve.wait_ge(g_ready, 4)
            dve.tensor_scalar(k.gpar[0:64, GP_SIGN:GP_SIGN + 1], k.gpar[0:64, GP_ML:GP_ML + 1], -2.0, 1.0, ALU.mult, ALU.add).then_inc(g_ready, 1)
            dve.tensor_scalar(k.gpar[0:64, GP_COEF:GP_COEF + 1], k.gpar[0:64, GP_COEF:GP_COEF + 1], -1.0, None, ALU.mult).then_inc(g_ready, 1)
            dve.wait_ge(rstd_ready, 1)
            for i in range(KT):
                if i >= 2:
                    dve.wait_ge(lo_done, i - 1)
                dve.tensor_tensor(norm[:, i % 2, :], xT[:, i, :], rstd[:], ALU.mult).then_inc(n_scaled, 1)
                if i >= 1:
                    dve.wait_ge(hi_done, i)
                    dve.tensor_tensor(k.hl[:, i - 1, :], norm[:, (i - 1) % 2, :], k.hh[:, i - 1, :].bitcast(F32), ALU.subtract).then_inc(lo_done, 1)
            dve.wait_ge(hi_done, KT)
            dve.tensor_tensor(k.hl[:, KT - 1, :], norm[:, (KT - 1) % 2, :], k.hh[:, KT - 1, :].bitcast(F32), ALU.subtract).then_inc(lo_done, 1)
            dve.wait_ge(lo_done, KT)




def open_ring(k):
    k.go(AT_RING)
    k.raw = k.sb("raw", [P, 2, KT, P])
    k.hi = k.sb("w_hi", [P, 2, KT, P], F32R)
    k.lo = k.sb("w_lo", [P, 2, KT, P], F32R)
    assert k.at - k.base <= AT_HIGH


class Ring:

    def __init__(self, k, name):
        self.k = k
        self.loaded = [k.sem(f"{name}_raw_loaded{s}") for s in range(2)]
        self.split = k.sem(f"{name}_weights_split")
        self.rounded = k.sem(f"{name}_weights_rounded")
        self.used = k.sem(f"{name}_weights_used")
        self.kept = k.sem(f"{name}_product_kept")

    def load(self, sp, t, s, source, rows=KT):
        sp.wait_ge(self.split, t + 1)
        sp.dma_start(self.k.raw[:, s, 0:rows, :], source).then_inc(self.loaded[s], 16)

    def round(self, act, t, half, s):
        act.wait_ge(self.loaded[s], half * 16 + 16)
        act.wait_ge(self.used, t + 1)
        act.activation(self.k.hi[:, s], self.k.raw[:, s], ACT.Copy).then_inc(self.rounded, 1)

    def subtract(self, pool, t, s):
        pool.wait_ge(self.rounded, t + 1)
        pool.tensor_tensor(self.k.lo[:, s], self.k.raw[:, s], self.k.hi[:, s].bitcast(F32), ALU.subtract).then_inc(self.split, 1)

    def multiply(self, pe, t, s, outs, kt=KT, kept=None):
        k = self.k
        pe.wait_ge(self.split, t + 3)
        pe.wait_ge(*(kept or (self.kept, t + 1)))
        for i in range(kt):
            for bank, hi, lo in outs:
                pe.matmul(bank, k.hi[:, s, i, :], hi[:, i, :], start=(i == 0), stop=False)
                pe.matmul(bank, k.hi[:, s, i, :], lo[:, i, :], start=False, stop=False)
            for bank, hi, lo in outs:
                mm = pe.matmul(bank, k.lo[:, s, i, :], hi[:, i, :], start=False, stop=(i == kt - 1))
        mm.then_inc(self.used, 1)


ADA_STEPS = N_LATE // 2


def projections(k):
    nc, io = k.nc, k.io
    open_ring(k)
    k.go(AT_HIGH)
    pad = [k.sb(f"pad{s}", [P, TOK + 8]) for s in range(2)]
    acc = [k.sb(f"acc{s}", [P, TOK + 4]) for s in range(2)]
    done = [k.sb(f"done{s}", [P, TOK]) for s in range(2)]
    cw = [k.sb(f"cw{s}", [P, SHORT]) for s in range(2)]
    cb = [k.sb(f"cb{s}", [P, 1]) for s in range(2)]
    wgin = k.sb("wgin", [P, KT, 48])
    gates = [k.sb(f"gate_rows{s}", [64, TOK]) for s in range(2)]
    part_sum = [[k.sb(f"ada_sum{s}{e}", [P, 2 * P]) for e in range(2)] for s in range(2)]
    gates_at = k.at - k.base
    wg = k.sb("wg", [P, KT, P])
    wgh = k.sb("wgh", [P, KT, P], F32R)
    wgl = k.sb("wgl", [P, KT, P], F32R)
    top = k.at
    k.go(gates_at)
    adaw = [k.sb(f"late_adaw{q}", [P, KT // 2, 2 * P]) for q in range(2)]
    assert k.at <= top
    k.at = top
    assert k.at <= nc.sbuf_usable_end, k.at
    CX, LT, LATENT = 2, CTX + 6, CTX + 4

    ring = Ring(k, "in")
    gate_loaded, gate_zero, gate_set = k.sem("gate_loaded"), k.sem("gate_zero"), k.sem("gate_set")
    gate_hi, gate_lo, gate_done, gate_kept = (k.sem(n) for n in ("gate_hi", "gate_lo", "gate_done", "gate_kept"))
    gate_stored = k.sem("gate_stored")
    pad_zero, filled, convolved = k.sem("pad_zero"), k.sem("pad_filled"), k.sem("convolved")
    cw_set, tapped, finished = k.sem("cw_set"), k.sem("tapped"), k.sem("tile_finished")
    stored = [k.sem(f"tile_stored{s}") for s in range(2)]
    ada_in = [k.sem(f"late_ada_in{q}") for q in range(2)]
    ada_steps, ada_half, ada_summed, ada_turned, mod_made = (k.sem(n) for n in ("ada_steps", "ada_half_read", "ada_summed", "ada_turned", "late_mod_made"))
    ada_d = io["ada_w"].rearrange("l (p k) n -> p (l k) n", p=P)
    w = io["w_in"].rearrange("l (k p) n -> p (l k) n", p=P)
    lat, ctx = slice(CTX, TOK), slice(0, CTX)

    def conv_before(t0):
        return sum(n for a, n, _, what in REGIONS if a < t0 and what in ("conv", "lru"))

    with nc.Block() as block:
        @block.sync
        def _(sp):
            for n, (col, width) in enumerate(((DN_A, 16), (SSD_DT, 16), (ML_I, 16))):
                sp.dma_start(wgin[:, :, 16 * n:16 * n + 16], w[:, :, col:col + width]).then_inc(gate_loaded, 16)
            for t0, n, col in COLUMN_RUNS:
                with sp.Fori(0, n // 2) as j:
                    for s in range(2):
                        ring.load(sp, j * 2 + (t0 + s), s, w[:, :, bass.ds(j * (2 * P) + (col + s * P), P)])
                        if not 2 <= t0 < ADA_STEPS + 2:
                            continue
                        step = t0 + s - 2
                        sp.wait_ge(gate_done, 1)
                        for q in range(2):
                            if q == 0:
                                sp.wait_ge(ada_half, j * 2 + (step + 1))
                            else:
                                sp.wait_ge(ada_summed, j * 4 + (step * 2 + 2))
                            sp.dma_start(adaw[q][:], ada_d[:, q * (KT // 2):(q + 1) * (KT // 2),
                                                           bass.ds(j * (4 * P) + (G1 * D_MODEL + 2 * step * P), 2 * P)]
                                         ).then_inc(ada_in[q], 16)
            sp.wait_ge(gate_kept, 2)
            for s in range(2):
                sp.dma_start(k.rows_dram[s], gates[s][:]).then_inc(gate_stored, 16)
            sp.wait_ge(gate_stored, 32)

        @block.gpsimd
        def _(pool):
            pool.sem_inc(ring.split, 2)
            pool.memset(wg[:], 0.0).then_inc(gate_zero, 1)
            for s in range(2):
                pool.memset(pad[s][:], 0.0).then_inc(pad_zero, 1)
            pool.wait_ge(gate_loaded, 48)
            pool.wait_ge(gate_zero, 1)
            for d in range(2):
                for dst, src, n in ((32 * d + R_DN, 4 * d, 4), (32 * d + R_SSD, 16 + 8 * d, 8), (32 * d + R_ML, 40 + 4 * d, 4),
                                    (64 + 32 * d + R_DN, 8 + 4 * d, 4), (64 + 32 * d + R_ML, 32 + 4 * d, 4)):
                    pool.tensor_copy(wg[:, :, dst:dst + n], wgin[:, :, src:src + n]).then_inc(gate_set, 1)
            pool.wait_ge(gate_hi, 1)
            pool.tensor_tensor(wgl[:], wg[:], wgh[:].bitcast(F32), ALU.subtract).then_inc(gate_lo, 1)
            with pool.Fori(0, TILES // 2) as j:
                for s in range(2):
                    ring.subtract(pool, j * 2 + s, s)

        @block.scalar
        def _(act):
            act.wait_ge(gate_set, 10)
            act.activation(wgh[:], wg[:], ACT.Copy).then_inc(gate_hi, 1)
            for s in range(2):
                ring.round(act, s, 0, s)
            act.wait_ge(gate_done, 1)
            act.activation(gates[0][:, lat], k.psum[4][0:64, :], ACT.Copy)
            act.activation(gates[0][:, ctx], k.psum[5][0:64, ctx], ACT.Copy).then_inc(gate_kept, 1)
            act.activation(gates[1][:, lat], k.psum[4][64:128, :], ACT.Copy)
            act.activation(gates[1][:, ctx], k.psum[5][64:128, ctx], ACT.Copy).then_inc(gate_kept, 1)

            def tile(t, half, s, has_ctx, what, nconv, more):
                act.wait_ge(ring.used, t + 3)
                if what in ("conv", "lru"):
                    place, bank = pad[s][:, LT:LT + SEQ], k.psum[s][:]
                    if what == "lru":
                        place = place.rearrange("p (w r) -> p r w", r=GRID_ROWS)
                        bank = bank.rearrange("p (r w) -> p r w", r=GRID_ROWS)
                    if has_ctx:
                        act.activation(pad[s][:, CX:CX + CTX], k.psum[2 + s][:, ctx], ACT.Copy).then_inc(filled, 1)
                    else:
                        act.sem_inc(filled, 1)
                    act.activation(place, bank, ACT.Copy).then_inc(filled, 1)
                    act.wait_ge(filled, (nconv + 1) * 2)
                    act.sem_inc(ring.kept, 1)
                if more:
                    ring.round(act, t + 2, half + 1, s)
                act.wait_ge(stored[s], half * 16 + 16)
                if what in ("conv", "lru"):
                    act.wait_ge(convolved, nconv + 1)
                    func = ACT.Silu if what == "conv" else ACT.Identity
                    if has_ctx:
                        act.activation(done[s][:, ctx], acc[s][:, ctx], func, bias=cb[s][:])
                    act.activation(done[s][:, lat], acc[s][:, LATENT:LATENT + SEQ], func, bias=cb[s][:]).then_inc(finished, 1)
                    act.wait_ge(finished, t + 3)
                else:
                    func = {"silu": ACT.Silu, "gelu": ACT.Gelu_apprx_tanh, "sigmoid": ACT.Sigmoid, "copy": ACT.Copy}[what]
                    if has_ctx:
                        act.activation(done[s][:, ctx], k.psum[2 + s][:, ctx], func)
                    act.activation(done[s][:, lat], k.psum[s][:], func).then_inc(finished, 1)
                    act.wait_ge(finished, t + 3)
                    act.sem_inc(ring.kept, 1)
                cols = slice(0 if has_ctx else CTX, TOK)
                act.dma_start(k.proj[bass.ds(t, 1), :, cols].rearrange("t p n -> (t p) n"), done[s][:, cols]).then_inc(stored[s], 16)

            for s in range(2):
                act.sem_inc(stored[s], 16)
            act.sem_inc(ring.kept, 2)
            act.sem_inc(finished, 2)
            act.wait_ge(pad_zero, 2)
            for t0, n, has_ctx, what in REGIONS:
                before = conv_before(t0)
                last = t0 + n == TILES
                with act.Fori(0, n // 2 - last) as j:
                    for s in range(2):
                        tile(j * 2 + (t0 + s), j + t0 // 2, s, has_ctx, what, j * 2 + (before + s), True)
            for s in range(2):
                tile(TILES - 2 + s, TILES // 2 - 1, s, REGIONS[-1][2], REGIONS[-1][3], 0, False)
            for s in range(2):
                act.wait_ge(stored[s], 16 * (TILES // 2 + 1))

        @block.tensor
        def _(pe):
            pe.sem_inc(ring.used, 2)
            pe.wait_ge(gate_lo, 1)
            for i in range(KT):
                for bank, cols in ((k.psum[4][:], lat), (k.psum[5][:, ctx], ctx)):
                    pe.matmul(bank, wgh[:, i, :], k.hh[:, i, cols], start=(i == 0), stop=False)
                    pe.matmul(bank, wgh[:, i, :], k.hl[:, i, cols], start=False, stop=False)
                    mm = pe.matmul(bank, wgl[:, i, :], k.hh[:, i, cols], start=False, stop=(i == KT - 1))
            mm.then_inc(gate_done, 1)
            pe.sem_inc(ada_turned, 1)

            def turn(t, bank, s):
                pe.wait_ge(ada_summed, t * 2 + 2)
                for q in range(2):
                    for e in range(2):
                        mm = pe.matmul(bank(q), part_sum[s][e][:, q * P:(q + 1) * P], k.ones[:, 0:1], start=(e == 0), stop=(e == 1))
                mm.then_inc(ada_turned, 1)

            for t0, n, has_ctx, what in REGIONS:
                with pe.Fori(0, n // 2) as j:
                    for s in range(2):
                        outs = [(k.psum[s][:], k.hh[:, :, lat], k.hl[:, :, lat])]
                        if has_ctx:
                            outs.append((k.psum[2 + s][:, ctx], k.hh[:, :, ctx], k.hl[:, :, ctx]))
                        ring.multiply(pe, j * 2 + (t0 + s), s, outs)
                        if t0 < ADA_STEPS:
                            turn(j * 2 + (t0 + s), lambda q: k.psum[6][:, bass.ds(j * 4 + (2 * (t0 + s) + q), 1)], 1 - s)
                if t0 + n == ADA_STEPS:
                    turn(ADA_STEPS, lambda q: k.psum[6][:, 2 * ADA_STEPS + q:2 * ADA_STEPS + q + 1], 1)

        @block.vector
        def _(dve):
            def conv(t, s, table, first, taps_apart, bias, nconv, has_ctx):
                dve.wait_ge(finished, t + 1)
                dve.tensor_copy(cw[s][:], table(first, taps_apart)).then_inc(cw_set, 1)
                if bias is None:
                    dve.memset(cb[s][:], 0.0).then_inc(cw_set, 1)
                else:
                    dve.tensor_copy(cb[s][:], k.par[:, bass.ds(bias, 1)]).then_inc(cw_set, 1)
                dve.wait_ge(cw_set, (nconv + 1) * 2)
                dve.wait_ge(filled, (nconv + 1) * 2)
                lo = 0 if has_ctx else LATENT
                view = acc[s][:, lo:]
                dve.tensor_scalar(view, pad[s][:, lo:TOK + 4], cw[s][:, 0:1], None, ALU.mult).then_inc(tapped, 1)
                for tap in range(1, SHORT):
                    dve.wait_ge(tapped, nconv * (SHORT - 1) + tap)
                    ins = dve.scalar_tensor_tensor(out=view, in0=pad[s][:, lo + tap:TOK + 4 + tap], scalar=cw[s][:, tap:tap + 1],
                                                   in1=view, op0=ALU.mult, op1=ALU.add)
                    ins.then_inc(tapped if tap < SHORT - 1 else convolved, 1)

            def table(first, apart):
                return k.par[:, bass.ds(first, SHORT, step=apart)]

            def macs(t, i):
                if i == KT // 2 - 1:
                    return ada_half, t + 2
                return ada_steps, t * (KT - 3) + (i + 1 if i < KT // 2 - 1 else i)

            def ada(t, s):
                dve.wait_ge(ada_turned, t + 1)
                for i in range(KT):
                    q, row = i // (KT // 2), i % (KT // 2)
                    if row == 0:
                        dve.wait_ge(ada_in[q], t * 16 + 16)
                    to, c = part_sum[s][i % 2][:], k.csil[:, i, 0:1]
                    if i < 2:
                        ins = dve.tensor_scalar(to, adaw[q][:, row, :], c, None, ALU.mult)
                    else:
                        dve.wait_ge(*macs(t, i - 2))
                        ins = dve.scalar_tensor_tensor(out=to, in0=adaw[q][:, row, :], scalar=c, in1=to, op0=ALU.mult, op1=ALU.add)
                    if i == KT // 2 - 1:
                        ins.then_inc(ada_half, 1)
                    elif i >= KT - 2:
                        ins.then_inc(ada_summed, 1)
                    else:
                        ins.then_inc(ada_steps, 1)

            dve.sem_inc(ada_half, 1)
            for e in range(2):
                dve.memset(part_sum[1][e][:], 0.0).then_inc(ada_summed, 1)
            for t0, n, has_ctx, what in REGIONS:
                if what not in ("conv", "lru"):
                    if t0 < ADA_STEPS:
                        with dve.Fori(0, n // 2) as j:
                            for s in range(2):
                                ada(j * 2 + (t0 + s), s)
                    continue
                before = conv_before(t0)
                if t0 < T_Z:
                    first, apart, bias = PAR["dn_cw"] + t0, 12, None
                elif what == "lru":
                    first, apart, bias = PAR["lru_cw"], 4, PAR["lru_cb"]
                else:
                    c = {T_SX: 0, T_SB: 4, T_SC: 6}[t0]
                    first, apart, bias = PAR["ssd_cw"] + c, 8, PAR["ssd_cb"] + c
                with dve.Fori(0, n // 2) as j:
                    for s in range(2):
                        if t0 < ADA_STEPS:
                            ada(j * 2 + (t0 + s), s)
                        conv(j * 2 + (t0 + s), s, table, j * 2 + (first + s), apart,
                             None if bias is None else j * 2 + (bias + s), j * 2 + (before + s), has_ctx)
            dve.wait_ge(ada_turned, ADA_STEPS + 2)
            dve.tensor_tensor(k.mod[:, G1 * KT:, 0], k.psum[6][:, 2:2 * ADA_STEPS + 2], k.par[:, PAR["ada_b"]:PAR["ada_b"] + N_LATE],
                              ALU.add).then_inc(mod_made, 1)
            dve.wait_ge(mod_made, 1)
            dve.scalar_tensor_tensor(out=k.gain2[:], in0=k.mod[:, SC2 * KT:(SC2 + 1) * KT, 0], scalar=1.0,
                                     in1=k.par[:, PAR["norm2"]:PAR["norm2"] + KT], op0=ALU.add, op1=ALU.mult)




class Steps:

    def __init__(self, engine, sem):
        self.engine, self.sem, self.count = engine, sem, 0

    def __call__(self, ins):
        self.count += 1
        ins.then_inc(self.sem, 1)
        self.engine.wait_ge(self.sem, self.count)


LOG1P_TERMS = 7


def softplus_exp(steps, act, z, e):
    steps(act.activation(e, z, ACT.Abs))
    steps(act.activation(e, e, ACT.Exp, scale=-1.0))


def softplus_sum(steps, dve, z, e, s, u):
    steps(dve.tensor_scalar(s, e, 2.0, None, ALU.add))
    steps(dve.reciprocal(s, s))
    steps(dve.tensor_tensor(s, s, e, ALU.mult))
    steps(dve.tensor_tensor(e, s, s, ALU.mult))
    steps(dve.tensor_scalar(u, e, 1.0 / (2 * LOG1P_TERMS + 1), None, ALU.mult))
    for n in range(LOG1P_TERMS - 1, 0, -1):
        steps(dve.scalar_tensor_tensor(out=u, in0=u, scalar=1.0 / (2 * n + 1), in1=e, op0=ALU.add, op1=ALU.mult))
    steps(dve.scalar_tensor_tensor(out=u, in0=u, scalar=1.0, in1=s, op0=ALU.add, op1=ALU.mult))
    steps(dve.tensor_scalar(u, u, 2.0, None, ALU.mult))
    steps(dve.scalar_tensor_tensor(out=z, in0=z, scalar=0.0, in1=u, op0=ALU.max, op1=ALU.add))


LEVELS = 7
COL_C, COL_W, COL_BETA, COL_DT, COL_NBE = range(5)


def gate_rows(k):
    nc, io = k.nc, k.io
    k.go(AT_LOW)
    row = {n: k.sb(f"row_{n}", [64, TOK]) for n in ("R", "E", "beta", "xm")}
    k.row = row
    k.gcol = k.sb("gcol", [P, 5, CHUNKS, 64])
    k.decay = k.sb("decay", [P, 2, CHUNKS, GROWS])
    k.sel_at = k.at - k.base
    k.sel = k.sb("sel", [64, 2, GROWS, P])
    k.causal = k.sb("causal", [P, 2, P])
    k.level = k.sb("level", [P, 2, LEVELS, P])
    k.at_mix = k.at - k.base
    assert k.at_mix <= AT_LOW + 48 * KB
    raw = [k.sb(f"gate_raw{s}", [64, TOK]) for s in range(2)]
    e, s_, u, m, ld, cs, c_row, w_row, nbe, reset = (k.sb(f"row_{n}", [64, TOK]) for n in
                                                    ("e", "s", "u", "m", "ld", "cs", "c", "w", "nbe", "reset"))
    ms = k.sb("m_start", [64, CHUNKS])
    rl = k.sb("r_last", [64, CHUNKS])
    el = k.sb("e_last", [64, CHUNKS])
    dg = k.sb("decay_diag", [64, 2, CHUNKS, GROWS])
    nml = k.sb("minus_ml", [64, 1])

    loaded, pool_steps, a_steps, v_steps = (k.sem(n) for n in ("rows_loaded", "mask_steps", "gate_act_steps", "gate_dve_steps"))
    masks, z_ready, exp_ready, rc_ready, ms_ready = (k.sem(n) for n in ("masks_ready", "z_ready", "exp_ready", "rc_ready", "ms_ready"))
    e_ready, rows_ready, dg_ready, turned, cols_kept = (k.sem(n) for n in ("e_rows_ready", "rows_ready", "dg_ready", "rows_turned", "gcols_kept"))
    fwd, bwd = slice(0, 32), slice(32, 64)
    gp = lambda c, rows=slice(0, 64): k.gpar[rows, c:c + 1]

    with nc.Block() as block:
        @block.sync
        def _(sp):
            for s in range(2):
                sp.dma_start(raw[s][:], k.rows_dram[s]).then_inc(loaded, 16)

        @block.gpsimd
        def _(pool):
            step = Steps(pool, pool_steps)
            step(pool.memset(reset[:], 1.0))
            step(pool.memset(reset[fwd, 0:TOK:P], 0.0))
            step(pool.memset(reset[bwd, P - 1:TOK:P], 0.0))
            pool.sem_inc(masks, 1)
            step(pool.memset(dg[:], 0.0))
            step(pool.memset(k.sel[:], 0.0))
            step(pool.affine_select(out=k.sel[:], in_=k.sel[:], compare_op=ALU.not_equal, fill=1.0, base=0,
                                    pattern=[[-32, 2], [-1, GROWS], [0, P]], channel_multiplier=1))
            pool.sem_inc(masks, 1)
            step(pool.memset(k.causal[:], 0.0))
            for d, sign in ((0, 1), (1, -1)):
                step(pool.affine_select(out=k.causal[:, d, :], in_=k.causal[:, d, :], compare_op=ALU.is_ge, fill=NEG, base=0,
                                        pattern=[[sign, P]], channel_multiplier=-sign))
            step(pool.memset(k.level[:], 0.0))
            for d in range(2):
                for lv in range(LEVELS):
                    h = 1 << lv
                    view = k.level[:, d, lv, :].rearrange("p (a b r) -> p a b r", b=2, r=h)[:, :, 1 - d, :]
                    step(pool.memset(view, 1.0))
                    step(pool.affine_select(out=view, in_=view, compare_op=ALU.is_ge, fill=0.0, base=-h * d,
                                            pattern=[[-2 * h, P // (2 * h)], [0, h]], channel_multiplier=1))
                    step(pool.affine_select(out=view, in_=view, compare_op=ALU.is_ge, fill=0.0, base=h - 1 + h * d,
                                            pattern=[[2 * h, P // (2 * h)], [0, h]], channel_multiplier=-1))

        @block.scalar
        def _(act):
            step = Steps(act, a_steps)
            act.wait_ge(z_ready, 1)
            softplus_exp(step, act, raw[0][:], e[:])
            act.sem_inc(exp_ready, 1)
            act.wait_ge(loaded, 32)
            step(act.activation(row["beta"][:], raw[1][:], ACT.Sigmoid))
            act.wait_ge(rc_ready, 1)
            for c in range(CHUNKS):
                cols = slice(c * P, (c + 1) * P)
                act.activation(row["E"][:, cols], row["R"][:, cols], ACT.Exp, bias=ms[:, c:c + 1])
                act.activation(w_row[:, cols], c_row[:, cols], ACT.Exp, scale=-1.0, bias=rl[:, c:c + 1])
            step(act.activation(row["xm"][:], m[:], ACT.Exp, scale=-1.0))
            act.sem_inc(e_ready, 1)

        @block.vector
        def _(dve):
            step = Steps(dve, v_steps)
            dve.wait_ge(loaded, 32)
            step(dve.tensor_scalar(raw[0][:], raw[0][:], gp(GP_BIAS), gp(GP_SIGN), ALU.add, ALU.mult))
            dve.sem_inc(z_ready, 1)
            dve.wait_ge(exp_ready, 1)
            softplus_sum(step, dve, raw[0][:], e[:], s_[:], u[:])
            step(dve.tensor_scalar(ld[:], raw[0][:], gp(GP_COEF), None, ALU.mult))
            dve.wait_ge(masks, 1)
            dve.tensor_tensor_scan(cs[fwd, :], reset[fwd, :], ld[fwd, :], 0.0, ALU.mult, ALU.add)
            step(dve.tensor_tensor_scan(cs[bwd, ::-1], reset[bwd, ::-1], ld[bwd, ::-1], 0.0, ALU.mult, ALU.add))
            step(dve.tensor_scalar(u[:], raw[1][:], gp(GP_IGB), None, ALU.add))
            step(dve.tensor_tensor_scan(m[fwd, :], ld[fwd, :], u[fwd, :], 0.0, ALU.add, ALU.max))
            step(dve.tensor_tensor_scan(m[bwd, CTX - 1::-1], ld[bwd, CTX - 1::-1], u[bwd, CTX - 1::-1], 0.0, ALU.add, ALU.max))
            step(dve.tensor_tensor_scan(m[bwd, TOK - 1:CTX - 1:-1], ld[bwd, TOK - 1:CTX - 1:-1], u[bwd, TOK - 1:CTX - 1:-1],
                                        m[bwd, 0:1], ALU.add, ALU.max))
            step(dve.tensor_scalar(nml[:], gp(GP_ML), -1.0, None, ALU.mult))
            step(dve.scalar_tensor_tensor(out=row["R"][:], in0=m[:], scalar=nml[:], in1=cs[:], op0=ALU.mult, op1=ALU.add))
            step(dve.scalar_tensor_tensor(out=c_row[:], in0=u[:], scalar=nml[:], in1=cs[:], op0=ALU.mult, op1=ALU.add))
            step(dve.memset(ms[:], 0.0))
            dve.tensor_copy(ms[fwd, 1:CHUNKS], m[fwd, P - 1:TOK - P:P])
            dve.tensor_copy(ms[bwd, 0:1], m[bwd, P:P + 1])
            dve.tensor_copy(ms[bwd, CHUNKS - 1:CHUNKS], m[bwd, 0:1])
            dve.tensor_copy(ms[bwd, CTX_CHUNKS:CHUNKS - 1], m[bwd, CTX + P:TOK:P])
            dve.tensor_copy(rl[fwd, :], row["R"][fwd, P - 1:TOK:P])
            step(dve.tensor_copy(rl[bwd, :], row["R"][bwd, 0:TOK:P]))
            step(dve.tensor_scalar(ms[:], ms[:], gp(GP_ML), None, ALU.mult))
            dve.sem_inc(rc_ready, 1)
            dve.wait_ge(e_ready, 1)
            step(dve.scalar_tensor_tensor(out=nbe[:], in0=row["E"][:], scalar=-1.0, in1=row["beta"][:], op0=ALU.mult, op1=ALU.mult))
            dve.sem_inc(rows_ready, 1)
            dve.wait_ge(masks, 2)
            dve.tensor_copy(el[fwd, :], row["E"][fwd, P - 1:TOK:P])
            step(dve.tensor_copy(el[bwd, :], row["E"][bwd, 0:TOK:P]))
            for d in range(2):
                rows = slice(32 * d, 32 * d + 32)
                step(dve.tensor_tensor(dg[rows, d], el[rows, :].unsqueeze(2).to_broadcast([32, CHUNKS, GROWS]),
                                       k.ident[rows, 32 * d:32 * d + GROWS].unsqueeze(1).to_broadcast([32, CHUNKS, GROWS]), ALU.mult))
            dve.sem_inc(dg_ready, 1)
            dve.wait_ge(turned, 1)
            for n in range(5):
                step(dve.tensor_copy(k.gcol[:, n], k.psum[n][:, 0:CHUNKS * 64].rearrange("p (c g) -> p c g", g=64)))
            step(dve.tensor_copy(k.decay[:], k.psum[5][:, 0:2 * CHUNKS * GROWS].rearrange("p (d c g) -> p d c g", d=2, g=GROWS)))

        @block.tensor
        def _(pe):
            pe.wait_ge(rows_ready, 1)
            for n, source in enumerate((c_row, w_row, row["beta"], raw[0], nbe)):
                for c in range(CHUNKS):
                    pe.transpose(k.psum[n][:, c * 64:(c + 1) * 64], source[:, c * P:(c + 1) * P], k.ident[0:64, 0:64])
            pe.wait_ge(dg_ready, 1)
            pe.matmul(k.psum[5][:, 0:2 * CHUNKS * GROWS], k.ones[0:64, :], dg[:].rearrange("p d c g -> p (d c g)"),
                      start=True, stop=True).then_inc(turned, 1)


def rglru(k):
    nc, io = k.nc, k.io
    LT, U = GROUP_W // P, 2 * GROUP_W // P
    k.go(k.at_mix)
    x = k.sb("lru_x", [P, LT, TOK])
    g = k.sb("lru_g", [P, LT, SEQ])
    w = k.sb("lru_w", [P, 2, U, P])
    r = k.sb("lru_r", [P, U, TOK])
    i_ = k.sb("lru_i", [P, U, TOK])
    q = k.sb("lru_q", [P, U, TOK])
    h = k.sb("lru_h", [P, U, TOK])
    y = k.sb("lru_y", [P, LT, SEQ])
    lam, le, ls, lu = (k.sb(f"lam_{n}", [P, U]) for n in "zesu")
    assert k.at <= nc.sbuf_usable_end, k.at
    x_in, g_in, w_in, w_zero = (k.sem(n) for n in ("lru_x_in", "lru_g_in", "lru_w_in", "lru_w_zero"))
    a_steps, v_steps, lam_z, lam_e = (k.sem(n) for n in ("lru_act_steps", "lru_dve_steps", "lam_z", "lam_e"))
    mult, gated, log_a, a_done = (k.sem(n) for n in ("lru_products", "lru_gated", "lru_log_a", "lru_a_made"))
    one_minus, rooted, y_made, y_stored = (k.sem(n) for n in ("lru_one_minus", "lru_rooted", "lru_y_made", "lru_y_stored"))
    par = lambda name, u: k.par[:, PAR[name] + u:PAR[name] + u + 1]
    lat, ctx = slice(CTX, TOK), slice(0, CTX)

    with nc.Block() as block:
        @block.sync
        def _(sp):
            sp.dma_start(x[:], k.proj[T_LX:T_LX + LT].rearrange("t p n -> p t n")).then_inc(x_in, 16)
            sp.dma_start(g[:], k.proj[T_LG:T_LG + LT, :, CTX:].rearrange("t p n -> p t n")).then_inc(g_in, 16)
            sp.wait_ge(w_zero, 1)
            for n, name in enumerate(("lru_w_a", "lru_w_i")):
                for half in range(2):
                    rows = slice(64 * half, 64 * half + 64)
                    src = io[name].rearrange("l d (t b) j c -> b j (l d t) c", b=2)[half]
                    sp.dma_start(w[rows, n, :, rows], src).then_inc(w_in, 16)
            sp.wait_ge(y_made, LT)
            sp.dma_start(k.mix[2 * LT:3 * LT].rearrange("t p n -> p t n"), y[:]).then_inc(y_stored, 16)
            sp.wait_ge(y_stored, 16)

        @block.gpsimd
        def _(pool):
            pool.memset(w[:], 0.0).then_inc(w_zero, 1)

        @block.tensor
        def _(pe):
            pe.wait_ge(x_in, 16)
            pe.wait_ge(w_in, 64)
            for u in range(U):
                t = u % LT
                if u >= 2:
                    pe.wait_ge(gated, u - 1)
                for n in range(2):
                    b = 4 * (u % 2) + 2 * n
                    pe.matmul(k.psum[b][:], w[:, n, u, :], x[:, t, lat], start=True, stop=True)
                    mm = pe.matmul(k.psum[b + 1][:, ctx], w[:, n, u, :], x[:, t, ctx], start=True, stop=True)
                mm.then_inc(mult, 1)

        @block.scalar
        def _(act):
            step = Steps(act, a_steps)
            act.wait_ge(lam_z, 1)
            softplus_exp(step, act, lam[:], le[:])
            act.sem_inc(lam_e, 1)
            for u in range(U):
                act.wait_ge(mult, u + 1)
                for n, (dst, bias) in enumerate(((r, "lru_ba"), (i_, "lru_bi"))):
                    b = 4 * (u % 2) + 2 * n
                    act.activation(dst[:, u, lat], k.psum[b][:], ACT.Sigmoid, bias=par(bias, u))
                    ins = act.activation(dst[:, u, ctx], k.psum[b + 1][:, ctx], ACT.Sigmoid, bias=par(bias, u))
                ins.then_inc(gated, 1)
            for u in range(U):
                act.wait_ge(log_a, u + 1)
                step(act.activation(q[:, u, :], r[:, u, :], ACT.Tanh, scale=-1.0))
                act.activation(r[:, u, :], r[:, u, :], ACT.Exp).then_inc(a_done, 1)
            for u in range(U):
                act.wait_ge(one_minus, u + 1)
                act.activation(q[:, u, :], q[:, u, :], ACT.Sqrt).then_inc(rooted, 1)

        @block.vector
        def _(dve):
            step = Steps(dve, v_steps)
            step(dve.tensor_scalar(lam[:], k.par[:, PAR["lru_lam"]:PAR["lru_lam"] + U], -1.0, None, ALU.mult))
            dve.sem_inc(lam_z, 1)
            dve.wait_ge(lam_e, 1)
            softplus_sum(step, dve, lam[:], le[:], ls[:], lu[:])
            step(dve.tensor_scalar(lam[:], lam[:], -8.0, None, ALU.mult))
            dve.wait_ge(x_in, 16)
            for u in range(U):
                dve.wait_ge(gated, u + 1)
                dve.tensor_scalar(r[:, u, :], r[:, u, :], lam[:, u:u + 1], None, ALU.mult).then_inc(log_a, 1)
                step(dve.tensor_tensor(i_[:, u, :], i_[:, u, :], x[:, u % LT, :], ALU.mult))
            for u in range(U):
                dve.wait_ge(a_done, u + 1)
                step(dve.tensor_tensor(h[:, u, :], r[:, u, :], r[:, u, :], ALU.mult))
                dve.scalar_tensor_tensor(out=q[:, u, :], in0=h[:, u, :], scalar=1.0, in1=q[:, u, :],
                                         op0=ALU.add, op1=ALU.mult).then_inc(one_minus, 1)
            dve.wait_ge(g_in, 16)
            for t in range(LT):
                for d in range(2):
                    u = d * LT + t
                    dve.wait_ge(rooted, u + 1)
                    step(dve.tensor_tensor(i_[:, u, :], i_[:, u, :], q[:, u, :], ALU.mult))
                    a, b, o = (z[:, u, :] for z in (r, i_, h))
                    if d == 0:
                        step(dve.tensor_tensor_scan(o[:, ctx], a[:, ctx], b[:, ctx], 0.0, ALU.mult, ALU.add))
                        step(dve.tensor_tensor_scan(o[:, lat], a[:, lat], b[:, lat], o[:, CTX - 1:CTX], ALU.mult, ALU.add))
                    else:
                        back_c, back_l = slice(CTX - 1, None, -1), slice(TOK - 1, CTX - 1, -1)
                        step(dve.tensor_tensor_scan(o[:, back_c], a[:, back_c], b[:, back_c], 0.0, ALU.mult, ALU.add))
                        step(dve.tensor_tensor_scan(o[:, back_l], a[:, back_l], b[:, back_l], o[:, 0:1], ALU.mult, ALU.add))
                step(dve.tensor_tensor(h[:, t, lat], h[:, t, lat], h[:, LT + t, lat], ALU.add))
                dve.tensor_tensor(y[:, t, :].rearrange("p (r w) -> p r w", r=GRID_ROWS),
                                  h[:, t, lat].rearrange("p (w r) -> p r w", r=GRID_ROWS),
                                  g[:, t, :].rearrange("p (r w) -> p r w", r=GRID_ROWS), ALU.mult).then_inc(y_made, 1)




class Finish:

    def __init__(self, k, name, o, per, gain, gate, first, sq, std):
        self.k, self.o, self.per, self.gain, self.gate, self.first, self.sq, self.std = k, o, per, gain, gate, first, sq, std
        self.ready, self.squared, self.summed, self.logged, self.rooted, self.made, self.stored = (
            k.sem(f"{name}_{x}") for x in ("o_ready", "o_squared", "o_summed", "o_logged", "o_rooted", "mix_made", "mix_stored"))
        self.steps = k.sem(f"{name}_finish_steps")

    def scalar(self, act):
        act.wait_ge(self.ready, 1)
        act.activation(self.sq[:], self.o[:], ACT.Square).then_inc(self.squared, 1)
        for n in range(4 // self.per):
            act.wait_ge(self.summed, n + 1)
            act.activation(self.std[:, n, :], self.k.psum[n][:], ACT.Ln, scale=1.0 / (P * self.per),
                           bias=self.k.eps[:]).then_inc(self.logged, 1)
        for n in range(4 // self.per):
            act.wait_ge(self.logged, n + 1)
            act.activation(self.std[:, n, :], self.std[:, n, :], ACT.Exp, scale=-0.5).then_inc(self.rooted, 1)

    def tensor(self, pe):
        pe.wait_ge(self.squared, 1)
        for t in range(4):
            n = t // self.per
            mm = pe.matmul(self.k.psum[n][:], self.k.ones[:], self.sq[:, t, :], start=(t % self.per == 0),
                           stop=(t % self.per == self.per - 1))
            if t % self.per == self.per - 1:
                mm.then_inc(self.summed, 1)

    def vector(self, dve):
        dve.sem_inc(self.ready, 1)
        step = Steps(dve, self.steps)
        for t in range(4):
            n = t // self.per
            dve.wait_ge(self.rooted, n + 1)
            ins = dve.scalar_tensor_tensor(out=self.o[:, t, :], in0=self.o[:, t, :], scalar=self.gain(t), in1=self.std[:, n, :],
                                           op0=ALU.mult, op1=ALU.mult)
            if self.gate is None:
                ins.then_inc(self.made, 1)
            else:
                step(ins)
                dve.tensor_tensor(self.o[:, t, :], self.o[:, t, :], self.gate[:, t, :], ALU.mult).then_inc(self.made, 1)

    def sync(self, sp):
        sp.wait_ge(self.made, 4)
        sp.dma_start(self.k.mix[self.first:self.first + 4].rearrange("t p n -> p t n"), self.o[:]).then_inc(self.stored, 16)
        sp.wait_ge(self.stored, 16)


UNITS = [(n, d) for n in range(CHUNKS) for d in range(2)]


def latent(n):
    return n >= CTX_CHUNKS


def cols(c):
    return slice(c * P, (c + 1) * P)


def lcols(c):
    return slice((c - CTX_CHUNKS) * P, (c - CTX_CHUNKS + 1) * P)


def first_visit(n, d):
    c = chunk_of(d, n)
    other = [m for m in range(CHUNKS) if chunk_of(1 - d, m) == c][0]
    return (n, d) < (other, 1 - d)


def heads(view):
    return view.rearrange("p (h n) -> p h n", h=4)


def mlstm(k):
    nc, io = k.nc, k.io
    k.go(k.at_mix)
    q = k.sb("ml_q", [P, 2, SEQ])
    kk = k.sb("ml_k", [P, 2, TOK])
    v = k.sb("ml_v", [P, 4, TOK])
    o_gate = k.sb("ml_o", [P, 4, SEQ])
    qz = k.sb("ml_qz", [P, ML_HEADS, SEQ])
    kt = k.sb("ml_kt", [P, CHUNKS, 2 * P])
    vt = k.sb("ml_vt", [P, CHUNKS, 4 * P])
    dm, st, qw, xm, ad, hh = ([k.sb(f"ml_{n}{d}", [P, 4, P]) for d in range(2)] for n in ("dm", "st", "qw", "xm", "ad", "hh"))
    wk = [k.sb(f"ml_wk{d}", [P, 4, ML_DK]) for d in range(2)]
    state = [k.sb(f"ml_state{d}", [P, 2, 2 * P]) for d in range(2)]
    o = k.sb("ml_out", [P, 4, SEQ])
    assert k.at <= nc.sbuf_usable_end, k.at
    S = lambda n: k.sem("ml_" + n)
    qkv_in, o_in, q_zero, q_set = S("qkv_in"), S("o_in"), S("q_zero"), S("q_set")
    turned, kt_kept, vt_kept = S("turned"), S("kt_kept"), S("vt_kept")
    rows_done, masked, decayed, scored, q_weighted, xm_kept = (S(n) for n in ("rows_done", "masked", "decayed", "scored", "q_weighted", "xm_kept"))
    num_done, den_kept, h_steps, out_added, wk_made, outer_done, state_kept = (
        S(n) for n in ("num_done", "den_kept", "h_steps", "out_added", "wk_made", "outer_done", "state_kept"))
    fin = Finish(k, "ml", o, 1, lambda t: k.par[:, PAR["ml_norm"] + t:PAR["ml_norm"] + t + 1], o_gate, 3 * 4, qz, v[:, :, 0:SEQ])
    gc = lambda what, c, d, h: k.gcol[:, what, c, 32 * d + R_ML + h:32 * d + R_ML + h + 1]
    L = lambda n, d: 2 * (n - CTX_CHUNKS) + d

    with nc.Block() as block:
        @block.sync
        def _(sp):
            sp.dma_start(kk[:], k.proj[T_MK:T_MK + 2].rearrange("t p n -> p t n")).then_inc(qkv_in, 16)
            sp.dma_start(v[:], k.proj[T_MV:T_MV + 4].rearrange("t p n -> p t n")).then_inc(qkv_in, 16)
            sp.dma_start(q[:], k.proj[T_MQ:T_MQ + 2, :, CTX:].rearrange("t p n -> p t n")).then_inc(qkv_in, 16)
            sp.dma_start(o_gate[:], k.proj[T_MO:T_MO + 4, :, CTX:].rearrange("t p n -> p t n")).then_inc(o_in, 16)
            fin.sync(sp)

        @block.gpsimd
        def _(pool):
            pool.memset(qz[:], 0.0).then_inc(q_zero, 1)
            for u, (n, d) in enumerate(UNITS):
                c = chunk_of(d, n)
                pool.wait_ge(kt_kept, c + 1)
                if n:
                    pool.wait_ge(outer_done, u - 1)
                pool.tensor_tensor(wk[d][:], kt[:, c, :].rearrange("p (h x) -> p h x", h=4),
                                   k.gcol[:, COL_W, c, 32 * d + R_ML:32 * d + R_ML + 4].unsqueeze(2).to_broadcast([P, 4, ML_DK]),
                                   ALU.mult).then_inc(wk_made, 1)

        @block.tensor
        def _(pe):
            pe.wait_ge(qkv_in, 48)
            for c in range(CHUNKS):
                b = 4 * (c % 2)
                if c >= 2:
                    pe.wait_ge(kt_kept, c - 1)
                    pe.wait_ge(vt_kept, c - 1)
                for t in range(4):
                    pe.transpose(k.psum[b][:, cols(t)], v[:, t, cols(c)], k.ident[:])
                for t in range(2):
                    mm = pe.transpose(k.psum[b + 1][:, cols(t)], kk[:, t, cols(c)], k.ident[:])
                mm.then_inc(turned, 1)
            pe.wait_ge(kt_kept, CHUNKS)
            pe.wait_ge(vt_kept, CHUNKS)
            pe.wait_ge(q_set, 2)
            for n in range(CHUNKS):
                for d in range(2):
                    if not latent(n):
                        continue
                    c, b = chunk_of(d, n), 4 * d
                    if L(n, d) >= 2:
                        pe.wait_ge(out_added, L(n, d) - 1)
                    pe.wait_ge(state_kept, 2 * n + d - 1)
                    for bank, row in ((b, "R"), (b + 2, "E"), (b + 3, "xm")):
                        for h in range(4):
                            pe.matmul(k.psum[bank][:, cols(h)], k.sel[:, d, R_ML + h, :], k.row[row][:, cols(c)], start=True, stop=True)
                    for h in range(4):
                        mm = pe.matmul(k.psum[b + 1][:, cols(h)], kk[:, h // 2, cols(c)], qz[:, h, lcols(c)], start=True, stop=True)
                    mm.then_inc(rows_done, 1)
                for d in range(2):
                    if not latent(n):
                        continue
                    c, b = chunk_of(d, n), 4 * d
                    pe.wait_ge(scored, L(n, d) + 1)
                    pe.wait_ge(q_weighted, L(n, d) + 1)
                    for h in range(4):
                        pe.matmul(k.psum[b][:, cols(h)], vt[:, c, cols(h)], st[d][:, h, :], start=True, stop=False)
                        pe.matmul(k.psum[b][:, cols(h)], state[d][:, h // 2, 0:P], qw[d][:, h, :], start=False, stop=True)
                    for h in range(4):
                        pe.matmul(k.psum[b + 1][:, cols(h)], k.ones[:], st[d][:, h, :], start=True, stop=False)
                        mm = pe.matmul(k.psum[b + 1][:, cols(h)], state[d][:, h // 2, P:2 * P], qw[d][:, h, :], start=False, stop=True)
                    mm.then_inc(num_done, 1)
                for d in range(2):
                    c, b, u = chunk_of(d, n), 4 * d, 2 * n + d
                    pe.wait_ge(wk_made, u + 1)
                    if n:
                        pe.wait_ge(state_kept, u - 1)
                    for h in range(4):
                        rows = slice(64 * (h % 2), 64 * (h % 2) + 64)
                        at = 256 * (h // 2)
                        pe.matmul(k.psum[b + 2][rows, at:at + P], wk[d][:, h, :], vt[:, c, cols(h)], start=True, stop=True)
                        mm = pe.matmul(k.psum[b + 2][rows, at + P:at + 2 * P], wk[d][:, h, :], k.ones[:], start=True, stop=True)
                    mm.then_inc(outer_done, 1)
            fin.tensor(pe)

        @block.scalar
        def _(act):
            for c in range(CHUNKS):
                act.wait_ge(turned, c + 1)
                act.activation(vt[:, c, :], k.psum[4 * (c % 2)][:], ACT.Copy).then_inc(vt_kept, 1)
            for n in range(CTX_CHUNKS, CHUNKS):
                for d in range(2):
                    act.wait_ge(rows_done, L(n, d) + 1)
                    act.activation(xm[d][:], heads(k.psum[4 * d + 3][:]), ACT.Copy).then_inc(xm_kept, 1)
                    act.wait_ge(masked, L(n, d) + 1)
                    act.activation(dm[d][:], dm[d][:], ACT.Exp).then_inc(decayed, 1)
                for d in range(2):
                    act.wait_ge(num_done, L(n, d) + 1)
                    act.activation(ad[d][:], heads(k.psum[4 * d + 1][:]), ACT.Abs).then_inc(den_kept, 1)
            fin.scalar(act)

        @block.vector
        def _(dve):
            step = Steps(dve, h_steps)
            dve.wait_ge(qkv_in, 48)
            dve.wait_ge(q_zero, 1)
            for half in range(2):
                rows = slice(64 * half, 64 * half + 64)
                dve.tensor_scalar(qz[rows, half::2, :], q[rows], ML_DK ** -0.5, None, ALU.mult).then_inc(q_set, 1)
            for c in range(CHUNKS):
                dve.wait_ge(turned, c + 1)
                dve.tensor_copy(kt[:, c, :], k.psum[4 * (c % 2) + 1][:, 0:2 * P]).then_inc(kt_kept, 1)
            for n in range(CHUNKS):
                for d in range(2):
                    if not latent(n):
                        continue
                    c, b = chunk_of(d, n), 4 * d
                    dve.wait_ge(rows_done, L(n, d) + 1)
                    for h in range(4):
                        ins = dve.scalar_tensor_tensor(out=dm[d][:, h, :], in0=k.psum[b][:, cols(h)], scalar=gc(COL_C, c, d, h),
                                                       in1=k.causal[:, d, :], op0=ALU.subtract, op1=ALU.min)
                    ins.then_inc(masked, 1)
                    dve.tensor_tensor(qw[d][:], qz[:, :, lcols(c)], heads(k.psum[b + 2][:]), ALU.mult).then_inc(q_weighted, 1)
                    dve.wait_ge(decayed, L(n, d) + 1)
                    dve.tensor_tensor(st[d][:], dm[d][:], heads(k.psum[b + 1][:]), ALU.mult).then_inc(scored, 1)
                for d in range(2):
                    if not latent(n):
                        continue
                    c, b = chunk_of(d, n), 4 * d
                    dve.wait_ge(den_kept, L(n, d) + 1)
                    dve.wait_ge(xm_kept, L(n, d) + 1)
                    step(dve.tensor_tensor(ad[d][:], ad[d][:], xm[d][:], ALU.max))
                    step(dve.reciprocal(ad[d][:], ad[d][:]))
                    if first_visit(n, d):
                        dve.tensor_tensor(o[:, :, lcols(c)], heads(k.psum[b][:]), ad[d][:], ALU.mult).then_inc(out_added, 1)
                    else:
                        step(dve.tensor_tensor(hh[d][:], heads(k.psum[b][:]), ad[d][:], ALU.mult))
                        dve.tensor_tensor(o[:, :, lcols(c)], o[:, :, lcols(c)], hh[d][:], ALU.add).then_inc(out_added, 1)
                    dve.wait_ge(out_added, L(n, d) + 1)
                for d in range(2):
                    c, u = chunk_of(d, n), 2 * n + d
                    dve.wait_ge(outer_done, u + 1)
                    new = k.psum[4 * d + 2][:].rearrange("p (a x) -> p a x", a=2)
                    if n == 0:
                        dve.tensor_copy(state[d][:], new).then_inc(state_kept, 1)
                        continue
                    dve.wait_ge(state_kept, u)
                    for h in range(4):
                        rows = slice(64 * (h % 2), 64 * (h % 2) + 64)
                        ins = dve.scalar_tensor_tensor(out=state[d][rows, h // 2, :], in0=state[d][rows, h // 2, :],
                                                       scalar=k.decay[rows, d, c, R_ML + h:R_ML + h + 1], in1=new[rows, h // 2, :],
                                                       op0=ALU.mult, op1=ALU.add)
                    ins.then_inc(state_kept, 1)
            dve.wait_ge(o_in, 16)
            fin.vector(dve)




def ssd(k):
    nc, io = k.nc, k.io
    k.go(k.at_mix)
    x = k.sb("ssd_x", [P, 4, TOK])
    z = k.sb("ssd_z", [P, 4, SEQ])
    bm = k.sb("ssd_b", [P, 2, TOK])
    cm = k.sb("ssd_c", [P, 2, SEQ])
    xt = k.sb("ssd_xt", [P, CHUNKS, 4 * P])
    bt = k.sb("ssd_bt", [P, CHUNKS, 2 * P])
    xd, xw, state = ([k.sb(f"ssd_{n}{d}", [P, SSD_HEADS, SSD_P]) for d in range(2)] for n in ("xd", "xw", "state"))
    dm, st, ce = ([k.sb(f"ssd_{n}{d}", [P, 4, P]) for d in range(2)] for n in ("dm", "st", "ce"))
    o = k.sb("ssd_out", [P, 4, SEQ])
    sq = k.sb("ssd_sq", [P, 4, SEQ])
    std = k.sb("ssd_std", [P, 2, SEQ])
    assert k.at <= nc.sbuf_usable_end, k.at
    S = lambda n: k.sem("ssd_" + n)
    xb_in, c_in, z_in = S("xb_in"), S("c_in"), S("z_in")
    turned, xt_kept, bt_kept = S("turned"), S("xt_kept"), S("bt_kept")
    rows_done, masked, decayed, scored, c_weighted = (S(n) for n in ("rows_done", "masked", "decayed", "scored", "c_weighted"))
    xd_made, xw_made, y_done, y_added, outer_done, state_steps, state_kept = (
        S(n) for n in ("xd_made", "xw_made", "y_done", "y_added", "outer_done", "state_steps", "state_kept"))
    fin = Finish(k, "ssd", o, 2, lambda t: k.par[:, PAR["ssd_norm"] + t:PAR["ssd_norm"] + t + 1], None, 4, sq, std)
    G = lambda n, g, d: ((n - CTX_CHUNKS) * 2 + g) * 2 + d

    def per_head(what, c, d, n):
        at = 32 * d + R_SSD
        return k.gcol[:, what, c, at:at + SSD_HEADS].unsqueeze(2).to_broadcast([P, SSD_HEADS, n])

    with nc.Block() as block:
        @block.sync
        def _(sp):
            sp.dma_start(x[:], k.proj[T_SX:T_SX + 4].rearrange("t p n -> p t n")).then_inc(xb_in, 16)
            sp.dma_start(bm[:], k.proj[T_SB:T_SB + 2].rearrange("t p n -> p t n")).then_inc(xb_in, 16)
            sp.dma_start(cm[:], k.proj[T_SC:T_SC + 2, :, CTX:].rearrange("t p n -> p t n")).then_inc(c_in, 16)
            sp.dma_start(z[:], k.proj[T_SZ:T_SZ + 4, :, CTX:].rearrange("t p n -> p t n")).then_inc(z_in, 16)
            fin.sync(sp)

        @block.gpsimd
        def _(pool):
            for u, (n, d) in enumerate(UNITS):
                c = chunk_of(d, n)
                pool.wait_ge(xt_kept, c + 1)
                if latent(n) and n > CTX_CHUNKS:
                    pool.wait_ge(y_done, G(n - 1, 1, d) + 1)
                pool.tensor_tensor(xd[d][:], xt[:, c, :].rearrange("p (h x) -> p h x", x=SSD_P), per_head(COL_DT, c, d, SSD_P),
                                   ALU.mult).then_inc(xd_made, 1)
                pool.wait_ge(xd_made, u + 1)
                if n:
                    pool.wait_ge(outer_done, u - 1)
                pool.tensor_tensor(xw[d][:], xd[d][:], per_head(COL_W, c, d, SSD_P), ALU.mult).then_inc(xw_made, 1)

        @block.tensor
        def _(pe):
            pe.wait_ge(xb_in, 32)
            for c in range(CHUNKS):
                b = 4 * (c % 2)
                if c >= 2:
                    pe.wait_ge(xt_kept, c - 1)
                    pe.wait_ge(bt_kept, c - 1)
                for t in range(4):
                    pe.transpose(k.psum[b][:, cols(t)], x[:, t, cols(c)], k.ident[:])
                for t in range(2):
                    mm = pe.transpose(k.psum[b + 1][:, cols(t)], bm[:, t, cols(c)], k.ident[:])
                mm.then_inc(turned, 1)
            pe.wait_ge(xt_kept, CHUNKS)
            pe.wait_ge(bt_kept, CHUNKS)
            pe.wait_ge(c_in, 16)
            for n in range(CHUNKS):
                for g in range(2):
                    if not latent(n):
                        continue
                    for d in range(2):
                        c, b, i = chunk_of(d, n), 4 * d, G(n, g, d)
                        if i >= 2:
                            pe.wait_ge(y_added, i - 1)
                            pe.wait_ge(c_weighted, i - 1)
                        for bank, row in ((b, "R"), (b + 1, "E")):
                            for h in range(4):
                                pe.matmul(k.psum[bank][:, cols(h)], k.sel[:, d, R_SSD + 4 * g + h, :], k.row[row][:, cols(c)], start=True, stop=True)
                        pe.matmul(k.psum[b + 2][:, 0:P], bm[:, g, cols(c)], cm[:, g, lcols(c)], start=True, stop=True).then_inc(rows_done, 1)
                    for d in range(2):
                        c, b, i = chunk_of(d, n), 4 * d, G(n, g, d)
                        pe.wait_ge(scored, i + 1)
                        pe.wait_ge(c_weighted, i + 1)
                        pe.wait_ge(xd_made, 2 * n + d + 1)
                        pe.wait_ge(state_kept, 2 * n + d - 1)
                        for h in range(4):
                            out = k.psum[b + 2][64 * (h % 2):64 * (h % 2) + 64, P * (1 + h // 2):P * (2 + h // 2)]
                            pe.matmul(out, xd[d][:, 4 * g + h, :], st[d][:, h, :], start=True, stop=False)
                            mm = pe.matmul(out, state[d][:, 4 * g + h, :], ce[d][:, h, :], start=False, stop=True)
                        mm.then_inc(y_done, 1)
                for d in range(2):
                    c, b, u = chunk_of(d, n), 4 * d, 2 * n + d
                    pe.wait_ge(xw_made, u + 1)
                    if n:
                        pe.wait_ge(state_kept, u - 1)
                    for g in range(2):
                        mm = pe.matmul(k.psum[b + 3][:, 256 * g:256 * g + 256], bt[:, c, cols(g)],
                                       xw[d][:, 4 * g:4 * g + 4, :].rearrange("p h x -> p (h x)"), start=True, stop=True)
                    mm.then_inc(outer_done, 1)
            fin.tensor(pe)

        @block.scalar
        def _(act):
            for c in range(CHUNKS):
                act.wait_ge(turned, c + 1)
                act.activation(xt[:, c, :], k.psum[4 * (c % 2)][:], ACT.Copy).then_inc(xt_kept, 1)
            for i in range(G(CHUNKS, 0, 0)):
                act.wait_ge(masked, i + 1)
                act.activation(dm[i % 2][:], dm[i % 2][:], ACT.Exp).then_inc(decayed, 1)
            fin.scalar(act)

        @block.vector
        def _(dve):
            step = Steps(dve, state_steps)
            for c in range(CHUNKS):
                dve.wait_ge(turned, c + 1)
                dve.tensor_copy(bt[:, c, :], k.psum[4 * (c % 2) + 1][:, 0:2 * P]).then_inc(bt_kept, 1)
            dve.wait_ge(c_in, 16)
            for n in range(CHUNKS):
                for g in range(2):
                    if not latent(n):
                        continue
                    for d in range(2):
                        c, b, i = chunk_of(d, n), 4 * d, G(n, g, d)
                        dve.wait_ge(rows_done, i + 1)
                        for h in range(4):
                            at = 32 * d + R_SSD + 4 * g + h
                            ins = dve.scalar_tensor_tensor(out=dm[d][:, h, :], in0=k.psum[b][:, cols(h)],
                                                           scalar=k.gcol[:, COL_C, c, at:at + 1],
                                                           in1=k.causal[:, d, :], op0=ALU.subtract, op1=ALU.min)
                        ins.then_inc(masked, 1)
                        dve.tensor_tensor(ce[d][:], heads(k.psum[b + 1][:]), cm[:, g, lcols(c)].unsqueeze(1).to_broadcast([P, 4, P]),
                                          ALU.mult).then_inc(c_weighted, 1)
                    for d in range(2):
                        c, b, i = chunk_of(d, n), 4 * d, G(n, g, d)
                        dve.wait_ge(decayed, i + 1)
                        dve.tensor_tensor(st[d][:], dm[d][:], k.psum[b + 2][:, 0:P].unsqueeze(1).to_broadcast([P, 4, P]),
                                          ALU.mult).then_inc(scored, 1)
                    for d in range(2):
                        c, b, i = chunk_of(d, n), 4 * d, G(n, g, d)
                        dve.wait_ge(y_done, i + 1)
                        y = k.psum[b + 2][:, P:3 * P].rearrange("p (t n) -> p t n", t=2)
                        out = o[:, 2 * g:2 * g + 2, lcols(c)]
                        if first_visit(n, d):
                            dve.tensor_copy(out, y).then_inc(y_added, 1)
                        else:
                            dve.tensor_tensor(out, out, y, ALU.add).then_inc(y_added, 1)
                for d in range(2):
                    c, u = chunk_of(d, n), 2 * n + d
                    dve.wait_ge(outer_done, u + 1)
                    new = k.psum[4 * d + 3][:].rearrange("p (h x) -> p h x", x=SSD_P)
                    if n == 0:
                        dve.tensor_copy(state[d][:], new).then_inc(state_kept, 1)
                        continue
                    dve.wait_ge(state_kept, u)
                    step(dve.tensor_tensor(state[d][:], state[d][:],
                                           k.decay[:, d, c, R_SSD:R_SSD + SSD_HEADS].unsqueeze(2).to_broadcast([P, SSD_HEADS, SSD_P]), ALU.mult))
                    dve.tensor_tensor(state[d][:], state[d][:], new, ALU.add).then_inc(state_kept, 1)
            dve.wait_ge(y_added, G(CHUNKS, 0, 0))
            dve.wait_ge(z_in, 16)
            for t in range(4):
                step(dve.scalar_tensor_tensor(out=o[:, t, :], in0=x[:, t, CTX:], scalar=k.par[:, PAR["ssd_d"] + t:PAR["ssd_d"] + t + 1],
                                              in1=o[:, t, :], op0=ALU.mult, op1=ALU.add))
            step(dve.tensor_tensor(o[:], o[:], z[:], ALU.mult))
            fin.vector(dve)


def deltanet(k):
    nc, io = k.nc, k.io
    k.go(k.at_mix)
    q = k.sb("dn_q", [P, 4, SEQ])
    kk = k.sb("dn_k", [P, 4, TOK])
    at = k.at
    v = k.sb("dn_v", [P, 4, TOK])
    k.at = at
    nt = k.sb("dn_nt", [P, 2 * CHUNKS, 4, P])
    kt = k.sb("dn_kt", [P, CHUNKS, 4 * P])
    vt = k.sb("dn_vt", [P, CHUNKS, 4 * P])
    pair = lambda n: [k.sb(f"dn_{n}{d}", [P, 4, P]) for d in range(2)]
    dm, X, vb, kw, state, xt_even = (pair(n) for n in ("dm", "x", "vb", "kw", "state", "xt_even"))
    Y = dm
    attn = k.sb("dn_attn", [P, 2 * (CHUNKS - CTX_CHUNKS), 4, P])
    qe = k.sb("dn_qe", [P, 2 * (CHUNKS - CTX_CHUNKS), 4, P])
    parts_at = k.at - k.base
    parts = [k.sb(f"dn_parts{d}", [P, LEVELS, 4, P]) for d in range(2)]
    top = k.at
    assert k.at <= nc.sbuf_usable_end, k.at
    k.go(parts_at)
    sq = [k.sb(f"dn_sq{s}", [P, TOK]) for s in range(2)]
    rn = [k.sb(f"dn_rn{s}", [P, TOK]) for s in range(2)]
    k.go(k.at_mix)
    o = k.sb("dn_out", [P, 4, SEQ])
    k.go(k.sel_at)
    vn, xt_odd = pair("vn"), pair("xt_odd")
    assert k.at - k.base <= k.sel_at + 2 * GROWS * P * 4
    XT = (xt_even, xt_odd)
    k.go(parts_at)
    z = k.sb("dn_z", [P, 4, SEQ])
    osq = k.sb("dn_osq", [P, 4, SEQ])
    ostd = k.sb("dn_ostd", [P, 4, SEQ])
    S = lambda n: k.sem("dn_" + n)
    qk_in, v_in, z_in = S("qk_in"), S("v_in"), S("z_in")
    squared, summed, logged, rooted, normed = S("squared"), S("summed"), S("logged"), S("rooted"), S("normed")
    turned, kt_kept, vt_kept = S("turned"), S("kt_kept"), S("vt_kept")
    rows_done, masked, decayed, beta_done, n_steps = (S(n) for n in ("rows_done", "masked", "decayed", "beta_done", "n_steps"))
    n_made, part_made, qk_done, attn_made, q_weighted = (S(n) for n in ("n_made", "part_made", "qk_done", "attn_made", "q_weighted"))
    nx_done, y_made, x_done, x_kept, xt_made, xt_done, xt_kept = (
        S(n) for n in ("nx_done", "y_made", "x_done", "x_kept", "xt_made", "xt_done", "xt_kept"))
    vk_made, ks_done, r_made, vn_done, vn_kept, out_done, out_added, outer_done, state_kept = (
        S(n) for n in ("vk_made", "ks_done", "r_made", "vn_done", "vn_kept", "out_done", "out_added", "outer_done", "state_kept"))
    fin = Finish(k, "dn", o, 1, lambda t: k.par[:, PAR["dn_norm"]:PAR["dn_norm"] + 1], z, 0, osq, ostd)
    L = lambda n, d: 2 * (n - CTX_CHUNKS) + d
    col = lambda what, c, d, h: k.gcol[:, what, c, 32 * d + R_DN + h:32 * d + R_DN + h + 1]

    def per_head(what, c, d):
        return k.gcol[:, what, c, 32 * d:32 * d + 4].unsqueeze(2).to_broadcast([P, 4, P])

    def over_heads(x):
        return x.unsqueeze(1).to_broadcast([P, 4, P])

    def y_count(n, lv, d):
        return 2 * (LEVELS * n + lv) + d + 1

    def xt_count(n, lv, d):
        return 2 * ((LEVELS - 1) * n + lv - 1) + d + 1

    def xk_count(n, lv, d):
        return 2 * ((LEVELS - 2) * n + lv - 1) + d + 1

    L2 = [(q, h, False) for h in range(4)] + [(kk, h, True) for h in range(4)]

    with nc.Block() as block:
        @block.sync
        def _(sp):
            sp.dma_start(q[:], k.proj[T_Q:T_Q + 4, :, CTX:].rearrange("t p n -> p t n")).then_inc(qk_in, 16)
            sp.dma_start(kk[:], k.proj[T_K:T_K + 4].rearrange("t p n -> p t n")).then_inc(qk_in, 16)
            sp.dma_start(v[:], k.proj[T_V:T_V + 4].rearrange("t p n -> p t n")).then_inc(v_in, 16)
            sp.wait_ge(out_added, L(CHUNKS, 0))
            sp.wait_ge(state_kept, 2 * CHUNKS)
            sp.dma_start(z[:], k.proj[T_Z:T_Z + 4, :, CTX:].rearrange("t p n -> p t n")).then_inc(z_in, 16)
            fin.sync(sp)

        @block.gpsimd
        def _(pool):
            for n in range(CHUNKS):
                for lv in range(LEVELS):
                    for d in range(2):
                        pool.wait_ge(n_made, 2 * n + d + 1)
                        if n:
                            pool.wait_ge(nx_done, y_count(n - 1, lv, d))
                        pool.tensor_tensor(parts[d][:, lv], nt[:, 2 * n + d], over_heads(k.level[:, d, lv, :]), ALU.mult).then_inc(part_made, 1)
                        if lv == 0:
                            pool.wait_ge(part_made, y_count(n, 0, d))
                            if n >= 2:
                                pool.wait_ge(vn_done, 2 * (n - 2) + d + 1)
                            pool.tensor_tensor(XT[n % 2][d][:], over_heads(k.ident[:]), parts[d][:, 0], ALU.subtract).then_inc(xt_made, 1)
                for d in range(2):
                    c = chunk_of(d, n)
                    pool.wait_ge(kt_kept, c + 1)
                    pool.wait_ge(vt_kept, c + 1)
                    if n:
                        pool.wait_ge(state_kept, 2 * (n - 1) + d + 1)
                    pool.tensor_tensor(vb[d][:], heads(vt[:, c, :]), per_head(COL_BETA, c, d), ALU.mult)
                    pool.tensor_tensor(kw[d][:], heads(kt[:, c, :]), per_head(COL_W, c, d), ALU.mult).then_inc(vk_made, 1)

        @block.tensor
        def _(pe):
            pe.wait_ge(qk_in, 32)
            for i, (x, h, has_ctx) in enumerate(L2):
                s = i % 2
                pe.wait_ge(squared, i + 1)
                if i >= 2:
                    pe.wait_ge(rooted, i - 1)
                mm = pe.matmul(k.psum[s][:], k.ones[:], sq[s][:, CTX:], start=True, stop=True)
                if has_ctx:
                    mm = pe.matmul(k.psum[2 + s][:, 0:CTX], k.ones[:], sq[s][:, 0:CTX], start=True, stop=True)
                mm.then_inc(summed, 1)
            pe.wait_ge(normed, len(L2))
            pe.wait_ge(v_in, 16)
            for c in range(CHUNKS):
                b = 4 * (c % 2)
                if c >= 2:
                    pe.wait_ge(kt_kept, c - 1)
                    pe.wait_ge(vt_kept, c - 1)
                for t in range(4):
                    pe.transpose(k.psum[b][:, cols(t)], v[:, t, cols(c)], k.ident[:])
                for t in range(4):
                    mm = pe.transpose(k.psum[b + 1][:, cols(t)], kk[:, t, cols(c)], k.ident[:])
                mm.then_inc(turned, 1)
            pe.wait_ge(kt_kept, CHUNKS)
            pe.wait_ge(vt_kept, CHUNKS)
            for n in range(CHUNKS):
                for d in range(2):
                    c, b, u = chunk_of(d, n), 4 * d, 2 * n + d
                    if n:
                        pe.wait_ge(n_made, u - 1)
                    if n > CTX_CHUNKS:
                        pe.wait_ge(attn_made, L(n, d) - 1)
                    for bank, row in ((b, "R"), (b + 1, "E"), (b + 2, "beta")):
                        if row == "E" and not latent(n):
                            continue
                        for h in range(4):
                            pe.matmul(k.psum[bank][:, cols(h)], k.sel[:, d, R_DN + h, :], k.row[row][:, cols(c)], start=True, stop=True)
                    for h in range(4):
                        mm = pe.matmul(k.psum[b + 3][:, cols(h)], kk[:, h, cols(c)], kk[:, h, cols(c)], start=True, stop=True)
                    mm.then_inc(rows_done, 1)
                for d in range(2):
                    if not latent(n):
                        continue
                    c, b, u = chunk_of(d, n), 4 * d, 2 * n + d
                    pe.wait_ge(beta_done, u + 1)
                    for h in range(4):
                        mm = pe.matmul(k.psum[b + 3][:, cols(h)], kk[:, h, cols(c)], q[:, h, lcols(c)], start=True, stop=True)
                    mm.then_inc(qk_done, 1)
            pe.wait_ge(n_made, 2 * CHUNKS)
            pe.wait_ge(attn_made, L(CHUNKS, 0))

            def level(n, lv):
                for d in range(2):
                    b = 4 * d
                    if lv >= 2:
                        pe.wait_ge(x_kept, xk_count(n, lv - 1, d))
                        if n or lv > 2:
                            pe.wait_ge(xt_kept, xt_count(n, lv - 1, d) - 2)
                        for h in range(4):
                            mm = pe.transpose(k.psum[b + 2][:, cols(h)], X[d][:, h, :], k.ident[:])
                        mm.then_inc(xt_done, 1)
                    pe.wait_ge(part_made, y_count(n, lv, d))
                    if lv or n:
                        pe.wait_ge(y_made, y_count(n, lv, d) - 2)
                    for h in range(4):
                        if lv == 0:
                            mm = pe.transpose(k.psum[b][:, cols(h)], parts[d][:, lv, h, :], k.ident[:])
                        else:
                            mm = pe.matmul(k.psum[b][:, cols(h)], parts[d][:, lv, h, :], X[d][:, h, :], start=True, stop=True)
                    mm.then_inc(nx_done, 1)
                for d in range(2):
                    if lv == 0:
                        continue
                    b = 4 * d
                    pe.wait_ge(y_made, y_count(n, lv, d))
                    if lv == 1:
                        pe.wait_ge(xt_made, 2 * n + d + 1)
                    else:
                        pe.wait_ge(xt_kept, xt_count(n, lv - 1, d))
                    if lv < LEVELS - 1:
                        for h in range(4):
                            mm = pe.matmul(k.psum[b + 1][:, cols(h)], XT[n % 2][d][:, h, :], Y[d][:, h, :], start=True, stop=True)
                        mm.then_inc(x_done, 1)
                    else:
                        for h in range(4):
                            mm = pe.matmul(k.psum[b + 2][:, cols(h)], Y[d][:, h, :], XT[n % 2][d][:, h, :], start=True, stop=True)
                        mm.then_inc(xt_done, 1)

            def behind(n, lv):
                for d in range(2):
                    c, bank, u = chunk_of(d, n), k.psum[4 * d + 3], 2 * n + d
                    if lv == 0 and n:
                        pe.wait_ge(state_kept, u - 1)
                        for h in range(4):
                            mm = pe.matmul(bank[:, cols(h)], kk[:, h, cols(c)], state[d][:, h, :], start=True, stop=True)
                        mm.then_inc(ks_done, 1)
                    elif lv == 1:
                        pe.wait_ge(xt_kept, xt_count(n, LEVELS - 1, d))
                        if n:
                            pe.wait_ge(r_made, u - 1)
                        else:
                            pe.wait_ge(vk_made, u + 1)
                        for h in range(4):
                            mm = pe.matmul(bank[:, cols(h)], XT[n % 2][d][:, h, :], vb[d][:, h, :], start=True, stop=True)
                        mm.then_inc(vn_done, 1)
                    elif lv == 2 and latent(n):
                        pe.wait_ge(vn_kept, u + 1)
                        for h in range(4):
                            pe.matmul(bank[:, cols(h)], state[d][:, h, :], qe[:, L(n, d), h, :], start=True, stop=False)
                            mm = pe.matmul(bank[:, cols(h)], vn[d][:, h, :], attn[:, L(n, d), h, :], start=False, stop=True)
                        mm.then_inc(out_done, 1)
                    elif lv == 3:
                        pe.wait_ge(vn_kept, u + 1)
                        pe.wait_ge(vk_made, u + 1)
                        if latent(n):
                            pe.wait_ge(out_added, L(n, d) + 1)
                        for h in range(4):
                            mm = pe.matmul(bank[:, cols(h)], kw[d][:, h, :], vn[d][:, h, :], start=True, stop=True)
                        mm.then_inc(outer_done, 1)

            for n in range(CHUNKS + 1):
                for lv in range(LEVELS):
                    if n < CHUNKS:
                        level(n, lv)
                    if n:
                        behind(n - 1, lv)
            fin.tensor(pe)

        @block.scalar
        def _(act):
            act.wait_ge(qk_in, 32)

            def root(i):
                x, h, has_ctx = L2[i]
                act.wait_ge(summed, i + 1)
                if i >= 2:
                    act.wait_ge(normed, i - 1)
                view = rn[i % 2][:, 0 if has_ctx else CTX:]
                ins = act.activation(rn[i % 2][:, CTX:], k.psum[i % 2][:], ACT.Ln, bias=k.eps[:])
                if has_ctx:
                    ins = act.activation(rn[i % 2][:, 0:CTX], k.psum[2 + i % 2][:, 0:CTX], ACT.Ln, bias=k.eps[:])
                ins.then_inc(logged, 1)
                act.wait_ge(logged, i + 1)
                act.activation(view, view, ACT.Exp, scale=-0.5).then_inc(rooted, 1)

            for i, (x, h, has_ctx) in enumerate(L2):
                if i >= 2:
                    act.wait_ge(summed, i - 1)
                if has_ctx:
                    act.activation(sq[i % 2][:], x[:, h, :], ACT.Square).then_inc(squared, 1)
                else:
                    act.activation(sq[i % 2][:, CTX:], x[:, h, :], ACT.Square).then_inc(squared, 1)
                if i >= 1:
                    root(i - 1)
            root(len(L2) - 1)
            for c in range(CHUNKS):
                act.wait_ge(turned, c + 1)
                act.activation(vt[:, c, :], k.psum[4 * (c % 2)][:], ACT.Copy).then_inc(vt_kept, 1)
            for n in range(CHUNKS):
                for d in range(2):
                    act.wait_ge(masked, 2 * n + d + 1)
                    act.activation(dm[d][:], dm[d][:], ACT.Exp).then_inc(decayed, 1)

            def turned_kept(n, lv, d):
                act.wait_ge(xt_done, xt_count(n, lv, d))
                act.activation(XT[n % 2][d][:], heads(k.psum[4 * d + 2][:]), ACT.Copy).then_inc(xt_kept, 1)

            for n in range(CHUNKS + 1):
                for lv in range(1, LEVELS):
                    if n < CHUNKS:
                        for d in range(2):
                            if lv >= 2:
                                turned_kept(n, lv - 1, d)
                        for d in range(2):
                            if lv < LEVELS - 1:
                                act.wait_ge(x_done, xk_count(n, lv, d))
                                act.activation(X[d][:], heads(k.psum[4 * d + 1][:]), ACT.Copy).then_inc(x_kept, 1)
                            else:
                                turned_kept(n, lv, d)
                    if n and lv == 1:
                        for d in range(2):
                            act.wait_ge(vn_done, 2 * (n - 1) + d + 1)
                            act.activation(vn[d][:], heads(k.psum[4 * d + 3][:]), ACT.Copy).then_inc(vn_kept, 1)
            fin.scalar(act)

        @block.vector
        def _(dve):
            for i, (x, h, has_ctx) in enumerate(L2):
                dve.wait_ge(rooted, i + 1)
                view = rn[i % 2][:, 0 if has_ctx else CTX:]
                dve.scalar_tensor_tensor(out=x[:, h, :], in0=x[:, h, :], scalar=1.0 if has_ctx else float(P) ** -0.5, in1=view,
                                         op0=ALU.mult, op1=ALU.mult).then_inc(normed, 1)
            for c in range(CHUNKS):
                dve.wait_ge(turned, c + 1)
                dve.tensor_copy(kt[:, c, :], k.psum[4 * (c % 2) + 1][:]).then_inc(kt_kept, 1)
            for n in range(CHUNKS):
                for d in range(2):
                    c, b, u = chunk_of(d, n), 4 * d, 2 * n + d
                    dve.wait_ge(rows_done, u + 1)
                    for h in range(4):
                        ins = dve.scalar_tensor_tensor(out=dm[d][:, h, :], in0=k.psum[b][:, cols(h)], scalar=col(COL_C, c, d, h),
                                                       in1=k.causal[:, d, :], op0=ALU.subtract, op1=ALU.min)
                    ins.then_inc(masked, 1)
                    if latent(n):
                        dve.tensor_tensor(qe[:, L(n, d)], q[:, :, lcols(c)], heads(k.psum[b + 1][:]), ALU.mult).then_inc(q_weighted, 1)
                for d in range(2):
                    c, b, u = chunk_of(d, n), 4 * d, 2 * n + d
                    dve.wait_ge(decayed, u + 1)
                    dve.tensor_tensor(nt[:, u], dm[d][:], heads(k.psum[b + 3][:]), ALU.mult).then_inc(beta_done, 1)
                    dve.wait_ge(beta_done, u + 1)
                    dve.tensor_tensor(nt[:, u], nt[:, u], heads(k.psum[b + 2][:]), ALU.mult).then_inc(n_made, 1)
                for d in range(2):
                    if latent(n):
                        dve.wait_ge(qk_done, L(n, d) + 1)
                        dve.tensor_tensor(attn[:, L(n, d)], dm[d][:], heads(k.psum[4 * d + 3][:]), ALU.mult).then_inc(attn_made, 1)

            def behind(n, lv):
                for d in range(2):
                    c, bank, u = chunk_of(d, n), k.psum[4 * d + 3], 2 * n + d
                    if lv == 0 and n:
                        dve.wait_ge(ks_done, u - 1)
                        dve.wait_ge(vk_made, u + 1)
                        for h in range(4):
                            ins = dve.scalar_tensor_tensor(out=vb[d][:, h, :], in0=bank[:, cols(h)], scalar=col(COL_NBE, c, d, h),
                                                           in1=vb[d][:, h, :], op0=ALU.mult, op1=ALU.add)
                        ins.then_inc(r_made, 1)
                    elif lv == 2 and latent(n):
                        dve.wait_ge(out_done, L(n, d) + 1)
                        out = o[:, :, lcols(c)]
                        if first_visit(n, d):
                            dve.tensor_copy(out, heads(bank[:])).then_inc(out_added, 1)
                        else:
                            dve.tensor_tensor(out, out, heads(bank[:]), ALU.add).then_inc(out_added, 1)
                    elif lv == 3:
                        dve.wait_ge(outer_done, u + 1)
                        if n == 0:
                            dve.tensor_copy(state[d][:], heads(bank[:])).then_inc(state_kept, 1)
                            continue
                        dve.wait_ge(state_kept, u - 1)
                        for h in range(4):
                            ins = dve.scalar_tensor_tensor(out=state[d][:, h, :], in0=state[d][:, h, :],
                                                           scalar=k.decay[:, d, c, R_DN + h:R_DN + h + 1],
                                                           in1=bank[:, cols(h)], op0=ALU.mult, op1=ALU.add)
                        ins.then_inc(state_kept, 1)

            for n in range(CHUNKS + 1):
                for lv in range(LEVELS):
                    if n < CHUNKS:
                        for d in range(2):
                            dve.wait_ge(nx_done, y_count(n, lv, d))
                            dve.tensor_tensor((X if lv == 0 else Y)[d][:], over_heads(k.ident[:]), heads(k.psum[4 * d][:]),
                                              ALU.subtract).then_inc(y_made, 1)
                    if n:
                        behind(n - 1, lv)
            dve.wait_ge(out_added, L(CHUNKS, 0))
            dve.wait_ge(z_in, 16)
            fin.vector(dve)




def output_projection(k):
    nc, io = k.nc, k.io
    k.go(AT_LOW)
    mh = k.sb("mix_hi", [P, KT, SEQ], F32R)
    ml = k.sb("mix_lo", [P, KT, SEQ], F32R)
    assert k.at - k.base <= AT_LAT
    k.go(AT_LAT)
    k.lat = k.sb("lat", [P, KT, SEQ])
    k.go(AT_HIGH)
    mixed = k.sb("mixed", [P, KT, SEQ])
    g1 = [k.sb(f"g1_{s}", [P, 1]) for s in range(2)]
    ring = Ring(k, "out")
    mix_loaded = [k.sem(f"mix_loaded{q}") for q in range(4)]
    lat_loaded, m_hi, m_lo, g1_set = (k.sem(n) for n in ("lat_loaded", "mix_hi_made", "mix_lo_made", "g1_set"))
    w = io["w_out"].rearrange("l (k p) n -> p (l k) n", p=P)

    with nc.Block() as block:
        @block.sync
        def _(sp):
            for q in range(4):
                sp.dma_start(mixed[:, 4 * q:4 * q + 4, :], k.mix[4 * q:4 * q + 4].rearrange("k p n -> p k n")).then_inc(mix_loaded[q], 16)
            for s in range(2):
                ring.load(sp, s, s, w[:, :, s * P:(s + 1) * P])
            sp.dma_start(k.lat[:], k.xT_dram).then_inc(lat_loaded, 16)
            with sp.Fori(1, KT // 2) as j:
                for s in range(2):
                    ring.load(sp, j * 2 + s, s, w[:, :, bass.ds(j * (2 * P) + s * P, P)])

        @block.gpsimd
        def _(pool):
            pool.sem_inc(ring.split, 2)
            with pool.Fori(0, KT // 2) as j:
                for s in range(2):
                    ring.subtract(pool, j * 2 + s, s)

        @block.scalar
        def _(act):
            for i in range(KT):
                act.wait_ge(mix_loaded[i // 4], 16)
                act.activation(mh[:, i, :], mixed[:, i, :], ACT.Copy).then_inc(m_hi, 1)
            with act.Fori(0, KT // 2) as j:
                for s in range(2):
                    ring.round(act, j * 2 + s, j, s)

        @block.tensor
        def _(pe):
            pe.sem_inc(ring.used, 2)
            pe.wait_ge(m_lo, KT)
            with pe.Fori(0, KT // 2) as j:
                for s in range(2):
                    ring.multiply(pe, j * 2 + s, s, [(k.psum[s][:], mh, ml)])

        @block.vector
        def _(dve):
            dve.sem_inc(ring.kept, 2)
            for i in range(KT):
                dve.wait_ge(m_hi, i + 1)
                dve.tensor_tensor(ml[:, i, :], mixed[:, i, :], mh[:, i, :].bitcast(F32), ALU.subtract).then_inc(m_lo, 1)
            dve.wait_ge(lat_loaded, 16)
            with dve.Fori(0, KT // 2) as j:
                for s in range(2):
                    t = j * 2 + s
                    dve.wait_ge(ring.kept, t + 1)
                    dve.tensor_copy(g1[s][:], k.mod[:, bass.ds(t + G1 * KT, 1), 0]).then_inc(g1_set, 1)
                    dve.wait_ge(g1_set, t + 1)
                    dve.wait_ge(ring.used, t + 3)
                    row = k.lat[:, bass.ds(t, 1), :].rearrange("p a n -> p (a n)")
                    dve.scalar_tensor_tensor(out=row, in0=k.psum[s][:], scalar=g1[s][:], in1=row,
                                             op0=ALU.mult, op1=ALU.add).then_inc(ring.kept, 1)
            dve.wait_ge(ring.kept, KT + 2)


FFN_PARTS = 4
F_PART = FT // FFN_PARTS
PART_TILES = 2 * F_PART + KT


def feed_forward(k):
    nc, io = k.nc, k.io
    k.go(AT_LOW)
    fh = k.sb("f_hi", [P, KT, SEQ], F32R)
    fl = k.sb("f_lo", [P, KT, SEQ], F32R)
    assert k.at - k.base <= AT_LAT
    k.go(AT_HIGH)
    ah = k.sb("a_hi", [P, F_PART, SEQ], F32R)
    al = k.sb("a_lo", [P, F_PART, SEQ], F32R)
    u_row = k.sb("u_row", [P, SEQ])
    g_pad = k.sb("g_pad", [P, SEQ + 2])
    g_acc = k.sb("g_acc", [P, SEQ])
    a_row = k.sb("a_row", [P, SEQ])
    fw = k.sb("fw", [P, 3])
    g2 = [k.sb(f"g2_{s}", [P, 1]) for s in range(2)]
    assert k.at <= nc.sbuf_usable_end, k.at
    k.go(AT_HIGH)
    sq = [k.sb(f"sq2_{s}", [P, SEQ]) for s in range(2)]
    std = k.sb("std2", [P, SEQ])
    normed = [k.sb(f"normed{s}", [P, SEQ]) for s in range(2)]
    moded = [k.sb(f"moded{s}", [P, SEQ]) for s in range(2)]

    ring = Ring(k, "ffn")
    sq_made, summed, std_made, rstd_made = (k.sem(n) for n in ("sq2_made", "sum2_done", "std2_made", "rstd2_made"))
    n_made, m_made, f_hi, f_lo = (k.sem(n) for n in ("norm2_made", "mod2_made", "f_hi_made", "f_lo_made"))
    u_kept, g_kept, pad_zero2 = k.sem("u_kept"), k.sem("g_kept"), k.sem("g_pad_zero")
    fw_set, g_tap, g_conv, g_act = (k.sem(n) for n in ("fw_set", "g_tap", "g_convolved", "g_activated"))
    a_made, a_hi, a_lo, g2_set = (k.sem(n) for n in ("a_made", "a_hi_made", "a_lo_made", "g2_set"))
    down_kept = k.sem("down_kept")
    up = io["ffn_w_up"].rearrange("l (k p) n -> p (l k) n", p=P)
    down = io["ffn_w_down"].rearrange("l (k p) n -> p (l k) n", p=P)
    flat = lambda x: x.rearrange("p a n -> p (a n)")

    with nc.Block() as block:
        @block.sync
        def _(sp):
            with sp.Fori(0, FFN_PARTS) as b:
                with sp.Fori(0, F_PART) as f:
                    for s in range(2):
                        ring.load(sp, b * PART_TILES + f * 2 + s, s,
                                  up[:, :, bass.ds(b * (F_PART * P) + f * P + s * D_FF, P)])
                with sp.Fori(0, KT // 2) as j:
                    for s in range(2):
                        ring.load(sp, b * PART_TILES + j * 2 + (2 * F_PART + s), s,
                                  down[:, bass.ds(b * F_PART, F_PART), bass.ds(j * (2 * P) + s * P, P)], F_PART)

        @block.gpsimd
        def _(pool):
            pool.sem_inc(ring.split, 2)
            pool.memset(g_pad[:], 0.0).then_inc(pad_zero2, 1)
            with pool.Fori(0, FFN_PARTS * PART_TILES // 2) as j:
                for s in range(2):
                    ring.subtract(pool, j * 2 + s, s)

        @block.scalar
        def _(act):
            for i in range(KT):
                if i >= 2:
                    act.wait_ge(summed, i - 1)
                act.activation(sq[i % 2][:], k.lat[:, i, :], ACT.Square).then_inc(sq_made, 1)
            act.wait_ge(summed, KT)
            act.activation(std[:], k.psum[4][:], ACT.Ln, scale=1.0 / D_MODEL, bias=k.eps[:]).then_inc(std_made, 1)
            act.wait_ge(std_made, 1)
            act.activation(std[:], std[:], ACT.Exp, scale=-0.5).then_inc(rstd_made, 1)
            for s in range(2):
                ring.round(act, s, 0, s)
            for i in range(KT):
                act.wait_ge(n_made, i + 1)
                if i >= 2:
                    act.wait_ge(f_lo, i - 1)
                act.activation(moded[i % 2][:], normed[i % 2][:], ACT.Identity, scale=k.gain2[:, i:i + 1],
                               bias=k.mod[:, SH2 * KT + i, 0:1]).then_inc(m_made, 1)
                act.wait_ge(m_made, i + 1)
                act.activation(fh[:, i, :], moded[i % 2][:], ACT.Copy).then_inc(f_hi, 1)
            act.wait_ge(pad_zero2, 1)
            act.sem_inc(ring.kept, 2)

            def up_pair(t, f, half):
                act.wait_ge(ring.used, t + 3)
                act.wait_ge(a_made, f)
                act.activation(u_row[:], k.psum[0][:], ACT.Copy).then_inc(u_kept, 1)
                act.wait_ge(u_kept, f + 1)
                act.sem_inc(ring.kept, 1)
                ring.round(act, t + 2, half + 1, 0)
                act.wait_ge(ring.used, t + 4)
                act.activation(g_pad[:, 1:SEQ + 1], k.psum[1][:], ACT.Copy).then_inc(g_kept, 1)
                act.wait_ge(g_kept, f + 1)
                act.sem_inc(ring.kept, 1)
                ring.round(act, t + 3, half + 1, 1)
                act.wait_ge(g_conv, f + 1)
                act.activation(g_acc[:], g_acc[:], ACT.Silu).then_inc(g_act, 1)

            def part(b, last):
                with act.Fori(0, F_PART) as f:
                    up_pair(b * PART_TILES + f * 2, b * F_PART + f, b * (PART_TILES // 2) + f)
                with act.Fori(0, KT // 2 - last) as j:
                    for s in range(2):
                        ring.round(act, b * PART_TILES + j * 2 + (2 * F_PART + 2 + s), b * (PART_TILES // 2) + j + (F_PART + 1), s)

            with act.Fori(0, FFN_PARTS - 1) as b:
                part(b, 0)
            part(FFN_PARTS - 1, 1)

        @block.tensor
        def _(pe):
            pe.sem_inc(ring.used, 2)
            for i in range(KT):
                pe.wait_ge(sq_made, i + 1)
                pe.matmul(k.psum[4][:], k.ones[:], sq[i % 2][:], start=(i == 0), stop=(i == KT - 1)).then_inc(summed, 1)
            pe.wait_ge(f_lo, KT)
            with pe.Fori(0, FFN_PARTS) as b:
                with pe.Fori(0, F_PART) as f:
                    for s in range(2):
                        ring.multiply(pe, b * PART_TILES + f * 2 + s, s, [(k.psum[s][:], fh, fl)],
                                      kept=(ring.kept, (b * F_PART + f) * 2 + (s + 1)))
                with pe.Fori(0, KT // 2) as j:
                    for s in range(2):
                        pe.wait_ge(a_lo, b * F_PART + F_PART)
                        ring.multiply(pe, b * PART_TILES + j * 2 + (2 * F_PART + s), s, [(k.psum[2 + s][:], ah, al)], F_PART,
                                      kept=(down_kept, b * KT + j * 2 + (s + 1)))

        @block.vector
        def _(dve):
            dve.sem_inc(down_kept, 2)
            dve.wait_ge(rstd_made, 1)

            def low(i):
                dve.wait_ge(f_hi, i + 1)
                dve.tensor_tensor(fl[:, i, :], moded[i % 2][:], fh[:, i, :].bitcast(F32), ALU.subtract).then_inc(f_lo, 1)

            for i in range(KT):
                if i >= 2:
                    dve.wait_ge(m_made, i - 1)
                dve.tensor_tensor(normed[i % 2][:], k.lat[:, i, :], std[:], ALU.mult).then_inc(n_made, 1)
                if i >= 1:
                    low(i - 1)
            low(KT - 1)
            dve.wait_ge(f_lo, KT)

            with dve.Fori(0, FFN_PARTS) as b:
                with dve.Fori(0, F_PART) as f_in:
                    f = b * F_PART + f_in
                    dve.tensor_copy(fw[:], k.par[:, bass.ds(f + PAR["ffn_cw"], 3, step=FT)]).then_inc(fw_set, 1)
                    dve.wait_ge(fw_set, f + 1)
                    dve.wait_ge(g_kept, f + 1)
                    dve.tensor_scalar(g_acc[:], g_pad[:, 0:SEQ], fw[:, 0:1], None, ALU.mult).then_inc(g_tap, 1)
                    dve.wait_ge(g_tap, f * 2 + 1)
                    dve.scalar_tensor_tensor(out=g_acc[:], in0=g_pad[:, 1:SEQ + 1], scalar=fw[:, 1:2], in1=g_acc[:],
                                             op0=ALU.mult, op1=ALU.add).then_inc(g_tap, 1)
                    dve.wait_ge(g_tap, f * 2 + 2)
                    dve.scalar_tensor_tensor(out=g_acc[:], in0=g_pad[:, 2:SEQ + 2], scalar=fw[:, 2:3], in1=g_acc[:],
                                             op0=ALU.mult, op1=ALU.add).then_inc(g_conv, 1)
                    dve.wait_ge(g_act, f + 1)
                    dve.wait_ge(u_kept, f + 1)
                    dve.tensor_tensor(a_row[:], g_acc[:], u_row[:], ALU.mult).then_inc(a_made, 1)
                    dve.wait_ge(a_made, f + 1)
                    dve.tensor_copy(flat(ah[:, bass.ds(f_in, 1), :]), a_row[:]).then_inc(a_hi, 1)
                    dve.wait_ge(a_hi, f + 1)
                    dve.tensor_tensor(flat(al[:, bass.ds(f_in, 1), :]), a_row[:], flat(ah[:, bass.ds(f_in, 1), :]).bitcast(F32),
                                      ALU.subtract).then_inc(a_lo, 1)
                    dve.wait_ge(a_lo, f + 1)
                with dve.Fori(0, KT // 2) as j:
                    for s in range(2):
                        t = b * PART_TILES + j * 2 + (2 * F_PART + s)
                        dve.wait_ge(down_kept, b * KT + j * 2 + (s + 1))
                        dve.tensor_copy(g2[s][:], k.mod[:, bass.ds(j * 2 + (G2 * KT + s), 1), 0]).then_inc(g2_set, 1)
                        dve.wait_ge(g2_set, b * KT + j * 2 + (s + 1))
                        dve.wait_ge(ring.used, t + 3)
                        row = flat(k.lat[:, bass.ds(j * 2 + s, 1), :])
                        dve.scalar_tensor_tensor(out=row, in0=k.psum[2 + s][:], scalar=g2[s][:], in1=row,
                                                 op0=ALU.mult, op1=ALU.add).then_inc(down_kept, 1)
            dve.wait_ge(down_kept, FFN_PARTS * KT + 2)


def final_norm(k):
    nc = k.nc
    k.go(AT_LOW)
    sq = [k.sb(f"sq3_{s}", [P, SEQ]) for s in range(2)]
    rstd = k.sb("rstd3", [P, SEQ])
    k.go(AT_RING)
    rows = k.sb("out_rows", [P, SEQ // P, D_MODEL])
    sq_made, summed, std_made, rstd_made = (k.sem(n) for n in ("sq3_made", "sum3_done", "std3_made", "rstd3_made"))
    f_made, turned, kept, stored = (k.sem(n) for n in ("final_made", "final_turned", "final_kept", "out_stored"))
    gain = k.par[:, PAR["final"]:PAR["final"] + KT]
    out = k.out.rearrange("b (t p) d -> p (b t) d", p=P)

    with nc.Block() as block:
        @block.sync
        def _(sp):
            for q in range(4):
                sp.wait_ge(kept, 4 * (q + 1))
                cols = slice(q * 512, (q + 1) * 512)
                sp.dma_start(out[:, :, cols], rows[:, :, cols]).then_inc(stored, 16)
            sp.wait_ge(stored, 64)

        @block.scalar
        def _(act):
            for i in range(KT):
                if i >= 2:
                    act.wait_ge(summed, i - 1)
                act.activation(sq[i % 2][:], k.lat[:, i, :], ACT.Square).then_inc(sq_made, 1)
            act.wait_ge(summed, KT)
            act.activation(rstd[:], k.psum[4][:], ACT.Ln, scale=1.0 / D_MODEL, bias=k.eps[:]).then_inc(std_made, 1)
            act.wait_ge(std_made, 1)
            act.activation(rstd[:], rstd[:], ACT.Exp, scale=-0.5).then_inc(rstd_made, 1)
            for i in range(KT):
                act.wait_ge(turned, i + 1)
                act.activation(rows[:, :, i * P:(i + 1) * P], k.psum[i % 2][:].rearrange("p (t c) -> p t c", c=P), ACT.Copy).then_inc(kept, 1)

        @block.tensor
        def _(pe):
            for i in range(KT):
                pe.wait_ge(sq_made, i + 1)
                pe.matmul(k.psum[4][:], k.ones[:], sq[i % 2][:], start=(i == 0), stop=(i == KT - 1)).then_inc(summed, 1)
            for i in range(KT):
                pe.wait_ge(f_made, i + 1)
                if i >= 2:
                    pe.wait_ge(kept, i - 1)
                for t in range(SEQ // P):
                    mm = pe.transpose(k.psum[i % 2][:, t * P:(t + 1) * P], k.lat[:, i, t * P:(t + 1) * P], k.ident[:])
                mm.then_inc(turned, 1)

        @block.vector
        def _(dve):
            dve.wait_ge(rstd_made, 1)
            for i in range(KT):
                dve.scalar_tensor_tensor(out=k.lat[:, i, :], in0=k.lat[:, i, :], scalar=gain[:, i:i + 1], in1=rstd[:],
                                         op0=ALU.mult, op1=ALU.mult).then_inc(f_made, 1)




STAGES = [modulation_and_norm1, projections, gate_rows, rglru, mlstm, ssd, deltanet,
          output_projection, feed_forward, final_norm]


def hybrid_block(nc, io, out):
    k = Kit(nc, io, out)
    constants_and_state(k)
    for stage in STAGES:
        stage(k)
        k.end_block()


_INS = ["x", "c", "ctx", "c_ctx", "ada_w", "ada_b", "norm1_g", "norm2_g", "w_in",
        "dn_conv_w", "dn_a_log", "dn_dt_bias", "dn_norm_g",
        "ssd_conv_w", "ssd_conv_b", "ssd_a_log", "ssd_dt_bias", "ssd_d", "ssd_norm_g",
        "lru_conv_w", "lru_conv_b", "lru_w_a", "lru_b_a", "lru_w_i", "lru_b_i", "lru_lambda",
        "ml_ig_b", "ml_fg_b", "ml_norm_g", "w_out", "ffn_w_up", "ffn_conv_w", "ffn_w_down",
        "final_norm_g"]


def kernel(**inputs):
    import concourse.bacc as _bacc
    from concourse.bass_utils import run_bass_kernel_spmd as _run

    nc = _bacc.Bacc("TRN2", target_bir_lowering=False, num_devices=1)
    arrays, io = {}, {}
    for name in _INS:
        a = np.ascontiguousarray(inputs[name])
        arrays[f"in_{name}"] = a
        io[name] = nc.dram_tensor(f"in_{name}", a.shape, mybir.dt.from_np(a.dtype), kind="ExternalInput").ap()
    out = nc.dram_tensor("out_dram", (1, SEQ, D_MODEL), F32, kind="ExternalOutput").ap()
    hybrid_block(nc, io, out)
    r = _run(nc, [arrays], core_ids=[0])
    return r.results[0]["out_dram"]
```

```python
import numpy as np

import concourse.bass as bass
from concourse import mybir

F32 = mybir.dt.float32
F32R = mybir.dt.float32r
ALU = mybir.AluOpType
ACT = mybir.ActivationFunctionType

P = 128
D_MODEL = 2048
SEQ = 512
CTX = 256
TOK = CTX + SEQ
GRID_W = 64
GRID_ROWS = SEQ // GRID_W
GROUP_W = D_MODEL // 4
D_FF = 5632
EPS = 1e-6
KT = D_MODEL // P
FT = D_FF // P
N_MOD = 6
SH1, SC1, G1, SH2, SC2, G2 = range(N_MOD)
CHUNKS = TOK // P
CTX_CHUNKS = CTX // P
NEG = -1e30

DN_HEADS, SSD_HEADS, SSD_P, ML_HEADS, ML_DK = 4, 8, 64, 4, 64
SHORT = 5
DN_A, DN_B = 2048, 2056
SSD_DT, ML_I, ML_F = 3600, 6176, 6184

REGIONS = [
    (0, 4, False, "conv"),
    (4, 8, True, "conv"),
    (12, 4, False, "silu"),
    (16, 4, True, "conv"),
    (20, 4, False, "silu"),
    (24, 2, True, "conv"),
    (26, 2, False, "conv"),
    (28, 4, True, "lru"),
    (32, 4, False, "gelu"),
    (36, 2, False, "copy"),
    (38, 6, True, "copy"),
    (44, 4, False, "sigmoid"),
]
T_Q, T_K, T_V, T_Z, T_SX, T_SZ, T_SB, T_SC = 0, 4, 8, 12, 16, 20, 24, 26
T_LX, T_LG, T_MQ, T_MK, T_MV, T_MO, TILES = 28, 32, 36, 38, 40, 44, 48
COLUMN_RUNS = [(0, 2, 0), (2, 14, 2 * P), (16, 12, 2064), (28, 6, 3616), (34, 14, 3616 + 6 * P)]

PAR = {}
_at = 0
for _name, _n in (("norm1", KT), ("norm2", KT), ("final", KT), ("dn_norm", 1), ("ssd_norm", 4),
                  ("ml_norm", 4), ("ssd_cb", 8), ("lru_cb", 4), ("lru_ba", 8), ("lru_bi", 8),
                  ("lru_lam", 8), ("ssd_d", 4)):
    PAR[_name] = _at
    _at += _n
N_VEC = _at
PAR["dn_cw"], PAR["ssd_cw"], PAR["lru_cw"] = N_VEC, N_VEC + 60, N_VEC + 100
N_CW = 120
PAR["ffn_cw"] = N_VEC + N_CW
PAR["ada_b"] = N_VEC + N_CW + 3 * FT
N_LATE = (N_MOD - G1) * KT
N_PAR = PAR["ada_b"] + N_LATE

R_DN, R_SSD, R_ML, GROWS = 0, 4, 12, 16

KB = 1024
AT_LOW = 8 * KB
AT_LAT = 72 * KB
AT_RING = 104 * KB
AT_HIGH = 152 * KB


def chunk_of(d, n):
    if d == 0:
        return n
    return CTX_CHUNKS - 1 - n if n < CTX_CHUNKS else CHUNKS - 1 - (n - CTX_CHUNKS)


class Kit:

    def __init__(self, nc, io, out):
        self.nc, self.io, self.out = nc, io, out
        self.base = (nc.sbuf_base + 63) // 64 * 64
        self.sems = {}
        self.psum = [nc.alloc_psum_tensor(f"bank{b}", [P, 512], F32) for b in range(8)]
        self.at = self.base
        self.n = 0

    def sem(self, name):
        if name not in self.sems:
            self.sems[name] = self.nc.alloc_semaphore(name)
        return self.sems[name]

    def lasting_sem(self, name):
        return self.nc.alloc_semaphore(name)

    def end_block(self):
        self.nc.clear_and_free_semaphores(list(self.sems.values()))
        self.nc.all_engine_barrier()
        self.sems = {}

    def go(self, offset):
        self.at = self.base + offset

    def sb(self, name, shape, dtype=F32):
        size = 4
        for s in shape[1:]:
            size *= s
        t = self.nc.alloc_sbuf_tensor_at(name, shape, dtype, offset=self.at)
        self.at += (size + 63) // 64 * 64
        return t

    def dram(self, name, shape):
        return self.nc.dram_tensor(name, shape, F32, kind="Internal").ap()




def constants_and_state(k):
    k.go(0)
    k.ident = k.sb("ident", [P, P])
    k.ones = k.sb("ones", [P, P])
    k.par = k.sb("par", [P, N_PAR])
    k.mod = k.sb("mod", [P, N_MOD * KT, 2])
    k.csil = k.sb("csil", [P, KT, 2])
    k.gain1 = k.sb("gain1", [P, 2, KT])
    k.gain2 = k.sb("gain2", [P, KT])
    k.eps = k.sb("eps", [P, 1])
    k.gpar = k.sb("gpar", [P, 8])
    assert k.at - k.base <= AT_LOW, k.at - k.base
    k.xT_dram = k.dram("xT_dram", [P, KT, SEQ])
    k.proj = k.dram("proj", [TILES, P, TOK])
    k.rows_dram = k.dram("rows_dram", [2, 64, TOK])
    k.last_mix_stored = k.lasting_sem("dn_mix_stored")
    k.mix = k.dram("mix", [KT, P, SEQ])


GP_ALOG, GP_BIAS, GP_IGB, GP_SIGN, GP_COEF, GP_ML = range(6)


def modulation_and_norm1(k):
    nc, io = k.nc, k.io
    k.go(AT_LOW)
    adaw = [k.sb(f"adaw{s}", [P, KT, 512]) for s in range(2)]
    sheet = k.sb("sheet", [P, 5, P])
    dval = k.sb("dval", [1, SSD_HEADS])
    dwide = k.sb("dwide", [1, SSD_HEADS * SSD_P])
    cvec = k.sb("cvec", [P, 2, KT])
    modrow = [k.sb(f"modrow{s}", [2, 512]) for s in range(2)]
    biasrow = [k.sb(f"biasrow{s}", [2, 512]) for s in range(2)]
    assert k.at - k.base <= AT_RING
    k.go(AT_LOW)
    k.hh = k.sb("hh", [P, KT, TOK], F32R)
    k.hl = k.sb("hl", [P, KT, TOK], F32R)
    assert k.at - k.base <= AT_RING
    k.go(AT_RING)
    xT = k.sb("xT", [P, KT, TOK])
    k.go(AT_HIGH)
    xin = k.sb("xin", [P, TOK // P, D_MODEL])
    sq = [k.sb(f"sq{s}", [P, TOK]) for s in range(2)]
    k.go(AT_HIGH)
    norm = k.sb("norm", [P, 2, TOK])
    rstd = k.sb("rstd1", [P, TOK])

    x_loaded = [k.sem(f"x_loaded{q}") for q in range(4)]
    const_ready, zero_ready = k.sem("const_ready"), k.sem("zero_ready")
    d_loaded, d_ready = k.sem("d_loaded"), k.sem("d_ready")
    par_loaded, c_loaded, c_ready = k.sem("par_loaded"), k.sem("c_loaded"), k.sem("c_ready")
    gp_loaded = k.sem("gp_loaded")
    xt_done, xt_kept, sq_done, ss_done = (k.sem(n) for n in ("xt_done", "xt_kept", "sq_done", "ss_done"))
    ada_loaded = [k.sem(f"ada_loaded{s}") for s in range(2)]
    ada_done, row_kept, turn_done, mod_kept = (k.sem(n) for n in ("ada_done", "row_kept", "turn_done", "mod_kept"))
    par_done, par_kept = k.sem("par_done"), k.sem("par_kept")
    std_ready, rstd_ready, gain_ready = k.sem("std_ready"), k.sem("rstd_ready"), k.sem("gain_ready")
    n_scaled, n_mod, hi_done, lo_done = (k.sem(n) for n in ("n_scaled", "n_mod", "h_hi_done", "h_lo_done"))
    xt_stored = k.sem("xt_stored")
    g_ready = k.sem("g_ready")
    lat, ctx = slice(CTX, TOK), slice(0, CTX)
    NADA = G1 * D_MODEL // 512

    x2 = io["x"].rearrange("b (t p) d -> p (b t) d", p=P)
    c2 = io["ctx"].rearrange("b (t p) d -> p (b t) d", p=P)
    adaw_d = io["ada_w"].rearrange("l (p k) n -> p (l k) n", p=P)
    adab_d = io["ada_b"]

    def rows(name, per):
        return io[name].rearrange(per, p=P)

    vec_rows = [("norm1", rows("norm1_g", "l (j p) -> (l j) p")), ("norm2", rows("norm2_g", "l (j p) -> (l j) p")),
                ("final", rows("final_norm_g", "(j p) -> j p")), ("dn_norm", io["dn_norm_g"]),
                ("ssd_norm", rows("ssd_norm_g", "l (j p) -> (l j) p")), ("ml_norm", rows("ml_norm_g", "l (j p) -> (l j) p")),
                ("ssd_cb", rows("ssd_conv_b", "l (j p) -> (l j) p")), ("lru_cb", rows("lru_conv_b", "l (j p) -> (l j) p")),
                ("lru_ba", rows("lru_b_a", "l d (j p) -> (l d j) p")), ("lru_bi", rows("lru_b_i", "l d (j p) -> (l d j) p")),
                ("lru_lam", rows("lru_lambda", "l d (j p) -> (l d j) p"))]

    with nc.Block() as block:
        @block.sync
        def _(sp):
            for q in range(4):
                chans = slice(q * 512, (q + 1) * 512)
                sp.dma_start(xin[:, 0:CTX // P, chans], c2[:, :, chans]).then_inc(x_loaded[q], 16)
                sp.dma_start(xin[:, CTX // P:, chans], x2[:, :, chans]).then_inc(x_loaded[q], 16)
            for t in range(NADA):
                s = t % 2
                if t == 2:
                    sp.wait_ge(xt_kept, 2 * KT)
                    sp.dma_start(k.xT_dram, xT[:, :, CTX:]).then_inc(xt_stored, 16)
                if t >= 2:
                    sp.wait_ge(ada_done, t - 1)
                    sp.wait_ge(row_kept, t - 1)
                sp.dma_start(adaw[s][:], adaw_d[:, :, t * 512:(t + 1) * 512]).then_inc(ada_loaded[s], 16)
                sp.dma_start(biasrow[s][:], adab_d[:, t * 512:(t + 1) * 512].to_broadcast([2, 512])).then_inc(ada_loaded[s], 16)

        @block.gpsimd
        def _(pool):
            pool.memset(k.ident[:], 0.0).then_inc(zero_ready, 1)
            pool.memset(k.ones[:], 1.0).then_inc(const_ready, 1)
            pool.memset(k.eps[:], EPS).then_inc(const_ready, 1)
            pool.memset(sheet[:], 0.0).then_inc(zero_ready, 1)
            pool.memset(k.gpar[:], 0.0).then_inc(zero_ready, 1)
            pool.wait_ge(zero_ready, 1)
            pool.affine_select(out=k.ident[:], in_=k.ident[:], compare_op=ALU.not_equal, fill=1.0, base=0,
                               pattern=[[-1, P]], channel_multiplier=1).then_inc(const_ready, 1)

        @block.scalar
        def _(act):
            act.wait_ge(zero_ready, 3)
            act.dma_start(dval[:], io["ssd_d"]).then_inc(d_loaded, 16)
            act.dma_start(cvec[:, 0, :], io["c"].rearrange("b (p k) -> p (b k)", p=P)).then_inc(c_loaded, 16)
            act.dma_start(cvec[:, 1, :], io["c_ctx"].rearrange("(p k) -> p k", p=P)).then_inc(c_loaded, 16)
            act.wait_ge(c_loaded, 32)
            act.activation(k.csil[:].rearrange("p k b -> p b k"), cvec[:], ACT.Silu).then_inc(c_ready, 1)
            for name, src in vec_rows:
                at = PAR[name]
                act.dma_start(sheet[at:at + src.shape[0], 0, :], src).then_inc(par_loaded, 16)
            act.dma_start(sheet[0:60, 1, :], rows("dn_conv_w", "l t (j p) -> (l t j) p")).then_inc(par_loaded, 16)
            act.dma_start(sheet[60:100, 1, :], rows("ssd_conv_w", "l t (j p) -> (l t j) p")).then_inc(par_loaded, 16)
            act.dma_start(sheet[100:120, 1, :], rows("lru_conv_w", "l t (j p) -> (l t j) p")).then_inc(par_loaded, 16)
            ffn_rows = rows("ffn_conv_w", "l t (j p) -> (l t j) p")
            act.dma_start(sheet[0:88, 2, :], ffn_rows[0:88]).then_inc(par_loaded, 16)
            act.dma_start(sheet[0:44, 3, :], ffn_rows[88:132]).then_inc(par_loaded, 16)
            act.dma_start(sheet[0:N_LATE, 4, :], rows("ada_b", "l (j p) -> (l j) p")[G1 * KT:]).then_inc(par_loaded, 16)
            for d in range(2):
                for at, n, col, name in ((R_DN, 4, GP_ALOG, "dn_a_log"), (R_DN, 4, GP_BIAS, "dn_dt_bias"),
                                         (R_SSD, 8, GP_ALOG, "ssd_a_log"), (R_SSD, 8, GP_BIAS, "ssd_dt_bias"),
                                         (R_ML, 4, GP_BIAS, "ml_fg_b"), (R_ML, 4, GP_IGB, "ml_ig_b")):
                    act.dma_start(k.gpar[32 * d + at:32 * d + at + n, col:col + 1],
                                  io[name][0:1, d, :].rearrange("l h -> h l")).then_inc(gp_loaded, 16)
            act.wait_ge(d_loaded, 16)
            act.activation(dwide[:].rearrange("a (h p) -> a h p", p=SSD_P),
                           dval[:].unsqueeze(2).to_broadcast([1, SSD_HEADS, SSD_P]), ACT.Copy).then_inc(d_ready, 1)
            act.wait_ge(d_ready, 1)
            act.dma_start(sheet[PAR["ssd_d"]:PAR["ssd_d"] + 4, 0, :],
                          dwide[:].rearrange("a (j p) -> a j p", p=P)).then_inc(par_loaded, 16)
            for i in range(KT):
                act.wait_ge(xt_kept, 2 * (i + 1))
                if i >= 2:
                    act.wait_ge(ss_done, i - 1)
                act.activation(sq[i % 2][:], xT[:, i, :], ACT.Square).then_inc(sq_done, 1)
            act.wait_ge(ss_done, KT)
            act.wait_ge(const_ready, 3)
            act.activation(rstd[:, CTX:], k.psum[4][:], ACT.Ln, scale=1.0 / D_MODEL, bias=k.eps[:]).then_inc(std_ready, 1)
            act.activation(rstd[:, 0:CTX], k.psum[5][:, 0:CTX], ACT.Ln, scale=1.0 / D_MODEL, bias=k.eps[:]).then_inc(std_ready, 1)
            act.wait_ge(std_ready, 2)
            act.activation(rstd[:], rstd[:], ACT.Exp, scale=-0.5).then_inc(rstd_ready, 1)
            act.wait_ge(gp_loaded, 16 * 12)
            act.activation(k.gpar[0:64, GP_COEF:GP_COEF + 1], k.gpar[0:64, GP_ALOG:GP_ALOG + 1], ACT.Exp).then_inc(g_ready, 1)
            for i in range(KT):
                if i >= 2:
                    act.wait_ge(lo_done, i - 1)
                act.wait_ge(n_scaled, i + 1)
                if i == 0:
                    act.wait_ge(gain_ready, 2)
                for part, cols, to in ((0, lat, k.hh[:, i, lat]), (1, ctx, k.hh[:, i, ctx]), (1, ctx, norm[:, i % 2, ctx])):
                    ins = act.activation(to, xT[:, i, cols], ACT.Identity, bias=k.mod[:, SH1 * KT + i, part:part + 1],
                                         scale=k.gain1[:, part, i:i + 1])
                ins.then_inc(hi_done, 1)

        @block.tensor
        def _(pe):
            pe.wait_ge(const_ready, 3)
            for i in range(KT):
                pe.wait_ge(x_loaded[i // 4], 32)
                if i >= 2:
                    pe.wait_ge(xt_kept, 2 * (i - 1))
                for t in range(CTX // P):
                    pe.transpose(k.psum[2 + i % 2][:, t * P:(t + 1) * P], xin[:, t, i * P:(i + 1) * P], k.ident[:])
                for t in range(SEQ // P):
                    mm = pe.transpose(k.psum[i % 2][:, t * P:(t + 1) * P], xin[:, CTX // P + t, i * P:(i + 1) * P], k.ident[:])
                mm.then_inc(xt_done, 1)

            def ada(t):
                s = t % 2
                pe.wait_ge(ada_loaded[s], 32 * (t // 2 + 1))
                if t >= 2:
                    pe.wait_ge(row_kept, t - 1)
                for i in range(KT):
                    mm = pe.matmul(k.psum[6 + s][0:2, :], k.csil[:, i, :], adaw[s][:, i, :], start=(i == 0), stop=(i == KT - 1))
                mm.then_inc(ada_done, 1)

            def turn(t):
                pe.wait_ge(row_kept, t + 1)
                for q in range(4):
                    j = 4 * t + q
                    mm = pe.transpose(k.psum[0][:, 2 * j:2 * j + 2], modrow[t % 2][:, q * P:(q + 1) * P], k.ident[0:2, 0:2])
                mm.then_inc(turn_done, 1)

            pe.wait_ge(c_ready, 1)
            ada(0)
            ada(1)
            pe.wait_ge(par_loaded, 16 * (len(vec_rows) + 7))
            pe.wait_ge(xt_kept, 2 * KT)
            for n, (r, at) in enumerate(((N_VEC, 0), (N_CW, N_VEC), (88, N_VEC + N_CW), (44, N_VEC + N_CW + 88), (N_LATE, PAR["ada_b"]))):
                mm = pe.transpose(k.psum[1][:, at:at + r], sheet[0:r, n, :], k.ident[0:r, 0:r])
            mm.then_inc(par_done, 1)
            for i in range(KT):
                pe.wait_ge(sq_done, i + 1)
                pe.matmul(k.psum[4][:], k.ones[:], sq[i % 2][:, CTX:], start=(i == 0), stop=(i == KT - 1))
                pe.matmul(k.psum[5][:, 0:CTX], k.ones[:], sq[i % 2][:, 0:CTX], start=(i == 0), stop=(i == KT - 1)).then_inc(ss_done, 1)
            for t in range(NADA):
                if t >= 2:
                    ada(t)
                if t >= 1:
                    turn(t - 1)
            turn(NADA - 1)

        @block.vector
        def _(dve):
            for i in range(KT):
                dve.wait_ge(xt_done, i + 1)
                dve.tensor_copy(xT[:, i, CTX:], k.psum[i % 2][:]).then_inc(xt_kept, 1)
                dve.tensor_copy(xT[:, i, 0:CTX], k.psum[2 + i % 2][:, 0:CTX]).then_inc(xt_kept, 1)

            def row(t):
                dve.wait_ge(ada_done, t + 1)
                dve.wait_ge(ada_loaded[t % 2], 32 * (t // 2 + 1))
                if t >= 2:
                    dve.wait_ge(turn_done, t - 1)
                dve.tensor_tensor(modrow[t % 2][:], k.psum[6 + t % 2][0:2, :], biasrow[t % 2][:], ALU.add).then_inc(row_kept, 1)

            row(0)
            row(1)
            dve.wait_ge(par_done, 1)
            dve.tensor_copy(k.par[:], k.psum[1][:, 0:N_PAR]).then_inc(par_kept, 1)
            dve.wait_ge(rstd_ready, 1)
            dve.wait_ge(xt_stored, 16)
            for i in range(KT):
                dve.tensor_tensor(xT[:, i, :], xT[:, i, :], rstd[:], ALU.mult).then_inc(n_scaled, 1)
            for t in range(2, NADA):
                row(t)
            dve.wait_ge(turn_done, NADA)
            dve.tensor_copy(k.mod[:, 0:G1 * KT, :], k.psum[0][:, 0:2 * G1 * KT].rearrange("p (j b) -> p j b", b=2)).then_inc(mod_kept, 1)
            dve.wait_ge(mod_kept, 1)
            dve.wait_ge(par_kept, 1)
            for part in range(2):
                dve.scalar_tensor_tensor(out=k.gain1[:, part, :], in0=k.mod[:, SC1 * KT:(SC1 + 1) * KT, part], scalar=1.0,
                                         in1=k.par[:, PAR["norm1"]:PAR["norm1"] + KT], op0=ALU.add, op1=ALU.mult).then_inc(gain_ready, 1)
            dve.wait_ge(const_ready, 3)
            dve.wait_ge(gp_loaded, 16 * 12)
            dve.reduce_sum(k.gpar[0:64, GP_ML:GP_ML + 1], k.ident[0:64, R_ML:R_ML + 4], axis=mybir.AxisListType.X).then_inc(g_ready, 1)
            dve.reduce_sum(k.gpar[0:64, GP_SIGN:GP_SIGN + 1], k.ident[0:64, 32 + R_ML:32 + R_ML + 4], axis=mybir.AxisListType.X).then_inc(g_ready, 1)
            dve.wait_ge(g_ready, 3)
            dve.tensor_tensor(k.gpar[0:64, GP_ML:GP_ML + 1], k.gpar[0:64, GP_ML:GP_ML + 1], k.gpar[0:64, GP_SIGN:GP_SIGN + 1], ALU.add).then_inc(g_ready, 1)
            dve.wait_ge(g_ready, 4)
            dve.tensor_scalar(k.gpar[0:64, GP_SIGN:GP_SIGN + 1], k.gpar[0:64, GP_ML:GP_ML + 1], -2.0, 1.0, ALU.mult, ALU.add).then_inc(g_ready, 1)
            dve.tensor_scalar(k.gpar[0:64, GP_COEF:GP_COEF + 1], k.gpar[0:64, GP_COEF:GP_COEF + 1], -1.0, None, ALU.mult).then_inc(g_ready, 1)
            dve.wait_ge(gain_ready, 2)
            for i in range(KT):
                dve.tensor_scalar(norm[:, i % 2, lat], xT[:, i, lat], k.gain1[:, 0, i:i + 1], k.mod[:, SH1 * KT + i, 0:1],
                                  ALU.mult, ALU.add).then_inc(n_mod, 1)
                dve.wait_ge(n_mod, i + 1)
                dve.wait_ge(hi_done, i + 1)
                dve.tensor_tensor(k.hl[:, i, :], norm[:, i % 2, :], k.hh[:, i, :].bitcast(F32), ALU.subtract).then_inc(lo_done, 1)




def open_ring(k):
    k.go(AT_RING)
    k.raw = k.sb("raw", [P, 2, KT, P])
    k.hi = k.sb("w_hi", [P, 2, KT, P], F32R)
    k.lo = k.sb("w_lo", [P, 2, KT, P], F32R)
    assert k.at - k.base <= AT_HIGH


class Ring:

    def __init__(self, k, name):
        self.k = k
        self.loaded = [k.sem(f"{name}_raw_loaded{s}") for s in range(2)]
        self.split = k.sem(f"{name}_weights_split")
        self.rounded = k.sem(f"{name}_weights_rounded")
        self.used = k.sem(f"{name}_weights_used")
        self.kept = k.sem(f"{name}_product_kept")

    def load(self, sp, t, s, source, rows=KT):
        sp.wait_ge(self.split, t + 1)
        sp.dma_start(self.k.raw[:, s, 0:rows, :], source).then_inc(self.loaded[s], 16)

    def round(self, act, t, half, s):
        act.wait_ge(self.loaded[s], half * 16 + 16)
        act.wait_ge(self.used, t + 1)
        act.activation(self.k.hi[:, s], self.k.raw[:, s], ACT.Copy).then_inc(self.rounded, 1)

    def subtract(self, pool, t, s):
        pool.wait_ge(self.rounded, t + 1)
        pool.tensor_tensor(self.k.lo[:, s], self.k.raw[:, s], self.k.hi[:, s].bitcast(F32), ALU.subtract).then_inc(self.split, 1)

    def multiply(self, pe, t, s, outs, kt=KT, kept=None, parts=None, order=None):
        k = self.k
        pe.wait_ge(self.split, t + 3)
        pe.wait_ge(*(kept or (self.kept, t + 1)))
        for n, i in enumerate(order or range(kt)):
            if parts:
                pe.wait_ge(parts[0], parts[1] + (n + 1))
            for bank, hi, lo in outs:
                pe.matmul(bank, k.hi[:, s, i, :], hi[:, i, :], start=(n == 0), stop=False)
                pe.matmul(bank, k.hi[:, s, i, :], lo[:, i, :], start=False, stop=False)
            for bank, hi, lo in outs:
                mm = pe.matmul(bank, k.lo[:, s, i, :], hi[:, i, :], start=False, stop=(n == kt - 1))
        mm.then_inc(self.used, 1)


ADA_STEPS = N_LATE // 2


def projections(k):
    nc, io = k.nc, k.io
    open_ring(k)
    k.go(AT_HIGH)
    pad = [k.sb(f"pad{s}", [P, TOK + 8]) for s in range(2)]
    acc = [k.sb(f"acc{s}", [P, TOK + 4]) for s in range(2)]
    done = [k.sb(f"done{s}", [P, TOK]) for s in range(2)]
    cw = [k.sb(f"cw{s}", [P, SHORT]) for s in range(2)]
    cb = [k.sb(f"cb{s}", [P, 1]) for s in range(2)]
    wgin = k.sb("wgin", [P, KT, 48])
    gates = [k.sb(f"gate_rows{s}", [64, TOK]) for s in range(2)]
    part_sum = [[k.sb(f"ada_sum{s}{e}", [P, 2 * P]) for e in range(2)] for s in range(2)]
    gates_at = k.at - k.base
    wg = k.sb("wg", [P, KT, P])
    wgh = k.sb("wgh", [P, KT, P], F32R)
    wgl = k.sb("wgl", [P, KT, P], F32R)
    top = k.at
    k.go(gates_at)
    adaw = [k.sb(f"late_adaw{q}", [P, KT // 2, 2 * P]) for q in range(2)]
    assert k.at <= top
    k.at = top
    assert k.at <= nc.sbuf_usable_end, k.at
    CX, LT, LATENT = 2, CTX + 6, CTX + 4

    ring = Ring(k, "in")
    gate_loaded, gate_zero, gate_set = k.sem("gate_loaded"), k.sem("gate_zero"), k.sem("gate_set")
    gate_hi, gate_lo, gate_done, gate_kept = (k.sem(n) for n in ("gate_hi", "gate_lo", "gate_done", "gate_kept"))
    gate_stored = k.sem("gate_stored")
    pad_zero, filled, convolved = k.sem("pad_zero"), k.sem("pad_filled"), k.sem("convolved")
    cw_set, tapped, finished = k.sem("cw_set"), k.sem("tapped"), k.sem("tile_finished")
    stored = [k.sem(f"tile_stored{s}") for s in range(2)]
    ada_in = [k.sem(f"late_ada_in{q}") for q in range(2)]
    ada_steps, ada_half, ada_summed, ada_turned, mod_made = (k.sem(n) for n in ("ada_steps", "ada_half_read", "ada_summed", "ada_turned", "late_mod_made"))
    ada_d = io["ada_w"].rearrange("l (p k) n -> p (l k) n", p=P)
    w = io["w_in"].rearrange("l (k p) n -> p (l k) n", p=P)
    lat, ctx = slice(CTX, TOK), slice(0, CTX)

    def conv_before(t0):
        return sum(n for a, n, _, what in REGIONS if a < t0 and what in ("conv", "lru"))

    with nc.Block() as block:
        @block.sync
        def _(sp):
            for n, (col, width) in enumerate(((DN_A, 16), (SSD_DT, 16), (ML_I, 16))):
                sp.dma_start(wgin[:, :, 16 * n:16 * n + 16], w[:, :, col:col + width]).then_inc(gate_loaded, 16)
            for t0, n, col in COLUMN_RUNS:
                with sp.Fori(0, n // 2) as j:
                    for s in range(2):
                        ring.load(sp, j * 2 + (t0 + s), s, w[:, :, bass.ds(j * (2 * P) + (col + s * P), P)])
                        if not 2 <= t0 < ADA_STEPS + 2:
                            continue
                        step = t0 + s - 2
                        sp.wait_ge(gate_done, 1)
                        for q in range(2):
                            if q == 0:
                                sp.wait_ge(ada_half, j * 2 + (step + 1))
                            else:
                                sp.wait_ge(ada_summed, j * 4 + (step * 2 + 2))
                            sp.dma_start(adaw[q][:], ada_d[:, q * (KT // 2):(q + 1) * (KT // 2),
                                                           bass.ds(j * (4 * P) + (G1 * D_MODEL + 2 * step * P), 2 * P)]
                                         ).then_inc(ada_in[q], 16)
            sp.wait_ge(gate_kept, 2)
            for s in range(2):
                sp.dma_start(k.rows_dram[s], gates[s][:]).then_inc(gate_stored, 16)
            sp.wait_ge(gate_stored, 32)

        @block.gpsimd
        def _(pool):
            pool.sem_inc(ring.split, 2)
            pool.memset(wg[:], 0.0).then_inc(gate_zero, 1)
            for s in range(2):
                pool.memset(pad[s][:], 0.0).then_inc(pad_zero, 1)
            pool.wait_ge(gate_loaded, 48)
            pool.wait_ge(gate_zero, 1)
            for d in range(2):
                for dst, src, n in ((32 * d + R_DN, 4 * d, 4), (32 * d + R_SSD, 16 + 8 * d, 8), (32 * d + R_ML, 40 + 4 * d, 4),
                                    (64 + 32 * d + R_DN, 8 + 4 * d, 4), (64 + 32 * d + R_ML, 32 + 4 * d, 4)):
                    pool.tensor_copy(wg[:, :, dst:dst + n], wgin[:, :, src:src + n]).then_inc(gate_set, 1)
            pool.wait_ge(gate_hi, 1)
            pool.tensor_tensor(wgl[:], wg[:], wgh[:].bitcast(F32), ALU.subtract).then_inc(gate_lo, 1)
            with pool.Fori(0, TILES // 2) as j:
                for s in range(2):
                    ring.subtract(pool, j * 2 + s, s)

        @block.scalar
        def _(act):
            act.wait_ge(gate_set, 10)
            act.activation(wgh[:], wg[:], ACT.Copy).then_inc(gate_hi, 1)
            for s in range(2):
                ring.round(act, s, 0, s)
            act.wait_ge(gate_done, 1)
            act.activation(gates[0][:, lat], k.psum[4][0:64, :], ACT.Copy)
            act.activation(gates[0][:, ctx], k.psum[5][0:64, ctx], ACT.Copy).then_inc(gate_kept, 1)
            act.activation(gates[1][:, lat], k.psum[4][64:128, :], ACT.Copy)
            act.activation(gates[1][:, ctx], k.psum[5][64:128, ctx], ACT.Copy).then_inc(gate_kept, 1)

            def tile(t, half, s, has_ctx, what, nconv, more):
                act.wait_ge(ring.used, t + 3)
                if what in ("conv", "lru"):
                    place, bank = pad[s][:, LT:LT + SEQ], k.psum[s][:]
                    if what == "lru":
                        place = place.rearrange("p (w r) -> p r w", r=GRID_ROWS)
                        bank = bank.rearrange("p (r w) -> p r w", r=GRID_ROWS)
                    if has_ctx:
                        act.activation(pad[s][:, CX:CX + CTX], k.psum[2 + s][:, ctx], ACT.Copy).then_inc(filled, 1)
                    else:
                        act.sem_inc(filled, 1)
                    act.activation(place, bank, ACT.Copy).then_inc(filled, 1)
                    act.wait_ge(filled, (nconv + 1) * 2)
                    act.sem_inc(ring.kept, 1)
                if more:
                    ring.round(act, t + 2, half + 1, s)
                act.wait_ge(stored[s], half * 16 + 16)
                if what in ("conv", "lru"):
                    act.wait_ge(convolved, nconv + 1)
                    func = ACT.Silu if what == "conv" else ACT.Identity
                    if has_ctx:
                        act.activation(done[s][:, ctx], acc[s][:, ctx], func, bias=cb[s][:])
                    act.activation(done[s][:, lat], acc[s][:, LATENT:LATENT + SEQ], func, bias=cb[s][:]).then_inc(finished, 1)
                    act.wait_ge(finished, t + 3)
                else:
                    func = {"silu": ACT.Silu, "gelu": ACT.Gelu_apprx_tanh, "sigmoid": ACT.Sigmoid, "copy": ACT.Copy}[what]
                    if has_ctx:
                        act.activation(done[s][:, ctx], k.psum[2 + s][:, ctx], func)
                    act.activation(done[s][:, lat], k.psum[s][:], func).then_inc(finished, 1)
                    act.wait_ge(finished, t + 3)
                    act.sem_inc(ring.kept, 1)
                cols = slice(0 if has_ctx else CTX, TOK)
                act.dma_start(k.proj[bass.ds(t, 1), :, cols].rearrange("t p n -> (t p) n"), done[s][:, cols]).then_inc(stored[s], 16)

            for s in range(2):
                act.sem_inc(stored[s], 16)
            act.sem_inc(ring.kept, 2)
            act.sem_inc(finished, 2)
            act.wait_ge(pad_zero, 2)
            for t0, n, has_ctx, what in REGIONS:
                before = conv_before(t0)
                last = t0 + n == TILES
                with act.Fori(0, n // 2 - last) as j:
                    for s in range(2):
                        tile(j * 2 + (t0 + s), j + t0 // 2, s, has_ctx, what, j * 2 + (before + s), True)
            for s in range(2):
                tile(TILES - 2 + s, TILES // 2 - 1, s, REGIONS[-1][2], REGIONS[-1][3], 0, False)
            for s in range(2):
                act.wait_ge(stored[s], 16 * (TILES // 2 + 1))

        @block.tensor
        def _(pe):
            pe.sem_inc(ring.used, 2)
            pe.wait_ge(gate_lo, 1)
            for i in range(KT):
                for bank, cols in ((k.psum[4][:], lat), (k.psum[5][:, ctx], ctx)):
                    pe.matmul(bank, wgh[:, i, :], k.hh[:, i, cols], start=(i == 0), stop=False)
                    pe.matmul(bank, wgh[:, i, :], k.hl[:, i, cols], start=False, stop=False)
                    mm = pe.matmul(bank, wgl[:, i, :], k.hh[:, i, cols], start=False, stop=(i == KT - 1))
            mm.then_inc(gate_done, 1)
            pe.sem_inc(ada_turned, 1)

            def turn(t, bank, s):
                pe.wait_ge(ada_summed, t * 2 + 2)
                for q in range(2):
                    for e in range(2):
                        mm = pe.matmul(bank(q), part_sum[s][e][:, q * P:(q + 1) * P], k.ones[:, 0:1], start=(e == 0), stop=(e == 1))
                mm.then_inc(ada_turned, 1)

            for t0, n, has_ctx, what in REGIONS:
                with pe.Fori(0, n // 2) as j:
                    for s in range(2):
                        outs = [(k.psum[s][:], k.hh[:, :, lat], k.hl[:, :, lat])]
                        if has_ctx:
                            outs.append((k.psum[2 + s][:, ctx], k.hh[:, :, ctx], k.hl[:, :, ctx]))
                        ring.multiply(pe, j * 2 + (t0 + s), s, outs)
                        if t0 < ADA_STEPS:
                            turn(j * 2 + (t0 + s), lambda q: k.psum[6][:, bass.ds(j * 4 + (2 * (t0 + s) + q), 1)], 1 - s)
                if t0 + n == ADA_STEPS:
                    turn(ADA_STEPS, lambda q: k.psum[6][:, 2 * ADA_STEPS + q:2 * ADA_STEPS + q + 1], 1)

        @block.vector
        def _(dve):
            def conv(t, s, table, first, taps_apart, bias, nconv, has_ctx):
                dve.wait_ge(finished, t + 1)
                dve.tensor_copy(cw[s][:], table(first, taps_apart)).then_inc(cw_set, 1)
                if bias is None:
                    dve.memset(cb[s][:], 0.0).then_inc(cw_set, 1)
                else:
                    dve.tensor_copy(cb[s][:], k.par[:, bass.ds(bias, 1)]).then_inc(cw_set, 1)
                dve.wait_ge(cw_set, (nconv + 1) * 2)
                dve.wait_ge(filled, (nconv + 1) * 2)
                lo = 0 if has_ctx else LATENT
                view = acc[s][:, lo:]
                dve.tensor_scalar(view, pad[s][:, lo:TOK + 4], cw[s][:, 0:1], None, ALU.mult).then_inc(tapped, 1)
                for tap in range(1, SHORT):
                    dve.wait_ge(tapped, nconv * (SHORT - 1) + tap)
                    ins = dve.scalar_tensor_tensor(out=view, in0=pad[s][:, lo + tap:TOK + 4 + tap], scalar=cw[s][:, tap:tap + 1],
                                                   in1=view, op0=ALU.mult, op1=ALU.add)
                    ins.then_inc(tapped if tap < SHORT - 1 else convolved, 1)

            def table(first, apart):
                return k.par[:, bass.ds(first, SHORT, step=apart)]

            def macs(t, i):
                if i == KT // 2 - 1:
                    return ada_half, t + 2
                return ada_steps, t * (KT - 3) + (i + 1 if i < KT // 2 - 1 else i)

            def ada(t, s):
                dve.wait_ge(ada_turned, t + 1)
                for i in range(KT):
                    q, row = i // (KT // 2), i % (KT // 2)
                    if row == 0:
                        dve.wait_ge(ada_in[q], t * 16 + 16)
                    to, c = part_sum[s][i % 2][:], k.csil[:, i, 0:1]
                    if i < 2:
                        ins = dve.tensor_scalar(to, adaw[q][:, row, :], c, None, ALU.mult)
                    else:
                        dve.wait_ge(*macs(t, i - 2))
                        ins = dve.scalar_tensor_tensor(out=to, in0=adaw[q][:, row, :], scalar=c, in1=to, op0=ALU.mult, op1=ALU.add)
                    if i == KT // 2 - 1:
                        ins.then_inc(ada_half, 1)
                    elif i >= KT - 2:
                        ins.then_inc(ada_summed, 1)
                    else:
                        ins.then_inc(ada_steps, 1)

            dve.sem_inc(ada_half, 1)
            for e in range(2):
                dve.memset(part_sum[1][e][:], 0.0).then_inc(ada_summed, 1)
            for t0, n, has_ctx, what in REGIONS:
                if what not in ("conv", "lru"):
                    if t0 < ADA_STEPS:
                        with dve.Fori(0, n // 2) as j:
                            for s in range(2):
                                ada(j * 2 + (t0 + s), s)
                    continue
                before = conv_before(t0)
                if t0 < T_Z:
                    first, apart, bias = PAR["dn_cw"] + t0, 12, None
                elif what == "lru":
                    first, apart, bias = PAR["lru_cw"], 4, PAR["lru_cb"]
                else:
                    c = {T_SX: 0, T_SB: 4, T_SC: 6}[t0]
                    first, apart, bias = PAR["ssd_cw"] + c, 8, PAR["ssd_cb"] + c
                with dve.Fori(0, n // 2) as j:
                    for s in range(2):
                        if t0 < ADA_STEPS:
                            ada(j * 2 + (t0 + s), s)
                        conv(j * 2 + (t0 + s), s, table, j * 2 + (first + s), apart,
                             None if bias is None else j * 2 + (bias + s), j * 2 + (before + s), has_ctx)
            dve.wait_ge(ada_turned, ADA_STEPS + 2)
            dve.tensor_tensor(k.mod[:, G1 * KT:, 0], k.psum[6][:, 2:2 * ADA_STEPS + 2], k.par[:, PAR["ada_b"]:PAR["ada_b"] + N_LATE],
                              ALU.add).then_inc(mod_made, 1)
            dve.wait_ge(mod_made, 1)
            dve.scalar_tensor_tensor(out=k.gain2[:], in0=k.mod[:, SC2 * KT:(SC2 + 1) * KT, 0], scalar=1.0,
                                     in1=k.par[:, PAR["norm2"]:PAR["norm2"] + KT], op0=ALU.add, op1=ALU.mult)




class Steps:

    def __init__(self, engine, sem):
        self.engine, self.sem, self.count = engine, sem, 0

    def __call__(self, ins):
        self.count += 1
        ins.then_inc(self.sem, 1)
        self.engine.wait_ge(self.sem, self.count)


LOG1P_TERMS = 7


def softplus_exp(steps, act, z, e):
    steps(act.activation(e, z, ACT.Abs))
    steps(act.activation(e, e, ACT.Exp, scale=-1.0))


def softplus_sum(steps, dve, z, e, s, u):
    steps(dve.tensor_scalar(s, e, 2.0, None, ALU.add))
    steps(dve.reciprocal(s, s))
    steps(dve.tensor_tensor(s, s, e, ALU.mult))
    steps(dve.tensor_tensor(e, s, s, ALU.mult))
    steps(dve.tensor_scalar(u, e, 1.0 / (2 * LOG1P_TERMS + 1), None, ALU.mult))
    for n in range(LOG1P_TERMS - 1, 0, -1):
        steps(dve.scalar_tensor_tensor(out=u, in0=u, scalar=1.0 / (2 * n + 1), in1=e, op0=ALU.add, op1=ALU.mult))
    steps(dve.scalar_tensor_tensor(out=u, in0=u, scalar=1.0, in1=s, op0=ALU.add, op1=ALU.mult))
    steps(dve.tensor_scalar(u, u, 2.0, None, ALU.mult))
    steps(dve.scalar_tensor_tensor(out=z, in0=z, scalar=0.0, in1=u, op0=ALU.max, op1=ALU.add))


LEVELS = 7
COL_C, COL_W, COL_BETA, COL_DT, COL_NBE, COL_XM = range(6)


class Inputs:

    def __init__(self, k, at, tiles):
        k.go(at)
        self.k, self.tiles = k, tiles
        self.t = {name: k.sb(name, [P, n, TOK if has_ctx else SEQ]) for name, _, n, has_ctx in tiles}
        self.loaded = {name: k.lasting_sem(f"{name}_loaded") for name, _, _, _ in tiles}
        self.end = k.at - k.base

    def load(self, sp):
        for name, first, n, has_ctx in self.tiles:
            source = self.k.proj[first:first + n, :, 0 if has_ctx else CTX:].rearrange("t p n -> p t n")
            sp.dma_start(self.t[name][:], source).then_inc(self.loaded[name], 16)


def mixer_inputs(k):
    end = (k.nc.sbuf_usable_end - k.base) // 64 * 64
    k.go(end - 51 * KB)
    k.lru_w = k.sb("lru_w", [P, 2, 2 * GROUP_W // P, P])
    k.lru_w_loaded = k.lasting_sem("lru_w_loaded")
    k.lru_in = Inputs(k, end - 43 * KB, [("lru_x", T_LX, 4, True), ("lru_g", T_LG, 4, False)])
    k.ml_in = Inputs(k, k.lru_in.end, [("ml_k", T_MK, 2, True), ("ml_v", T_MV, 4, True), ("ml_q", T_MQ, 2, False)])
    k.ssd_in = Inputs(k, k.at_mix + 78 * KB + 512, [("ssd_x", T_SX, 4, True), ("ssd_b", T_SB, 2, True),
                                              ("ssd_c", T_SC, 2, False), ("ssd_z", T_SZ, 4, False)])
    k.dn_in = Inputs(k, k.at_mix, [("dn_q", T_Q, 4, False), ("dn_k", T_K, 4, True), ("dn_v", T_V, 4, True)])


def gate_rows(k):
    nc, io = k.nc, k.io
    k.go(AT_LOW)
    row = {n: k.sb(f"row_{n}", [64, TOK]) for n in ("R", "E", "beta", "xm")}
    k.row = row
    k.gcol = k.sb("gcol", [P, 6, CHUNKS, 64])
    k.decay = k.sb("decay", [P, 2, CHUNKS, GROWS])
    k.sel_at = k.at - k.base
    k.sel = k.sb("sel", [64, 2, GROWS, P])
    k.causal = k.sb("causal", [P, 2, P])
    k.level = k.sb("level", [P, 2, LEVELS, P])
    k.at_mix = k.at - k.base
    assert k.at_mix <= AT_LOW + 48 * KB
    mixer_inputs(k)
    k.go(k.at_mix)
    raw = [k.sb(f"gate_raw{s}", [64, TOK]) for s in range(2)]
    e, s_, u, m, ld, cs, c_row, w_row, nbe, reset = (k.sb(f"row_{n}", [64, TOK]) for n in
                                                    ("e", "s", "u", "m", "ld", "cs", "c", "w", "nbe", "reset"))
    ms = k.sb("m_start", [64, CHUNKS])
    rl = k.sb("r_last", [64, CHUNKS])
    el = k.sb("e_last", [64, CHUNKS])
    dg = k.sb("decay_diag", [64, 2, CHUNKS, GROWS])
    nml = k.sb("minus_ml", [64, 1])

    loaded, pool_steps, a_steps, v_steps = (k.sem(n) for n in ("rows_loaded", "mask_steps", "gate_act_steps", "gate_dve_steps"))
    masks, z_ready, exp_ready, rc_ready, ms_ready = (k.sem(n) for n in ("masks_ready", "z_ready", "exp_ready", "rc_ready", "ms_ready"))
    e_ready, rows_ready, dg_ready, turned, cols_kept = (k.sem(n) for n in ("e_rows_ready", "rows_ready", "dg_ready", "rows_turned", "gcols_kept"))
    w_zero = k.sem("lru_w_zero")
    fwd, bwd = slice(0, 32), slice(32, 64)
    gp = lambda c, rows=slice(0, 64): k.gpar[rows, c:c + 1]

    with nc.Block() as block:
        @block.sync
        def _(sp):
            for s in range(2):
                sp.dma_start(raw[s][:], k.rows_dram[s]).then_inc(loaded, 16)
            k.lru_in.load(sp)
            sp.wait_ge(w_zero, 1)
            for n, name in enumerate(("lru_w_a", "lru_w_i")):
                for half in range(2):
                    rows = slice(64 * half, 64 * half + 64)
                    src = io[name].rearrange("l d (t b) j c -> b j (l d t) c", b=2)[half]
                    sp.dma_start(k.lru_w[rows, n, :, rows], src).then_inc(k.lru_w_loaded, 16)

        @block.gpsimd
        def _(pool):
            step = Steps(pool, pool_steps)
            pool.memset(k.lru_w[:], 0.0).then_inc(w_zero, 1)
            step(pool.memset(reset[:], 1.0))
            step(pool.memset(reset[fwd, 0:TOK:P], 0.0))
            step(pool.memset(reset[bwd, P - 1:TOK:P], 0.0))
            pool.sem_inc(masks, 1)
            step(pool.memset(dg[:], 0.0))
            step(pool.memset(k.sel[:], 0.0))
            step(pool.affine_select(out=k.sel[:], in_=k.sel[:], compare_op=ALU.not_equal, fill=1.0, base=0,
                                    pattern=[[-32, 2], [-1, GROWS], [0, P]], channel_multiplier=1))
            pool.sem_inc(masks, 1)
            step(pool.memset(k.causal[:], 0.0))
            for d, sign in ((0, 1), (1, -1)):
                step(pool.affine_select(out=k.causal[:, d, :], in_=k.causal[:, d, :], compare_op=ALU.is_ge, fill=NEG, base=0,
                                        pattern=[[sign, P]], channel_multiplier=-sign))
            step(pool.memset(k.level[:], 0.0))
            for d in range(2):
                for lv in range(LEVELS):
                    h = 1 << lv
                    view = k.level[:, d, lv, :].rearrange("p (a b r) -> p a b r", b=2, r=h)[:, :, 1 - d, :]
                    step(pool.memset(view, 1.0))
                    step(pool.affine_select(out=view, in_=view, compare_op=ALU.is_ge, fill=0.0, base=-h * d,
                                            pattern=[[-2 * h, P // (2 * h)], [0, h]], channel_multiplier=1))
                    step(pool.affine_select(out=view, in_=view, compare_op=ALU.is_ge, fill=0.0, base=h - 1 + h * d,
                                            pattern=[[2 * h, P // (2 * h)], [0, h]], channel_multiplier=-1))

        @block.scalar
        def _(act):
            step = Steps(act, a_steps)
            act.wait_ge(z_ready, 1)
            softplus_exp(step, act, raw[0][:], e[:])
            act.sem_inc(exp_ready, 1)
            act.wait_ge(loaded, 32)
            step(act.activation(row["beta"][:], raw[1][:], ACT.Sigmoid))
            act.wait_ge(rc_ready, 1)
            for c in range(CHUNKS):
                cols = slice(c * P, (c + 1) * P)
                act.activation(row["E"][:, cols], row["R"][:, cols], ACT.Exp, bias=ms[:, c:c + 1])
                act.activation(w_row[:, cols], c_row[:, cols], ACT.Exp, scale=-1.0, bias=rl[:, c:c + 1])
            step(act.activation(row["xm"][:], m[:], ACT.Exp, scale=-1.0))
            act.sem_inc(e_ready, 1)

        @block.vector
        def _(dve):
            step = Steps(dve, v_steps)
            dve.wait_ge(loaded, 32)
            step(dve.tensor_scalar(raw[0][:], raw[0][:], gp(GP_BIAS), gp(GP_SIGN), ALU.add, ALU.mult))
            dve.sem_inc(z_ready, 1)
            dve.wait_ge(exp_ready, 1)
            softplus_sum(step, dve, raw[0][:], e[:], s_[:], u[:])
            step(dve.tensor_scalar(ld[:], raw[0][:], gp(GP_COEF), None, ALU.mult))
            dve.wait_ge(masks, 1)
            dve.tensor_tensor_scan(cs[fwd, :], reset[fwd, :], ld[fwd, :], 0.0, ALU.mult, ALU.add)
            step(dve.tensor_tensor_scan(cs[bwd, ::-1], reset[bwd, ::-1], ld[bwd, ::-1], 0.0, ALU.mult, ALU.add))
            step(dve.tensor_scalar(u[:], raw[1][:], gp(GP_IGB), None, ALU.add))
            step(dve.tensor_tensor_scan(m[fwd, :], ld[fwd, :], u[fwd, :], 0.0, ALU.add, ALU.max))
            step(dve.tensor_tensor_scan(m[bwd, CTX - 1::-1], ld[bwd, CTX - 1::-1], u[bwd, CTX - 1::-1], 0.0, ALU.add, ALU.max))
            step(dve.tensor_tensor_scan(m[bwd, TOK - 1:CTX - 1:-1], ld[bwd, TOK - 1:CTX - 1:-1], u[bwd, TOK - 1:CTX - 1:-1],
                                        m[bwd, 0:1], ALU.add, ALU.max))
            step(dve.tensor_scalar(nml[:], gp(GP_ML), -1.0, None, ALU.mult))
            step(dve.scalar_tensor_tensor(out=row["R"][:], in0=m[:], scalar=nml[:], in1=cs[:], op0=ALU.mult, op1=ALU.add))
            step(dve.scalar_tensor_tensor(out=c_row[:], in0=u[:], scalar=nml[:], in1=cs[:], op0=ALU.mult, op1=ALU.add))
            step(dve.memset(ms[:], 0.0))
            dve.tensor_copy(ms[fwd, 1:CHUNKS], m[fwd, P - 1:TOK - P:P])
            dve.tensor_copy(ms[bwd, 0:1], m[bwd, P:P + 1])
            dve.tensor_copy(ms[bwd, CHUNKS - 1:CHUNKS], m[bwd, 0:1])
            dve.tensor_copy(ms[bwd, CTX_CHUNKS:CHUNKS - 1], m[bwd, CTX + P:TOK:P])
            dve.tensor_copy(rl[fwd, :], row["R"][fwd, P - 1:TOK:P])
            step(dve.tensor_copy(rl[bwd, :], row["R"][bwd, 0:TOK:P]))
            step(dve.tensor_scalar(ms[:], ms[:], gp(GP_ML), None, ALU.mult))
            dve.sem_inc(rc_ready, 1)
            dve.wait_ge(e_ready, 1)
            step(dve.scalar_tensor_tensor(out=nbe[:], in0=row["E"][:], scalar=-1.0, in1=row["beta"][:], op0=ALU.mult, op1=ALU.mult))
            dve.sem_inc(rows_ready, 1)
            dve.wait_ge(masks, 2)
            dve.tensor_copy(el[fwd, :], row["E"][fwd, P - 1:TOK:P])
            step(dve.tensor_copy(el[bwd, :], row["E"][bwd, 0:TOK:P]))
            for d in range(2):
                rows = slice(32 * d, 32 * d + 32)
                step(dve.tensor_tensor(dg[rows, d], el[rows, :].unsqueeze(2).to_broadcast([32, CHUNKS, GROWS]),
                                       k.ident[rows, 32 * d:32 * d + GROWS].unsqueeze(1).to_broadcast([32, CHUNKS, GROWS]), ALU.mult))
            dve.sem_inc(dg_ready, 1)
            dve.wait_ge(turned, 1)
            for n in range(6):
                step(dve.tensor_copy(k.gcol[:, n], k.psum[n][:, 0:CHUNKS * 64].rearrange("p (c g) -> p c g", g=64)))
            step(dve.tensor_copy(k.decay[:], k.psum[6][:, 0:2 * CHUNKS * GROWS].rearrange("p (d c g) -> p d c g", d=2, g=GROWS)))

        @block.tensor
        def _(pe):
            pe.wait_ge(rows_ready, 1)
            for n, source in enumerate((c_row, w_row, row["beta"], raw[0], nbe, row["xm"])):
                for c in range(CHUNKS):
                    pe.transpose(k.psum[n][:, c * 64:(c + 1) * 64], source[:, c * P:(c + 1) * P], k.ident[0:64, 0:64])
            pe.wait_ge(dg_ready, 1)
            pe.matmul(k.psum[6][:, 0:2 * CHUNKS * GROWS], k.ones[0:64, :], dg[:].rearrange("p d c g -> p (d c g)"),
                      start=True, stop=True).then_inc(turned, 1)


def rglru(k):
    nc, io = k.nc, k.io
    LT, U = GROUP_W // P, 2 * GROUP_W // P
    k.go(k.at_mix)
    x, g = k.lru_in.t["lru_x"], k.lru_in.t["lru_g"]
    w = k.lru_w
    r = k.sb("lru_r", [P, U, TOK])
    i_ = k.sb("lru_i", [P, U, TOK])
    q = k.sb("lru_q", [P, U, TOK])
    h = k.sb("lru_h", [P, U, TOK])
    lam, le, ls, lu = (k.sb(f"lam_{n}", [P, U]) for n in "zesu")
    assert k.at <= nc.sbuf_usable_end, k.at
    assert k.at - k.base <= k.lru_in.end - 28 * KB
    k.go(k.lru_in.end - 20 * KB)
    y = k.sb("lru_y", [P, LT, SEQ])
    x_in, g_in = k.lru_in.loaded["lru_x"], k.lru_in.loaded["lru_g"]
    w_in = k.lru_w_loaded
    a_steps, v_steps, lam_z, lam_e = (k.sem(n) for n in ("lru_act_steps", "lru_dve_steps", "lam_z", "lam_e"))
    mult, gated, log_a, a_done = (k.sem(n) for n in ("lru_products", "lru_gated", "lru_log_a", "lru_a_made"))
    one_minus, rooted, y_made, y_stored = (k.sem(n) for n in ("lru_one_minus", "lru_rooted", "lru_y_made", "lru_y_stored"))
    par = lambda name, u: k.par[:, PAR[name] + u:PAR[name] + u + 1]
    lat, ctx = slice(CTX, TOK), slice(0, CTX)

    with nc.Block() as block:
        @block.sync
        def _(sp):
            k.ml_in.load(sp)
            sp.wait_ge(y_made, LT)
            sp.dma_start(k.mix[2 * LT:3 * LT].rearrange("t p n -> p t n"), y[:]).then_inc(y_stored, 16)
            sp.wait_ge(y_stored, 16)

        @block.tensor
        def _(pe):
            pe.wait_ge(x_in, 16)
            pe.wait_ge(w_in, 64)
            for u in range(U):
                t = u % LT
                if u >= 2:
                    pe.wait_ge(gated, u - 1)
                for n in range(2):
                    b = 4 * (u % 2) + 2 * n
                    pe.matmul(k.psum[b][:], w[:, n, u, :], x[:, t, lat], start=True, stop=True)
                    mm = pe.matmul(k.psum[b + 1][:, ctx], w[:, n, u, :], x[:, t, ctx], start=True, stop=True)
                mm.then_inc(mult, 1)

        @block.scalar
        def _(act):
            step = Steps(act, a_steps)
            act.wait_ge(lam_z, 1)
            softplus_exp(step, act, lam[:], le[:])
            act.sem_inc(lam_e, 1)
            for u in range(U):
                act.wait_ge(mult, u + 1)
                for n, (dst, bias) in enumerate(((r, "lru_ba"), (i_, "lru_bi"))):
                    b = 4 * (u % 2) + 2 * n
                    act.activation(dst[:, u, lat], k.psum[b][:], ACT.Sigmoid, bias=par(bias, u))
                    ins = act.activation(dst[:, u, ctx], k.psum[b + 1][:, ctx], ACT.Sigmoid, bias=par(bias, u))
                ins.then_inc(gated, 1)
            for u in range(U):
                act.wait_ge(log_a, u + 1)
                step(act.activation(q[:, u, :], r[:, u, :], ACT.Tanh, scale=-1.0))
                act.activation(r[:, u, :], r[:, u, :], ACT.Exp).then_inc(a_done, 1)
            for u in range(U):
                act.wait_ge(one_minus, u + 1)
                act.activation(q[:, u, :], q[:, u, :], ACT.Sqrt).then_inc(rooted, 1)

        @block.vector
        def _(dve):
            step = Steps(dve, v_steps)
            step(dve.tensor_scalar(lam[:], k.par[:, PAR["lru_lam"]:PAR["lru_lam"] + U], -1.0, None, ALU.mult))
            dve.sem_inc(lam_z, 1)
            dve.wait_ge(lam_e, 1)
            softplus_sum(step, dve, lam[:], le[:], ls[:], lu[:])
            step(dve.tensor_scalar(lam[:], lam[:], -8.0, None, ALU.mult))
            dve.wait_ge(x_in, 16)
            for u in range(U):
                dve.wait_ge(gated, u + 1)
                dve.tensor_scalar(r[:, u, :], r[:, u, :], lam[:, u:u + 1], None, ALU.mult).then_inc(log_a, 1)
                step(dve.tensor_tensor(i_[:, u, :], i_[:, u, :], x[:, u % LT, :], ALU.mult))
            for u in range(U):
                dve.wait_ge(a_done, u + 1)
                step(dve.tensor_tensor(h[:, u, :], r[:, u, :], r[:, u, :], ALU.mult))
                dve.scalar_tensor_tensor(out=q[:, u, :], in0=h[:, u, :], scalar=1.0, in1=q[:, u, :],
                                         op0=ALU.add, op1=ALU.mult).then_inc(one_minus, 1)
            dve.wait_ge(g_in, 16)
            for t in range(LT):
                for d in range(2):
                    u = d * LT + t
                    dve.wait_ge(rooted, u + 1)
                    step(dve.tensor_tensor(i_[:, u, :], i_[:, u, :], q[:, u, :], ALU.mult))
                    a, b, o = (z[:, u, :] for z in (r, i_, h))
                    if d == 0:
                        step(dve.tensor_tensor_scan(o[:, ctx], a[:, ctx], b[:, ctx], 0.0, ALU.mult, ALU.add))
                        step(dve.tensor_tensor_scan(o[:, lat], a[:, lat], b[:, lat], o[:, CTX - 1:CTX], ALU.mult, ALU.add))
                    else:
                        back_c, back_l = slice(CTX - 1, None, -1), slice(TOK - 1, CTX - 1, -1)
                        step(dve.tensor_tensor_scan(o[:, back_c], a[:, back_c], b[:, back_c], 0.0, ALU.mult, ALU.add))
                        step(dve.tensor_tensor_scan(o[:, back_l], a[:, back_l], b[:, back_l], o[:, 0:1], ALU.mult, ALU.add))
                step(dve.tensor_tensor(h[:, t, lat], h[:, t, lat], h[:, LT + t, lat], ALU.add))
                dve.tensor_tensor(y[:, t, :].rearrange("p (r w) -> p r w", r=GRID_ROWS),
                                  h[:, t, lat].rearrange("p (w r) -> p r w", r=GRID_ROWS),
                                  g[:, t, :].rearrange("p (r w) -> p r w", r=GRID_ROWS), ALU.mult).then_inc(y_made, 1)




class Finish:

    def __init__(self, k, name, o, per, gain, gate, first, sq, std):
        self.k, self.o, self.per, self.gain, self.gate, self.first, self.sq, self.std = k, o, per, gain, gate, first, sq, std
        self.ready, self.squared, self.summed, self.logged, self.rooted, self.made = (
            k.sem(f"{name}_{x}") for x in ("o_ready", "o_squared", "o_summed", "o_logged", "o_rooted", "mix_made"))
        self.stored = k.last_mix_stored if name == "dn" else k.sem(f"{name}_mix_stored")
        self.steps = k.sem(f"{name}_finish_steps")

    def scalar(self, act):
        act.wait_ge(self.ready, 1)
        for t in range(4):
            act.activation(self.sq[:, t, :], self.o[:, t, :], ACT.Square).then_inc(self.squared, 1)
        for n in range(4 // self.per):
            act.wait_ge(self.summed, n + 1)
            act.activation(self.std[:, n, :], self.k.psum[n][:], ACT.Ln, scale=1.0 / (P * self.per),
                           bias=self.k.eps[:]).then_inc(self.logged, 1)
        for n in range(4 // self.per):
            act.wait_ge(self.logged, n + 1)
            act.activation(self.std[:, n, :], self.std[:, n, :], ACT.Exp, scale=-0.5).then_inc(self.rooted, 1)

    def tensor(self, pe):
        for t in range(4):
            n = t // self.per
            pe.wait_ge(self.squared, t + 1)
            mm = pe.matmul(self.k.psum[n][:], self.k.ones[:], self.sq[:, t, :], start=(t % self.per == 0),
                           stop=(t % self.per == self.per - 1))
            if t % self.per == self.per - 1:
                mm.then_inc(self.summed, 1)

    def vector(self, dve, gate_in=None):
        dve.sem_inc(self.ready, 1)
        step = Steps(dve, self.steps)
        if self.gate is not None:
            dve.wait_ge(gate_in, 16)
            step(dve.tensor_tensor(self.gate[:], self.o[:], self.gate[:], ALU.mult))
            dve.wait_ge(self.squared, 4)
        for t in range(4):
            n = t // self.per
            dve.wait_ge(self.rooted, n + 1)
            source = self.o if self.gate is None else self.gate
            dve.scalar_tensor_tensor(out=self.o[:, t, :], in0=source[:, t, :], scalar=self.gain(t), in1=self.std[:, n, :],
                                     op0=ALU.mult, op1=ALU.mult).then_inc(self.made, 1)

    def sync(self, sp):
        sp.wait_ge(self.made, 4)
        sp.dma_start(self.k.mix[self.first:self.first + 4].rearrange("t p n -> p t n"), self.o[:]).then_inc(self.stored, 16)
        if self.stored is not self.k.last_mix_stored:
            sp.wait_ge(self.stored, 16)


UNITS = [(n, d) for n in range(CHUNKS) for d in range(2)]


def latent(n):
    return n >= CTX_CHUNKS


def cols(c):
    return slice(c * P, (c + 1) * P)


def lcols(c):
    return slice((c - CTX_CHUNKS) * P, (c - CTX_CHUNKS + 1) * P)


def first_visit(n, d):
    c = chunk_of(d, n)
    other = [m for m in range(CHUNKS) if chunk_of(1 - d, m) == c][0]
    return (n, d) < (other, 1 - d)


def heads(view):
    return view.rearrange("p (h n) -> p h n", h=4)


def mlstm(k):
    nc, io = k.nc, k.io
    k.go(k.at_mix)
    q, kk, v = (k.ml_in.t["ml_" + n] for n in "qkv")
    o_gate = k.sb("ml_o", [P, 4, SEQ])
    qz = k.sb("ml_qz", [P, ML_HEADS, SEQ])
    kt = k.sb("ml_kt", [P, CHUNKS, 2 * P])
    vt = k.sb("ml_vt", [P, CHUNKS, 4 * P])
    dm, st, qw, diag, num = ([k.sb(f"ml_{n}{d}", [P, 4, P]) for d in range(2)] for n in ("dm", "st", "qw", "diag", "num"))
    den = [k.sb(f"ml_den{d}", [P, 4]) for d in range(2)]
    wk = [k.sb(f"ml_wk{d}", [P, 4, ML_DK]) for d in range(2)]
    state = [[None] + [k.sb(f"ml_state{d}_{n}", [P, 2, P + 4]) for n in range(1, CHUNKS)] for d in range(2)]
    o = k.sb("ml_out", [P, 4, SEQ])
    assert k.at - k.base <= k.ssd_in.end - 30 * KB
    S = lambda n: k.sem("ml_" + n)
    q_in, k_in, v_in = (k.ml_in.loaded["ml_" + n] for n in "qkv")
    o_in, q_zero, q_set = S("o_in"), S("q_zero"), S("q_set")
    turned, kt_kept, vt_kept = S("turned"), S("kt_kept"), S("vt_kept")
    rows_done, masked, decayed, scored, q_weighted = (S(n) for n in ("rows_done", "masked", "decayed", "scored", "q_weighted"))
    num_done, num_kept, diag_made, spread, h_steps, out_added, wk_made, outer_done, state_kept = (
        S(n) for n in ("num_done", "num_kept", "diag_made", "spread", "h_steps", "out_added", "wk_made", "outer_done", "state_kept"))
    fin = Finish(k, "ml", o, 1, lambda t: k.par[:, PAR["ml_norm"] + t:PAR["ml_norm"] + t + 1], o_gate, 3 * 4, qz, v[:, :, 0:SEQ])
    gc = lambda what, c, d, h: k.gcol[:, what, c, 32 * d + R_ML + h:32 * d + R_ML + h + 1]
    L = lambda n, d: 2 * (n - CTX_CHUNKS) + d

    with nc.Block() as block:
        @block.sync
        def _(sp):
            sp.dma_start(o_gate[:], k.proj[T_MO:T_MO + 4, :, CTX:].rearrange("t p n -> p t n")).then_inc(o_in, 16)
            k.ssd_in.load(sp)
            fin.sync(sp)

        @block.gpsimd
        def _(pool):
            pool.memset(qz[:], 0.0).then_inc(q_zero, 1)
            for u, (n, d) in enumerate(UNITS[:-2]):
                c = chunk_of(d, n)
                pool.wait_ge(kt_kept, c + 1)
                if n:
                    pool.wait_ge(outer_done, u - 1)
                pool.tensor_tensor(wk[d][:], kt[:, c, :].rearrange("p (h x) -> p h x", h=4),
                                   k.gcol[:, COL_W, c, 32 * d + R_ML:32 * d + R_ML + 4].unsqueeze(2).to_broadcast([P, 4, ML_DK]),
                                   ALU.mult).then_inc(wk_made, 1)

        @block.tensor
        def _(pe):
            pe.wait_ge(k_in, 16)
            pe.wait_ge(v_in, 16)
            for c in range(CHUNKS):
                b = 4 * (c % 2)
                if c >= 2:
                    pe.wait_ge(kt_kept, c - 1)
                    pe.wait_ge(vt_kept, c - 1)
                for t in range(4):
                    pe.transpose(k.psum[b][:, cols(t)], v[:, t, cols(c)], k.ident[:])
                for t in range(2):
                    mm = pe.transpose(k.psum[b + 1][:, cols(t)], kk[:, t, cols(c)], k.ident[:])
                mm.then_inc(turned, 1)
            pe.wait_ge(kt_kept, CHUNKS)
            pe.wait_ge(vt_kept, CHUNKS)
            pe.wait_ge(q_set, 2)
            for n in range(CHUNKS):
                for d in range(2):
                    if not latent(n):
                        continue
                    c, b = chunk_of(d, n), 4 * d
                    if L(n, d) >= 2:
                        pe.wait_ge(out_added, L(n, d) - 1)
                    pe.wait_ge(state_kept, 2 * n + d - 1)
                    for bank, row in ((b, "R"), (b + 2, "E")):
                        for h in range(4):
                            pe.matmul(k.psum[bank][:, cols(h)], k.sel[:, d, R_ML + h, :], k.row[row][:, cols(c)], start=True, stop=True)
                    for h in range(4):
                        mm = pe.matmul(k.psum[b + 1][:, cols(h)], kk[:, h // 2, cols(c)], qz[:, h, lcols(c)], start=True, stop=True)
                    mm.then_inc(rows_done, 1)
                for d in range(2):
                    if n == CHUNKS - 1:
                        continue
                    c, b, u = chunk_of(d, n), 4 * d, 2 * n + d
                    pe.wait_ge(wk_made, u + 1)
                    if n:
                        pe.wait_ge(state_kept, u - 1)
                    if latent(n):
                        pe.wait_ge(q_weighted, L(n, d) + 1)
                    for h in range(4):
                        rows = slice(64 * (h % 2), 64 * (h % 2) + 64)
                        at = 256 * (h // 2)
                        pe.matmul(k.psum[b + 2][rows, at:at + P], wk[d][:, h, :], vt[:, c, cols(h)], start=True, stop=True)
                        mm = pe.matmul(k.psum[b + 2][rows, at + P:at + P + 1], wk[d][:, h, :], k.ones[:, 0:1], start=True, stop=True)
                    mm.then_inc(outer_done, 1)
                for d in range(2):
                    if not latent(n):
                        continue
                    c, b = chunk_of(d, n), 4 * d
                    pe.wait_ge(scored, L(n, d) + 1)
                    pe.wait_ge(q_weighted, L(n, d) + 1)
                    pe.wait_ge(state_kept, 2 * (n - 1) + d + 1)
                    for h in range(4):
                        pe.matmul(k.psum[b][:, cols(h)], vt[:, c, cols(h)], st[d][:, h, :], start=True, stop=False)
                        pe.matmul(k.psum[b][:, cols(h)], state[d][n][:, h // 2, 0:P], qw[d][:, h, :], start=False, stop=True)
                    for h in range(4):
                        pe.matmul(k.psum[b + 3][:, h:h + 1], st[d][:, h, :], k.ones[:, 0:1], start=True, stop=False)
                        mm = pe.matmul(k.psum[b + 3][:, h:h + 1], qw[d][:, h, :], state[d][n][:, h // 2, P:P + 1], start=False, stop=True)
                    mm.then_inc(num_done, 1)
                for d in range(2):
                    if not latent(n):
                        continue
                    pe.wait_ge(diag_made, L(n, d) + 1)
                    mm = pe.matmul(k.psum[4 * d + 1][:], k.ones[:], diag[d][:].rearrange("p h n -> p (h n)"), start=True, stop=True)
                    mm.then_inc(spread, 1)
            fin.tensor(pe)

        @block.scalar
        def _(act):
            for c in range(CHUNKS):
                act.wait_ge(turned, c + 1)
                act.activation(vt[:, c, :], k.psum[4 * (c % 2)][:], ACT.Copy).then_inc(vt_kept, 1)
            for n in range(CTX_CHUNKS, CHUNKS):
                for d in range(2):
                    act.wait_ge(masked, L(n, d) + 1)
                    act.activation(dm[d][:], dm[d][:], ACT.Exp).then_inc(decayed, 1)
                for d in range(2):
                    act.wait_ge(num_done, L(n, d) + 1)
                    if L(n, d) >= 2:
                        act.wait_ge(out_added, L(n, d) - 1)
                    act.activation(num[d][:], heads(k.psum[4 * d][:]), ACT.Copy).then_inc(num_kept, 1)
            fin.scalar(act)

        @block.vector
        def _(dve):
            step = Steps(dve, h_steps)
            dve.wait_ge(q_in, 16)
            dve.wait_ge(q_zero, 1)
            for half in range(2):
                rows = slice(64 * half, 64 * half + 64)
                dve.tensor_scalar(qz[rows, half::2, :], q[rows], ML_DK ** -0.5, None, ALU.mult).then_inc(q_set, 1)
            for c in range(CHUNKS):
                dve.wait_ge(turned, c + 1)
                dve.tensor_copy(kt[:, c, :], k.psum[4 * (c % 2) + 1][:, 0:2 * P]).then_inc(kt_kept, 1)
            for n in range(CHUNKS):
                for d in range(2):
                    if not latent(n):
                        continue
                    c, b = chunk_of(d, n), 4 * d
                    dve.wait_ge(rows_done, L(n, d) + 1)
                    for h in range(4):
                        ins = dve.scalar_tensor_tensor(out=dm[d][:, h, :], in0=k.psum[b][:, cols(h)], scalar=gc(COL_C, c, d, h),
                                                       in1=k.causal[:, d, :], op0=ALU.subtract, op1=ALU.min)
                    ins.then_inc(masked, 1)
                    dve.tensor_tensor(qw[d][:], qz[:, :, lcols(c)], heads(k.psum[b + 2][:]), ALU.mult).then_inc(q_weighted, 1)
                for d in range(2):
                    if not latent(n):
                        continue
                    dve.wait_ge(decayed, L(n, d) + 1)
                    dve.tensor_tensor(st[d][:], dm[d][:], heads(k.psum[4 * d + 1][:]), ALU.mult).then_inc(scored, 1)
                for d in range(2):
                    c, u = chunk_of(d, n), 2 * n + d
                    if n == CHUNKS - 1:
                        continue
                    dve.wait_ge(outer_done, u + 1)
                    new = k.psum[4 * d + 2][:].rearrange("p (a x) -> p a x", a=2)[:, :, 0:P + 1]
                    if n == 0:
                        dve.tensor_copy(state[d][1][:, :, 0:P + 1], new).then_inc(state_kept, 1)
                        continue
                    dve.wait_ge(state_kept, u - 1)
                    for h in range(4):
                        rows = slice(64 * (h % 2), 64 * (h % 2) + 64)
                        ins = dve.scalar_tensor_tensor(out=state[d][n + 1][rows, h // 2, 0:P + 1], in0=state[d][n][rows, h // 2, 0:P + 1],
                                                       scalar=k.decay[rows, d, c, R_ML + h:R_ML + h + 1], in1=new[rows, h // 2, :],
                                                       op0=ALU.mult, op1=ALU.add)
                    ins.then_inc(state_kept, 1)
                for d in range(2):
                    if not latent(n):
                        continue
                    c, at = chunk_of(d, n), 32 * d + R_ML
                    dve.wait_ge(num_done, L(n, d) + 1)
                    dn = k.psum[4 * d + 3][:, 0:4]
                    step(dve.scalar_tensor_tensor(out=den[d][:], in0=dn, scalar=-1.0, in1=k.gcol[:, COL_XM, c, at:at + 4],
                                                  op0=ALU.mult, op1=ALU.max))
                    step(dve.tensor_tensor(den[d][:], den[d][:], dn, ALU.max))
                    step(dve.reciprocal(den[d][:], den[d][:]))
                    dve.tensor_tensor(diag[d][:], k.ident[:].unsqueeze(1).to_broadcast([P, 4, P]),
                                      den[d][:].unsqueeze(2).to_broadcast([P, 4, P]), ALU.mult).then_inc(diag_made, 1)
                for d in range(2):
                    if not latent(n):
                        continue
                    c, out = chunk_of(d, n), o[:, :, lcols(chunk_of(d, n))]
                    dve.wait_ge(spread, L(n, d) + 1)
                    dve.wait_ge(num_kept, L(n, d) + 1)
                    one = heads(k.psum[4 * d + 1][:])
                    if first_visit(n, d):
                        dve.tensor_tensor(out, num[d][:], one, ALU.mult).then_inc(out_added, 1)
                    else:
                        step(dve.tensor_tensor(num[d][:], num[d][:], one, ALU.mult))
                        dve.tensor_tensor(out, out, num[d][:], ALU.add).then_inc(out_added, 1)
                    dve.wait_ge(out_added, L(n, d) + 1)
            fin.vector(dve, o_in)




def ssd(k):
    nc, io = k.nc, k.io
    x, z, bm, cm = (k.ssd_in.t["ssd_" + n] for n in "xzbc")
    k.go(k.dn_in.end)
    xt = k.sb("ssd_xt", [P, CHUNKS, 4 * P])
    bt = k.sb("ssd_bt", [P, CHUNKS, 2 * P])
    xd, xw = ([k.sb(f"ssd_{n}{d}", [P, SSD_HEADS, SSD_P]) for d in range(2)] for n in ("xd", "xw"))
    state = [[None] + [k.sb(f"ssd_state{d}_{n}", [P, SSD_HEADS, SSD_P]) for n in range(1, CHUNKS)] for d in range(2)]
    assert k.at - k.base <= k.ssd_in.end - 30 * KB
    k.go(k.ssd_in.end)
    dm, st, ce = ([k.sb(f"ssd_{n}{d}", [P, 4, P]) for d in range(2)] for n in ("dm", "st", "ce"))
    o = k.sb("ssd_out", [P, 4, SEQ])
    sq = k.sb("ssd_sq", [P, 4, SEQ])
    std = k.sb("ssd_std", [P, 2, SEQ])
    assert k.at <= nc.sbuf_usable_end, k.at
    S = lambda n: k.sem("ssd_" + n)
    x_in, z_in, b_in, c_in = (k.ssd_in.loaded["ssd_" + n] for n in "xzbc")
    turned, xt_kept, bt_kept = S("turned"), S("xt_kept"), S("bt_kept")
    rows_done, masked, decayed, scored, c_weighted = (S(n) for n in ("rows_done", "masked", "decayed", "scored", "c_weighted"))
    xd_made, xw_made, y_done, y_added, outer_done, state_steps, state_kept = (
        S(n) for n in ("xd_made", "xw_made", "y_done", "y_added", "outer_done", "state_steps", "state_kept"))
    fin = Finish(k, "ssd", o, 2, lambda t: k.par[:, PAR["ssd_norm"] + t:PAR["ssd_norm"] + t + 1], None, 4, sq, std)
    G = lambda n, g, d: ((n - CTX_CHUNKS) * 2 + g) * 2 + d
    STEPS = [(n, g, d) for n in range(CTX_CHUNKS, CHUNKS) for g in range(2) for d in range(2)]

    def per_head(what, c, d, n):
        at = 32 * d + R_SSD
        return k.gcol[:, what, c, at:at + SSD_HEADS].unsqueeze(2).to_broadcast([P, SSD_HEADS, n])

    with nc.Block() as block:
        @block.sync
        def _(sp):
            k.dn_in.load(sp)
            fin.sync(sp)

        @block.gpsimd
        def _(pool):
            for u, (n, d) in enumerate(UNITS):
                c = chunk_of(d, n)
                pool.wait_ge(xt_kept, c + 1)
                if latent(n) and n > CTX_CHUNKS:
                    pool.wait_ge(y_done, G(n - 1, 1, d) + 1)
                pool.tensor_tensor(xd[d][:], xt[:, c, :].rearrange("p (h x) -> p h x", x=SSD_P), per_head(COL_DT, c, d, SSD_P),
                                   ALU.mult).then_inc(xd_made, 1)
                if n == CHUNKS - 1:
                    continue
                pool.wait_ge(xd_made, u + 1)
                if n:
                    pool.wait_ge(outer_done, u - 1)
                pool.tensor_tensor(xw[d][:], xd[d][:], per_head(COL_W, c, d, SSD_P), ALU.mult).then_inc(xw_made, 1)

        @block.tensor
        def _(pe):
            pe.wait_ge(x_in, 16)
            pe.wait_ge(b_in, 16)
            for c in range(CHUNKS):
                b = 4 * (c % 2)
                if c >= 2:
                    pe.wait_ge(xt_kept, c - 1)
                    pe.wait_ge(bt_kept, c - 1)
                for t in range(4):
                    pe.transpose(k.psum[b][:, cols(t)], x[:, t, cols(c)], k.ident[:])
                for t in range(2):
                    mm = pe.transpose(k.psum[b + 1][:, cols(t)], bm[:, t, cols(c)], k.ident[:])
                mm.then_inc(turned, 1)
            pe.wait_ge(xt_kept, CHUNKS)
            pe.wait_ge(bt_kept, CHUNKS)
            pe.wait_ge(c_in, 16)

            def rows(i):
                n, g, d = STEPS[i]
                c, b = chunk_of(d, n), 4 * d
                if i >= 2:
                    pe.wait_ge(c_weighted, i - 1)
                    pe.wait_ge(scored, i - 1)
                for bank, row in ((b, "R"), (b + 1, "E")):
                    for h in range(4):
                        pe.matmul(k.psum[bank][:, cols(h)], k.sel[:, d, R_SSD + 4 * g + h, :], k.row[row][:, cols(c)], start=True, stop=True)
                pe.matmul(k.psum[b + 2][:, 0:P], bm[:, g, cols(c)], cm[:, g, lcols(c)], start=True, stop=True).then_inc(rows_done, 1)

            def outer(n):
                for d in range(2):
                    c, u = chunk_of(d, n), 2 * n + d
                    pe.wait_ge(xw_made, u + 1)
                    if n:
                        pe.wait_ge(state_kept, u - 1)
                    if n > CTX_CHUNKS:
                        pe.wait_ge(y_added, G(n - 1, 1, d) + 1)
                    for g in range(2):
                        mm = pe.matmul(k.psum[4 * d + 3][:, 256 * g:256 * g + 256], bt[:, c, cols(g)],
                                       xw[d][:, 4 * g:4 * g + 4, :].rearrange("p h x -> p (h x)"), start=True, stop=True)
                    mm.then_inc(outer_done, 1)

            def output(i):
                n, g, d = STEPS[i]
                pe.wait_ge(scored, i + 1)
                pe.wait_ge(c_weighted, i + 1)
                pe.wait_ge(xd_made, 2 * n + d + 1)
                pe.wait_ge(state_kept, 2 * (n if n < CHUNKS - 1 else n - 1) + d + 1)
                if g or n == CHUNKS - 1:
                    pe.wait_ge(y_added, i - 1)
                for h in range(4):
                    out = k.psum[4 * d + 3][64 * (h % 2):64 * (h % 2) + 64, P * (h // 2):P * (1 + h // 2)]
                    pe.matmul(out, xd[d][:, 4 * g + h, :], st[d][:, h, :], start=True, stop=False)
                    mm = pe.matmul(out, state[d][n][:, 4 * g + h, :], ce[d][:, h, :], start=False, stop=True)
                mm.then_inc(y_done, 1)

            rows(0)
            rows(1)
            for n in range(CTX_CHUNKS):
                outer(n)
            for i, (n, g, d) in enumerate(STEPS):
                if (g, d) == (0, 0) and n < CHUNKS - 1:
                    outer(n)
                output(i)
                if i + 2 < len(STEPS):
                    rows(i + 2)
            fin.tensor(pe)

        @block.scalar
        def _(act):
            for c in range(CHUNKS):
                act.wait_ge(turned, c + 1)
                act.activation(xt[:, c, :], k.psum[4 * (c % 2)][:], ACT.Copy).then_inc(xt_kept, 1)
            for i in range(G(CHUNKS, 0, 0)):
                act.wait_ge(masked, i + 1)
                act.activation(dm[i % 2][:], dm[i % 2][:], ACT.Exp).then_inc(decayed, 1)
            fin.scalar(act)

        @block.vector
        def _(dve):
            step = Steps(dve, state_steps)
            for c in range(CHUNKS):
                dve.wait_ge(turned, c + 1)
                dve.tensor_copy(bt[:, c, :], k.psum[4 * (c % 2) + 1][:, 0:2 * P]).then_inc(bt_kept, 1)
            dve.wait_ge(c_in, 16)

            def mask(i):
                n, g, d = STEPS[i]
                c, b = chunk_of(d, n), 4 * d
                dve.wait_ge(rows_done, i + 1)
                for h in range(4):
                    at = 32 * d + R_SSD + 4 * g + h
                    ins = dve.scalar_tensor_tensor(out=dm[d][:, h, :], in0=k.psum[b][:, cols(h)],
                                                   scalar=k.gcol[:, COL_C, c, at:at + 1],
                                                   in1=k.causal[:, d, :], op0=ALU.subtract, op1=ALU.min)
                ins.then_inc(masked, 1)
                dve.tensor_tensor(ce[d][:], heads(k.psum[b + 1][:]), cm[:, g, lcols(c)].unsqueeze(1).to_broadcast([P, 4, P]),
                                  ALU.mult).then_inc(c_weighted, 1)

            def score(i):
                d = STEPS[i][2]
                dve.wait_ge(decayed, i + 1)
                dve.tensor_tensor(st[d][:], dm[d][:], k.psum[4 * d + 2][:, 0:P].unsqueeze(1).to_broadcast([P, 4, P]),
                                  ALU.mult).then_inc(scored, 1)

            def new_state(n):
                for d in range(2):
                    c, u = chunk_of(d, n), 2 * n + d
                    dve.wait_ge(outer_done, u + 1)
                    new = k.psum[4 * d + 3][:].rearrange("p (h x) -> p h x", x=SSD_P)
                    if n == 0:
                        dve.tensor_copy(state[d][1][:], new).then_inc(state_kept, 1)
                        continue
                    dve.wait_ge(state_kept, u - 1)
                    step(dve.tensor_tensor(state[d][n + 1][:], state[d][n][:],
                                           k.decay[:, d, c, R_SSD:R_SSD + SSD_HEADS].unsqueeze(2).to_broadcast([P, SSD_HEADS, SSD_P]), ALU.mult))
                    dve.tensor_tensor(state[d][n + 1][:], state[d][n + 1][:], new, ALU.add).then_inc(state_kept, 1)

            def add(i):
                n, g, d = STEPS[i]
                c = chunk_of(d, n)
                dve.wait_ge(y_done, i + 1)
                y = k.psum[4 * d + 3][:, 0:2 * P].rearrange("p (t n) -> p t n", t=2)
                out = o[:, 2 * g:2 * g + 2, lcols(c)]
                if first_visit(n, d):
                    dve.tensor_copy(out, y).then_inc(y_added, 1)
                else:
                    dve.tensor_tensor(out, out, y, ALU.add).then_inc(y_added, 1)

            mask(0)
            mask(1)
            score(0)
            for n in range(CTX_CHUNKS):
                new_state(n)
            for i, (n, g, d) in enumerate(STEPS):
                if (g, d) == (0, 0) and n < CHUNKS - 1:
                    new_state(n)
                if i + 1 < len(STEPS):
                    score(i + 1)
                add(i)
                if i + 2 < len(STEPS):
                    mask(i + 2)
            dve.wait_ge(y_added, G(CHUNKS, 0, 0))
            dve.wait_ge(z_in, 16)
            for t in range(4):
                step(dve.scalar_tensor_tensor(out=o[:, t, :], in0=x[:, t, CTX:], scalar=k.par[:, PAR["ssd_d"] + t:PAR["ssd_d"] + t + 1],
                                              in1=o[:, t, :], op0=ALU.mult, op1=ALU.add))
            step(dve.tensor_tensor(o[:], o[:], z[:], ALU.mult))
            fin.vector(dve)


def deltanet(k):
    nc, io = k.nc, k.io
    k.go(k.at_mix)
    q, kk, v = (k.dn_in.t["dn_" + n] for n in "qkv")
    k.go(k.dn_in.end - 12 * KB)
    nt = k.sb("dn_nt", [P, 2 * CHUNKS, 4, P])
    kt = k.sb("dn_kt", [P, CHUNKS, 4 * P])
    vt = k.sb("dn_vt", [P, CHUNKS, 4 * P])
    pair = lambda n: [k.sb(f"dn_{n}{d}", [P, 4, P]) for d in range(2)]
    dm, X, vb, kw, state, xt_even = (pair(n) for n in ("dm", "x", "vb", "kw", "state", "xt_even"))
    Y = dm
    attn = k.sb("dn_attn", [P, 2 * (CHUNKS - CTX_CHUNKS), 4, P])
    qe = k.sb("dn_qe", [P, 2 * (CHUNKS - CTX_CHUNKS), 4, P])
    parts_at = k.at - k.base
    parts = [k.sb(f"dn_parts{d}", [P, LEVELS, 4, P]) for d in range(2)]
    top = k.at
    assert k.at <= nc.sbuf_usable_end, k.at
    k.go(parts_at)
    sq = [k.sb(f"dn_sq{s}", [P, TOK]) for s in range(2)]
    rn = [k.sb(f"dn_rn{i}", [P, TOK if i >= 4 else SEQ]) for i in range(8)]
    assert k.at <= top
    k.go(k.at_mix)
    o = k.sb("dn_out", [P, 4, SEQ])
    k.go(k.sel_at)
    vn, xt_odd = pair("vn"), pair("xt_odd")
    assert k.at - k.base <= k.sel_at + 2 * GROWS * P * 4
    XT = (xt_even, xt_odd)
    k.go(parts_at)
    z = k.sb("dn_z", [P, 4, SEQ])
    osq = k.sb("dn_osq", [P, 4, SEQ])
    ostd = k.sb("dn_ostd", [P, 4, SEQ])
    S = lambda n: k.sem("dn_" + n)
    q_in, k_in, v_in = (k.dn_in.loaded["dn_" + n] for n in "qkv")
    z_in = S("z_in")
    squared, summed, logged, rooted, normed = S("squared"), S("summed"), S("logged"), S("rooted"), S("normed")
    turned, kt_kept, vt_kept = S("turned"), S("kt_kept"), S("vt_kept")
    rows_done, masked, decayed, beta_done, n_steps = (S(n) for n in ("rows_done", "masked", "decayed", "beta_done", "n_steps"))
    n_made, part_made, qk_done, attn_made, q_weighted = (S(n) for n in ("n_made", "part_made", "qk_done", "attn_made", "q_weighted"))
    nx_done, y_made, x_done, x_kept, xt_made, xt_done, xt_kept = (
        S(n) for n in ("nx_done", "y_made", "x_done", "x_kept", "xt_made", "xt_done", "xt_kept"))
    vk_made, ks_done, r_made, vn_done, vn_kept, out_done, out_added, outer_done, state_kept = (
        S(n) for n in ("vk_made", "ks_done", "r_made", "vn_done", "vn_kept", "out_done", "out_added", "outer_done", "state_kept"))
    fin = Finish(k, "dn", o, 1, lambda t: k.par[:, PAR["dn_norm"]:PAR["dn_norm"] + 1], z, 0, osq, ostd)
    L = lambda n, d: 2 * (n - CTX_CHUNKS) + d
    col = lambda what, c, d, h: k.gcol[:, what, c, 32 * d + R_DN + h:32 * d + R_DN + h + 1]

    def per_head(what, c, d):
        return k.gcol[:, what, c, 32 * d:32 * d + 4].unsqueeze(2).to_broadcast([P, 4, P])

    def over_heads(x):
        return x.unsqueeze(1).to_broadcast([P, 4, P])

    def y_count(n, lv, d):
        return 2 * (LEVELS * n + lv) + d + 1

    def xt_count(n, lv, d):
        return 2 * ((LEVELS - 1) * n + lv - 1) + d + 1

    def xk_count(n, lv, d):
        return 2 * ((LEVELS - 2) * n + lv - 1) + d + 1

    L2 = [(q, h, False) for h in range(4)] + [(kk, h, True) for h in range(4)]

    with nc.Block() as block:
        @block.sync
        def _(sp):
            sp.wait_ge(out_added, L(CHUNKS, 0))
            sp.dma_start(z[:], k.proj[T_Z:T_Z + 4, :, CTX:].rearrange("t p n -> p t n")).then_inc(z_in, 16)
            fin.sync(sp)

        @block.gpsimd
        def _(pool):
            for n in range(CHUNKS):
                for lv in range(LEVELS):
                    for d in range(2):
                        pool.wait_ge(n_made, 2 * n + d + 1)
                        if n:
                            pool.wait_ge(nx_done, y_count(n - 1, lv, d))
                        pool.tensor_tensor(parts[d][:, lv], nt[:, 2 * n + d], over_heads(k.level[:, d, lv, :]), ALU.mult).then_inc(part_made, 1)
                        if lv == 0:
                            pool.wait_ge(part_made, y_count(n, 0, d))
                            if n >= 2:
                                pool.wait_ge(vn_done, 2 * (n - 2) + d + 1)
                            pool.tensor_tensor(XT[n % 2][d][:], over_heads(k.ident[:]), parts[d][:, 0], ALU.subtract).then_inc(xt_made, 1)
                for d in range(2):
                    c = chunk_of(d, n)
                    pool.wait_ge(kt_kept, c + 1)
                    pool.wait_ge(vt_kept, c + 1)
                    if n:
                        pool.wait_ge(state_kept, 2 * (n - 1) + d + 1)
                    ins = pool.tensor_tensor(vb[d][:], heads(vt[:, c, :]), per_head(COL_BETA, c, d), ALU.mult)
                    if n == CHUNKS - 1:
                        ins.then_inc(vk_made, 1)
                        continue
                    pool.tensor_tensor(kw[d][:], heads(kt[:, c, :]), per_head(COL_W, c, d), ALU.mult).then_inc(vk_made, 1)

        @block.tensor
        def _(pe):
            for i, (x, h, has_ctx) in enumerate(L2):
                s = i % 2
                pe.wait_ge(squared, i + 1)
                if i >= 2:
                    pe.wait_ge(logged, i - 1)
                mm = pe.matmul(k.psum[s][:], k.ones[:], sq[s][:, CTX:], start=True, stop=True)
                if has_ctx:
                    mm = pe.matmul(k.psum[2 + s][:, 0:CTX], k.ones[:], sq[s][:, 0:CTX], start=True, stop=True)
                mm.then_inc(summed, 1)
            pe.wait_ge(normed, len(L2))
            pe.wait_ge(v_in, 16)
            for c in range(CHUNKS):
                b = 4 * (c % 2)
                if c >= 2:
                    pe.wait_ge(kt_kept, c - 1)
                    pe.wait_ge(vt_kept, c - 1)
                for t in range(4):
                    pe.transpose(k.psum[b][:, cols(t)], v[:, t, cols(c)], k.ident[:])
                for t in range(4):
                    mm = pe.transpose(k.psum[b + 1][:, cols(t)], kk[:, t, cols(c)], k.ident[:])
                mm.then_inc(turned, 1)
            pe.wait_ge(kt_kept, CHUNKS)
            pe.wait_ge(vt_kept, CHUNKS)
            for n in range(CHUNKS):
                for d in range(2):
                    c, b, u = chunk_of(d, n), 4 * d, 2 * n + d
                    if n:
                        pe.wait_ge(n_made, u - 1)
                    if n > CTX_CHUNKS:
                        pe.wait_ge(attn_made, L(n, d) - 1)
                    for bank, row in ((b, "R"), (b + 1, "E"), (b + 2, "beta")):
                        if row == "E" and not latent(n):
                            continue
                        for h in range(4):
                            pe.matmul(k.psum[bank][:, cols(h)], k.sel[:, d, R_DN + h, :], k.row[row][:, cols(c)], start=True, stop=True)
                    for h in range(4):
                        mm = pe.matmul(k.psum[b + 3][:, cols(h)], kk[:, h, cols(c)], kk[:, h, cols(c)], start=True, stop=True)
                    mm.then_inc(rows_done, 1)
                for d in range(2):
                    if not latent(n):
                        continue
                    c, b, u = chunk_of(d, n), 4 * d, 2 * n + d
                    pe.wait_ge(beta_done, u + 1)
                    for h in range(4):
                        mm = pe.matmul(k.psum[b + 3][:, cols(h)], kk[:, h, cols(c)], q[:, h, lcols(c)], start=True, stop=True)
                    mm.then_inc(qk_done, 1)
            pe.wait_ge(n_made, 2 * CHUNKS)
            pe.wait_ge(attn_made, L(CHUNKS, 0))

            def level(n, lv):
                for d in range(2):
                    b = 4 * d
                    if lv >= 2:
                        pe.wait_ge(x_kept, xk_count(n, lv - 1, d))
                        if n or lv > 2:
                            pe.wait_ge(xt_kept, xt_count(n, lv - 1, d) - 2)
                        for h in range(4):
                            mm = pe.transpose(k.psum[b + 2][:, cols(h)], X[d][:, h, :], k.ident[:])
                        mm.then_inc(xt_done, 1)
                    pe.wait_ge(part_made, y_count(n, lv, d))
                    if lv or n:
                        pe.wait_ge(y_made, y_count(n, lv, d) - 2)
                    for h in range(4):
                        if lv == 0:
                            mm = pe.transpose(k.psum[b][:, cols(h)], parts[d][:, lv, h, :], k.ident[:])
                        else:
                            mm = pe.matmul(k.psum[b][:, cols(h)], parts[d][:, lv, h, :], X[d][:, h, :], start=True, stop=True)
                    mm.then_inc(nx_done, 1)
                for d in range(2):
                    if lv == 0:
                        continue
                    b = 4 * d
                    pe.wait_ge(y_made, y_count(n, lv, d))
                    if lv == 1:
                        pe.wait_ge(xt_made, 2 * n + d + 1)
                    else:
                        pe.wait_ge(xt_kept, xt_count(n, lv - 1, d))
                    if lv < LEVELS - 1:
                        for h in range(4):
                            mm = pe.matmul(k.psum[b + 1][:, cols(h)], XT[n % 2][d][:, h, :], Y[d][:, h, :], start=True, stop=True)
                        mm.then_inc(x_done, 1)
                    else:
                        for h in range(4):
                            mm = pe.matmul(k.psum[b + 2][:, cols(h)], Y[d][:, h, :], XT[n % 2][d][:, h, :], start=True, stop=True)
                        mm.then_inc(xt_done, 1)

            def behind(n, lv):
                for d in range(2):
                    c, bank, u = chunk_of(d, n), k.psum[4 * d + 3], 2 * n + d
                    if lv == 0 and n:
                        pe.wait_ge(state_kept, u - 1)
                        for h in range(4):
                            mm = pe.matmul(bank[:, cols(h)], kk[:, h, cols(c)], state[d][:, h, :], start=True, stop=True)
                        mm.then_inc(ks_done, 1)
                    elif lv == 1:
                        pe.wait_ge(xt_kept, xt_count(n, LEVELS - 1, d))
                        if n:
                            pe.wait_ge(r_made, u - 1)
                        else:
                            pe.wait_ge(vk_made, u + 1)
                        for h in range(4):
                            mm = pe.matmul(bank[:, cols(h)], XT[n % 2][d][:, h, :], vb[d][:, h, :], start=True, stop=True)
                        mm.then_inc(vn_done, 1)
                    elif lv == 2 and latent(n):
                        pe.wait_ge(vn_kept, u + 1)
                        for h in range(4):
                            pe.matmul(bank[:, cols(h)], state[d][:, h, :], qe[:, L(n, d), h, :], start=True, stop=False)
                            mm = pe.matmul(bank[:, cols(h)], vn[d][:, h, :], attn[:, L(n, d), h, :], start=False, stop=True)
                        mm.then_inc(out_done, 1)
                    elif lv == 3 and n < CHUNKS - 1:
                        pe.wait_ge(vn_kept, u + 1)
                        pe.wait_ge(vk_made, u + 1)
                        if latent(n):
                            pe.wait_ge(out_added, L(n, d) + 1)
                        for h in range(4):
                            mm = pe.matmul(bank[:, cols(h)], kw[d][:, h, :], vn[d][:, h, :], start=True, stop=True)
                        mm.then_inc(outer_done, 1)

            for n in range(CHUNKS + 1):
                for lv in range(LEVELS):
                    if n < CHUNKS:
                        level(n, lv)
                    if n:
                        behind(n - 1, lv)
            fin.tensor(pe)

        @block.scalar
        def _(act):
            act.wait_ge(q_in, 16)
            act.wait_ge(k_in, 16)

            def log(i):
                act.wait_ge(summed, i + 1)
                ins = act.activation(rn[i][:, -SEQ:], k.psum[i % 2][:], ACT.Ln, bias=k.eps[:])
                if L2[i][2]:
                    ins = act.activation(rn[i][:, 0:CTX], k.psum[2 + i % 2][:, 0:CTX], ACT.Ln, bias=k.eps[:])
                ins.then_inc(logged, 1)

            for i, (x, h, has_ctx) in enumerate(L2):
                if i >= 2:
                    act.wait_ge(summed, i - 1)
                act.activation(sq[i % 2][:, (0 if has_ctx else CTX):], x[:, h, :], ACT.Square).then_inc(squared, 1)
                if i >= 1:
                    log(i - 1)
            log(len(L2) - 1)
            for i in range(len(L2)):
                act.wait_ge(logged, i + 1)
                act.activation(rn[i][:], rn[i][:], ACT.Exp, scale=-0.5).then_inc(rooted, 1)
            for c in range(CHUNKS):
                act.wait_ge(turned, c + 1)
                act.activation(vt[:, c, :], k.psum[4 * (c % 2)][:], ACT.Copy).then_inc(vt_kept, 1)
            for n in range(CHUNKS):
                for d in range(2):
                    act.wait_ge(masked, 2 * n + d + 1)
                    act.activation(dm[d][:], dm[d][:], ACT.Exp).then_inc(decayed, 1)

            def turned_kept(n, lv, d):
                act.wait_ge(xt_done, xt_count(n, lv, d))
                act.activation(XT[n % 2][d][:], heads(k.psum[4 * d + 2][:]), ACT.Copy).then_inc(xt_kept, 1)

            for n in range(CHUNKS + 1):
                for lv in range(1, LEVELS):
                    if n < CHUNKS:
                        for d in range(2):
                            if lv >= 2:
                                turned_kept(n, lv - 1, d)
                        for d in range(2):
                            if lv < LEVELS - 1:
                                act.wait_ge(x_done, xk_count(n, lv, d))
                                act.activation(X[d][:], heads(k.psum[4 * d + 1][:]), ACT.Copy).then_inc(x_kept, 1)
                            else:
                                turned_kept(n, lv, d)
                    if n and lv == 1:
                        for d in range(2):
                            act.wait_ge(vn_done, 2 * (n - 1) + d + 1)
                            act.activation(vn[d][:], heads(k.psum[4 * d + 3][:]), ACT.Copy).then_inc(vn_kept, 1)
            fin.scalar(act)

        @block.vector
        def _(dve):
            for i, (x, h, has_ctx) in enumerate(L2):
                dve.wait_ge(rooted, i + 1)
                dve.scalar_tensor_tensor(out=x[:, h, :], in0=x[:, h, :], scalar=1.0 if has_ctx else float(P) ** -0.5, in1=rn[i][:],
                                         op0=ALU.mult, op1=ALU.mult).then_inc(normed, 1)
            for c in range(CHUNKS):
                dve.wait_ge(turned, c + 1)
                dve.tensor_copy(kt[:, c, :], k.psum[4 * (c % 2) + 1][:]).then_inc(kt_kept, 1)
            for n in range(CHUNKS):
                for d in range(2):
                    c, b, u = chunk_of(d, n), 4 * d, 2 * n + d
                    dve.wait_ge(rows_done, u + 1)
                    for h in range(4):
                        ins = dve.scalar_tensor_tensor(out=dm[d][:, h, :], in0=k.psum[b][:, cols(h)], scalar=col(COL_C, c, d, h),
                                                       in1=k.causal[:, d, :], op0=ALU.subtract, op1=ALU.min)
                    ins.then_inc(masked, 1)
                    if latent(n):
                        dve.tensor_tensor(qe[:, L(n, d)], q[:, :, lcols(c)], heads(k.psum[b + 1][:]), ALU.mult).then_inc(q_weighted, 1)
                for d in range(2):
                    c, b, u = chunk_of(d, n), 4 * d, 2 * n + d
                    dve.wait_ge(decayed, u + 1)
                    dve.tensor_tensor(nt[:, u], dm[d][:], heads(k.psum[b + 3][:]), ALU.mult).then_inc(beta_done, 1)
                    dve.wait_ge(beta_done, u + 1)
                    dve.tensor_tensor(nt[:, u], nt[:, u], heads(k.psum[b + 2][:]), ALU.mult).then_inc(n_made, 1)
                for d in range(2):
                    if latent(n):
                        dve.wait_ge(qk_done, L(n, d) + 1)
                        dve.tensor_tensor(attn[:, L(n, d)], dm[d][:], heads(k.psum[4 * d + 3][:]), ALU.mult).then_inc(attn_made, 1)

            def behind(n, lv):
                for d in range(2):
                    c, bank, u = chunk_of(d, n), k.psum[4 * d + 3], 2 * n + d
                    if lv == 0 and n:
                        dve.wait_ge(ks_done, u - 1)
                        dve.wait_ge(vk_made, u + 1)
                        for h in range(4):
                            ins = dve.scalar_tensor_tensor(out=vb[d][:, h, :], in0=bank[:, cols(h)], scalar=col(COL_NBE, c, d, h),
                                                           in1=vb[d][:, h, :], op0=ALU.mult, op1=ALU.add)
                        ins.then_inc(r_made, 1)
                    elif lv == 2 and latent(n):
                        dve.wait_ge(out_done, L(n, d) + 1)
                        out = o[:, :, lcols(c)]
                        if first_visit(n, d):
                            dve.tensor_copy(out, heads(bank[:])).then_inc(out_added, 1)
                        else:
                            dve.tensor_tensor(out, out, heads(bank[:]), ALU.add).then_inc(out_added, 1)
                    elif lv == 3 and n < CHUNKS - 1:
                        dve.wait_ge(outer_done, u + 1)
                        if n == 0:
                            dve.tensor_copy(state[d][:], heads(bank[:])).then_inc(state_kept, 1)
                            continue
                        dve.wait_ge(state_kept, u - 1)
                        for h in range(4):
                            ins = dve.scalar_tensor_tensor(out=state[d][:, h, :], in0=state[d][:, h, :],
                                                           scalar=k.decay[:, d, c, R_DN + h:R_DN + h + 1],
                                                           in1=bank[:, cols(h)], op0=ALU.mult, op1=ALU.add)
                        ins.then_inc(state_kept, 1)

            for n in range(CHUNKS + 1):
                for lv in range(LEVELS):
                    if n < CHUNKS:
                        for d in range(2):
                            dve.wait_ge(nx_done, y_count(n, lv, d))
                            dve.tensor_tensor((X if lv == 0 else Y)[d][:], over_heads(k.ident[:]), heads(k.psum[4 * d][:]),
                                              ALU.subtract).then_inc(y_made, 1)
                    if n:
                        behind(n - 1, lv)
            dve.wait_ge(out_added, L(CHUNKS, 0))
            fin.vector(dve, z_in)




class Squares:

    def __init__(self, k, name):
        self.k = k
        self.sq = [k.sb(f"{name}_sq{s}", [P, SEQ]) for s in range(2)]
        self.made, self.summed = k.sem(f"{name}_squares_made"), k.sem(f"{name}_squares_summed")

    def square(self, act, t, s, added, first=False):
        act.wait_ge(*added)
        if not first:
            act.wait_ge(self.summed, t - 1)
        act.activation(self.sq[s][:], self.k.lat[:, bass.ds(t, 1), :].rearrange("p a n -> p (a n)"), ACT.Square).then_inc(self.made, 1)

    def sum(self, pe, t, s, start=False, stop=False):
        pe.wait_ge(self.made, t + 1)
        pe.matmul(self.k.psum[4][:], self.k.ones[:], self.sq[s][:], start=start, stop=stop).then_inc(self.summed, 1)


def output_projection(k):
    nc, io = k.nc, k.io
    k.go(AT_LOW)
    mh = k.sb("mix_hi", [P, KT, SEQ], F32R)
    ml = k.sb("mix_lo", [P, KT, SEQ], F32R)
    assert k.at - k.base <= AT_LAT
    k.go(AT_LAT)
    k.lat = k.sb("lat", [P, KT, SEQ])
    k.go(AT_HIGH)
    mixed = k.sb("mixed", [P, KT, SEQ])
    g1 = [k.sb(f"g1_{s}", [P, 1]) for s in range(2)]
    squares = Squares(k, "norm2")
    ring = Ring(k, "out")
    mix_loaded = [k.sem(f"mix_loaded{q}") for q in range(4)]
    lat_loaded, m_hi, m_lo, g1_set = (k.sem(n) for n in ("lat_loaded", "mix_hi_made", "mix_lo_made", "g1_set"))
    w = io["w_out"].rearrange("l (k p) n -> p (l k) n", p=P)
    QUARTERS = (1, 2, 3, 0)
    order = [4 * q + i for q in QUARTERS for i in range(4)]

    with nc.Block() as block:
        @block.sync
        def _(sp):
            for s in range(2):
                ring.load(sp, s, s, w[:, :, s * P:(s + 1) * P])
            for q in QUARTERS:
                if q == 0:
                    sp.wait_ge(k.last_mix_stored, 16)
                sp.dma_start(mixed[:, 4 * q:4 * q + 4, :], k.mix[4 * q:4 * q + 4].rearrange("k p n -> p k n")).then_inc(mix_loaded[q], 16)
            sp.dma_start(k.lat[:], k.xT_dram).then_inc(lat_loaded, 16)
            with sp.Fori(1, KT // 2) as j:
                for s in range(2):
                    ring.load(sp, j * 2 + s, s, w[:, :, bass.ds(j * (2 * P) + s * P, P)])

        @block.gpsimd
        def _(pool):
            pool.sem_inc(ring.split, 2)
            with pool.Fori(0, KT // 2) as j:
                for s in range(2):
                    ring.subtract(pool, j * 2 + s, s)

        @block.scalar
        def _(act):
            for s in range(2):
                ring.round(act, s, 0, s)
            for i in order:
                act.wait_ge(mix_loaded[i // 4], 16)
                act.activation(mh[:, i, :], mixed[:, i, :], ACT.Copy).then_inc(m_hi, 1)
            for s in range(2):
                ring.round(act, 2 + s, 1, s)
                squares.square(act, s, s, (ring.kept, s + 3), True)
            with act.Fori(1, KT // 2 - 1) as j:
                for s in range(2):
                    ring.round(act, j * 2 + (2 + s), j + 1, s)
                    squares.square(act, j * 2 + s, s, (ring.kept, j * 2 + (s + 3)))
            for t in (KT - 2, KT - 1):
                squares.square(act, t, t % 2, (ring.kept, t + 3))

        @block.tensor
        def _(pe):
            pe.sem_inc(ring.used, 2)
            for s in range(2):
                ring.multiply(pe, s, s, [(k.psum[s][:], mh, ml)], parts=(m_lo, 0), order=order)
            squares.sum(pe, 0, 0, start=True)
            with pe.Fori(1, KT // 2) as j:
                for s in range(2):
                    ring.multiply(pe, j * 2 + s, s, [(k.psum[s][:], mh, ml)])
                    squares.sum(pe, j * 2 + (s - 1), 1 - s)
            squares.sum(pe, KT - 1, 1, stop=True)

        @block.vector
        def _(dve):
            dve.sem_inc(ring.kept, 2)
            dve.wait_ge(k.last_mix_stored, 16)
            for n, i in enumerate(order):
                dve.wait_ge(m_hi, n + 1)
                dve.tensor_tensor(ml[:, i, :], mixed[:, i, :], mh[:, i, :].bitcast(F32), ALU.subtract).then_inc(m_lo, 1)
            dve.wait_ge(lat_loaded, 16)
            with dve.Fori(0, KT // 2) as j:
                for s in range(2):
                    t = j * 2 + s
                    dve.wait_ge(ring.kept, t + 1)
                    dve.tensor_copy(g1[s][:], k.mod[:, bass.ds(t + G1 * KT, 1), 0]).then_inc(g1_set, 1)
                    dve.wait_ge(g1_set, t + 1)
                    dve.wait_ge(ring.used, t + 3)
                    row = k.lat[:, bass.ds(t, 1), :].rearrange("p a n -> p (a n)")
                    dve.scalar_tensor_tensor(out=row, in0=k.psum[s][:], scalar=g1[s][:], in1=row,
                                             op0=ALU.mult, op1=ALU.add).then_inc(ring.kept, 1)
            dve.wait_ge(ring.kept, KT + 2)


FFN_PARTS = 4
F_PART = FT // FFN_PARTS
PART_TILES = 2 * F_PART + KT


def feed_forward(k):
    nc, io = k.nc, k.io
    k.go(AT_LOW)
    fh = k.sb("f_hi", [P, KT, SEQ], F32R)
    fl = k.sb("f_lo", [P, KT, SEQ], F32R)
    assert k.at - k.base <= AT_LAT
    k.go(AT_HIGH)
    ah = k.sb("a_hi", [P, F_PART, SEQ], F32R)
    al = k.sb("a_lo", [P, F_PART, SEQ], F32R)
    u_row = k.sb("u_row", [P, SEQ])
    g_pad = k.sb("g_pad", [P, SEQ + 2])
    g_acc = k.sb("g_acc", [P, SEQ])
    a_row = k.sb("a_row", [P, SEQ])
    fw = k.sb("fw", [P, 3])
    g2 = [k.sb(f"g2_{s}", [P, 1]) for s in range(2)]
    assert k.at <= nc.sbuf_usable_end, k.at
    k.go(AT_HIGH)
    std = k.sb("std2", [P, SEQ])
    normed = [k.sb(f"normed{s}", [P, SEQ]) for s in range(2)]
    moded = [k.sb(f"moded{s}", [P, SEQ]) for s in range(2)]
    k.go(AT_LOW)
    squares = Squares(k, "final")

    ring = Ring(k, "ffn")
    std_made, rstd_made = k.sem("std2_made"), k.sem("rstd2_made")
    n_made, m_made, f_hi, f_lo = (k.sem(n) for n in ("norm2_made", "mod2_made", "f_hi_made", "f_lo_made"))
    u_kept, g_kept, pad_zero2 = k.sem("u_kept"), k.sem("g_kept"), k.sem("g_pad_zero")
    fw_set, g_tap, g_conv, g_act = (k.sem(n) for n in ("fw_set", "g_tap", "g_convolved", "g_activated"))
    a_made, a_hi, a_lo, g2_set = (k.sem(n) for n in ("a_made", "a_hi_made", "a_lo_made", "g2_set"))
    down_kept = k.sem("down_kept")
    up = io["ffn_w_up"].rearrange("l (k p) n -> p (l k) n", p=P)
    down = io["ffn_w_down"].rearrange("l (k p) n -> p (l k) n", p=P)
    flat = lambda x: x.rearrange("p a n -> p (a n)")

    with nc.Block() as block:
        @block.sync
        def _(sp):
            with sp.Fori(0, FFN_PARTS) as b:
                with sp.Fori(0, F_PART) as f:
                    for s in range(2):
                        ring.load(sp, b * PART_TILES + f * 2 + s, s,
                                  up[:, :, bass.ds(b * (F_PART * P) + f * P + s * D_FF, P)])
                with sp.Fori(0, KT // 2) as j:
                    for s in range(2):
                        ring.load(sp, b * PART_TILES + j * 2 + (2 * F_PART + s), s,
                                  down[:, bass.ds(b * F_PART, F_PART), bass.ds(j * (2 * P) + s * P, P)], F_PART)

        @block.gpsimd
        def _(pool):
            pool.sem_inc(ring.split, 2)
            pool.memset(g_pad[:], 0.0).then_inc(pad_zero2, 1)
            with pool.Fori(0, FFN_PARTS * PART_TILES // 2) as j:
                for s in range(2):
                    ring.subtract(pool, j * 2 + s, s)

        @block.scalar
        def _(act):
            act.sem_inc(ring.kept, 2)
            act.activation(std[:], k.psum[4][:], ACT.Ln, scale=1.0 / D_MODEL, bias=k.eps[:]).then_inc(std_made, 1)
            act.wait_ge(std_made, 1)
            act.activation(std[:], std[:], ACT.Exp, scale=-0.5).then_inc(rstd_made, 1)
            ring.round(act, 0, 0, 0)
            for i in range(KT):
                if i == 2:
                    ring.round(act, 1, 0, 1)
                act.wait_ge(n_made, i + 1)
                if i >= 2:
                    act.wait_ge(f_lo, i - 1)
                act.activation(moded[i % 2][:], normed[i % 2][:], ACT.Identity, scale=k.gain2[:, i:i + 1],
                               bias=k.mod[:, SH2 * KT + i, 0:1]).then_inc(m_made, 1)
                act.wait_ge(m_made, i + 1)
                act.activation(fh[:, i, :], moded[i % 2][:], ACT.Copy).then_inc(f_hi, 1)
            act.wait_ge(pad_zero2, 1)

            def up_pair(t, f, half):
                act.wait_ge(ring.used, t + 3)
                act.wait_ge(a_made, f + 1)
                act.activation(u_row[:], k.psum[0][:], ACT.Copy).then_inc(u_kept, 1)
                act.wait_ge(u_kept, f + 1)
                act.sem_inc(ring.kept, 1)
                ring.round(act, t + 2, half + 1, 0)
                act.wait_ge(ring.used, t + 4)
                act.activation(g_pad[:, 1:SEQ + 1], k.psum[1][:], ACT.Copy).then_inc(g_kept, 1)
                act.wait_ge(g_kept, f + 1)
                act.sem_inc(ring.kept, 1)
                ring.round(act, t + 3, half + 1, 1)
                act.wait_ge(g_conv, f + 1)
                act.activation(g_acc[:], g_acc[:], ACT.Silu).then_inc(g_act, 1)

            def part(b, last):
                with act.Fori(0, F_PART) as f:
                    up_pair(b * PART_TILES + f * 2, b * F_PART + f, b * (PART_TILES // 2) + f)
                if last:
                    for s in range(2):
                        ring.round(act, b * PART_TILES + (2 * F_PART + 2 + s), b * (PART_TILES // 2) + (F_PART + 1), s)
                        squares.square(act, s, s, (down_kept, b * KT + (s + 3)), True)
                with act.Fori(last, KT // 2 - last) as j:
                    for s in range(2):
                        ring.round(act, j * 2 + (b * PART_TILES + (2 * F_PART + 2 + s)), j + (b * (PART_TILES // 2) + (F_PART + 1)), s)
                        if last:
                            squares.square(act, j * 2 + s, s, (down_kept, j * 2 + (b * KT + s + 3)))
                if last:
                    for t in (KT - 2, KT - 1):
                        squares.square(act, t, t % 2, (down_kept, b * KT + t + 3))

            with act.Fori(0, FFN_PARTS - 1) as b:
                part(b, 0)
            part(FFN_PARTS - 1, 1)

        @block.tensor
        def _(pe):
            pe.sem_inc(ring.used, 2)

            def up_products(b, first=0):
                with pe.Fori(first, F_PART) as f:
                    for s in range(2):
                        ring.multiply(pe, f * 2 + (b * PART_TILES + s), s, [(k.psum[s][:], fh, fl)],
                                      kept=(ring.kept, f * 2 + (b * (2 * F_PART) + (s + 1))))

            def down_product(b, t, s, first=False):
                ring.multiply(pe, t + (b * PART_TILES + 2 * F_PART), s, [(k.psum[2 + s][:], ah, al)], F_PART,
                              kept=(down_kept, t + (b * KT + 1)), parts=(a_lo, b * F_PART) if first else None)

            for s in range(2):
                ring.multiply(pe, s, s, [(k.psum[s][:], fh, fl)], kept=(ring.kept, s + 1), parts=(f_lo, 0))
            up_products(0, 1)
            for s in range(2):
                down_product(0, s, s, True)
            with pe.Fori(1, KT // 2) as j:
                for s in range(2):
                    down_product(0, j * 2 + s, s)
            with pe.Fori(1, FFN_PARTS - 1) as b:
                up_products(b)
                with pe.Fori(0, KT // 2) as j:
                    for s in range(2):
                        down_product(b, j * 2 + s, s, True)
            last = FFN_PARTS - 1
            up_products(last)
            for s in range(2):
                down_product(last, s, s, True)
            squares.sum(pe, 0, 0, start=True)
            with pe.Fori(1, KT // 2) as j:
                for s in range(2):
                    down_product(last, j * 2 + s, s)
                    squares.sum(pe, j * 2 + (s - 1), 1 - s)
            squares.sum(pe, KT - 1, 1, stop=True)

        @block.vector
        def _(dve):
            dve.sem_inc(down_kept, 2)
            dve.sem_inc(a_made, 1)
            dve.wait_ge(rstd_made, 1)

            def low(i):
                dve.wait_ge(f_hi, i + 1)
                dve.tensor_tensor(fl[:, i, :], moded[i % 2][:], fh[:, i, :].bitcast(F32), ALU.subtract).then_inc(f_lo, 1)

            for i in range(KT):
                if i >= 2:
                    dve.wait_ge(m_made, i - 1)
                dve.tensor_tensor(normed[i % 2][:], k.lat[:, i, :], std[:], ALU.mult).then_inc(n_made, 1)
                if i >= 1:
                    low(i - 1)
            low(KT - 1)
            dve.wait_ge(f_lo, KT)

            with dve.Fori(0, FFN_PARTS) as b:
                with dve.Fori(0, F_PART) as f_in:
                    f = b * F_PART + f_in
                    dve.tensor_copy(fw[:], k.par[:, bass.ds(f + PAR["ffn_cw"], 3, step=FT)]).then_inc(fw_set, 1)
                    dve.wait_ge(fw_set, f + 1)
                    dve.wait_ge(g_kept, f + 1)
                    dve.tensor_scalar(g_acc[:], g_pad[:, 0:SEQ], fw[:, 0:1], None, ALU.mult).then_inc(g_tap, 1)
                    dve.wait_ge(g_tap, f * 2 + 1)
                    dve.scalar_tensor_tensor(out=g_acc[:], in0=g_pad[:, 1:SEQ + 1], scalar=fw[:, 1:2], in1=g_acc[:],
                                             op0=ALU.mult, op1=ALU.add).then_inc(g_tap, 1)
                    dve.wait_ge(g_tap, f * 2 + 2)
                    dve.scalar_tensor_tensor(out=g_acc[:], in0=g_pad[:, 2:SEQ + 2], scalar=fw[:, 2:3], in1=g_acc[:],
                                             op0=ALU.mult, op1=ALU.add).then_inc(g_conv, 1)
                    dve.wait_ge(g_act, f + 1)
                    dve.wait_ge(u_kept, f + 1)
                    dve.tensor_tensor(a_row[:], g_acc[:], u_row[:], ALU.mult).then_inc(a_made, 1)
                    dve.wait_ge(a_made, f + 2)
                    dve.tensor_copy(flat(ah[:, bass.ds(f_in, 1), :]), a_row[:]).then_inc(a_hi, 1)
                    dve.wait_ge(a_hi, f + 1)
                    dve.tensor_tensor(flat(al[:, bass.ds(f_in, 1), :]), a_row[:], flat(ah[:, bass.ds(f_in, 1), :]).bitcast(F32),
                                      ALU.subtract).then_inc(a_lo, 1)
                    dve.wait_ge(a_lo, f + 1)
                with dve.Fori(0, KT // 2) as j:
                    for s in range(2):
                        t = b * PART_TILES + j * 2 + (2 * F_PART + s)
                        dve.wait_ge(down_kept, b * KT + j * 2 + (s + 1))
                        dve.tensor_copy(g2[s][:], k.mod[:, bass.ds(j * 2 + (G2 * KT + s), 1), 0]).then_inc(g2_set, 1)
                        dve.wait_ge(g2_set, b * KT + j * 2 + (s + 1))
                        dve.wait_ge(ring.used, t + 3)
                        row = flat(k.lat[:, bass.ds(j * 2 + s, 1), :])
                        dve.scalar_tensor_tensor(out=row, in0=k.psum[2 + s][:], scalar=g2[s][:], in1=row,
                                                 op0=ALU.mult, op1=ALU.add).then_inc(down_kept, 1)
            dve.wait_ge(down_kept, FFN_PARTS * KT + 2)


def final_norm(k):
    nc = k.nc
    k.go(AT_LOW)
    rstd = k.sb("rstd3", [P, SEQ])
    k.go(AT_RING)
    rows = k.sb("out_rows", [P, SEQ // P, D_MODEL])
    std_made, rstd_made = k.sem("std3_made"), k.sem("rstd3_made")
    f_made, turned, kept, stored = (k.sem(n) for n in ("final_made", "final_turned", "final_kept", "out_stored"))
    gain = k.par[:, PAR["final"]:PAR["final"] + KT]
    out = k.out.rearrange("b (t p) d -> p (b t) d", p=P)

    with nc.Block() as block:
        @block.sync
        def _(sp):
            for q in range(8):
                sp.wait_ge(kept, 2 * (q + 1))
                cols = slice(q * 256, (q + 1) * 256)
                sp.dma_start(out[:, :, cols], rows[:, :, cols]).then_inc(stored, 16)
            sp.wait_ge(stored, 16 * 8)

        @block.scalar
        def _(act):
            act.activation(rstd[:], k.psum[4][:], ACT.Ln, scale=1.0 / D_MODEL, bias=k.eps[:]).then_inc(std_made, 1)
            act.wait_ge(std_made, 1)
            act.activation(rstd[:], rstd[:], ACT.Exp, scale=-0.5).then_inc(rstd_made, 1)
            for i in range(KT):
                act.wait_ge(turned, i + 1)
                act.activation(rows[:, :, i * P:(i + 1) * P], k.psum[i % 2][:].rearrange("p (t c) -> p t c", c=P), ACT.Copy).then_inc(kept, 1)

        @block.tensor
        def _(pe):
            for i in range(KT):
                pe.wait_ge(f_made, i + 1)
                if i >= 2:
                    pe.wait_ge(kept, i - 1)
                for t in range(SEQ // P):
                    mm = pe.transpose(k.psum[i % 2][:, t * P:(t + 1) * P], k.lat[:, i, t * P:(t + 1) * P], k.ident[:])
                mm.then_inc(turned, 1)

        @block.vector
        def _(dve):
            dve.wait_ge(rstd_made, 1)
            for i in range(KT):
                dve.scalar_tensor_tensor(out=k.lat[:, i, :], in0=k.lat[:, i, :], scalar=gain[:, i:i + 1], in1=rstd[:],
                                         op0=ALU.mult, op1=ALU.mult).then_inc(f_made, 1)




STAGES = [modulation_and_norm1, projections, gate_rows, rglru, mlstm, ssd, deltanet,
          output_projection, feed_forward, final_norm]


def hybrid_block(nc, io, out):
    k = Kit(nc, io, out)
    constants_and_state(k)
    for stage in STAGES:
        stage(k)
        k.end_block()


_INS = ["x", "c", "ctx", "c_ctx", "ada_w", "ada_b", "norm1_g", "norm2_g", "w_in",
        "dn_conv_w", "dn_a_log", "dn_dt_bias", "dn_norm_g",
        "ssd_conv_w", "ssd_conv_b", "ssd_a_log", "ssd_dt_bias", "ssd_d", "ssd_norm_g",
        "lru_conv_w", "lru_conv_b", "lru_w_a", "lru_b_a", "lru_w_i", "lru_b_i", "lru_lambda",
        "ml_ig_b", "ml_fg_b", "ml_norm_g", "w_out", "ffn_w_up", "ffn_conv_w", "ffn_w_down",
        "final_norm_g"]


def kernel(**inputs):
    import concourse.bacc as _bacc
    from concourse.bass_utils import run_bass_kernel_spmd as _run

    nc = _bacc.Bacc("TRN2", target_bir_lowering=False, num_devices=1)
    arrays, io = {}, {}
    for name in _INS:
        a = np.ascontiguousarray(inputs[name])
        arrays[f"in_{name}"] = a
        io[name] = nc.dram_tensor(f"in_{name}", a.shape, mybir.dt.from_np(a.dtype), kind="ExternalInput").ap()
    out = nc.dram_tensor("out_dram", (1, SEQ, D_MODEL), F32, kind="ExternalOutput").ap()
    hybrid_block(nc, io, out)
    r = _run(nc, [arrays], core_ids=[0])
    return r.results[0]["out_dram"]
```
